# Optimizing a Trainium2 kernel written in Bass

```python
import jax
import jax.numpy as jnp
from jax import lax
import numpy as np
import math
import jax, jax.numpy as jnp

D_MODEL = 1024
BATCH = 1
SEQ = 256
DEPTH = 2

GRID_W = 64
CTX_LEN = 256
HEAD_DIM = 64
N_Q_HEADS = 8
N_KV_HEADS = 2
ATTN_WIDTH = N_Q_HEADS * HEAD_DIM
KV_WIDTH = 2 * N_KV_HEADS * HEAD_DIM
CONV_CH = D_MODEL - ATTN_WIDTH
CONF_K = 31
ROPE_AXIS_DIM = HEAD_DIM // 2
ROPE_THETA = 10000.0
Q_BLOCK = 128
EVEN_IN = ATTN_WIDTH + KV_WIDTH + 2 * CONV_CH
SC_K = 3
N_EXPERTS = 16
EC_CAPACITY = 2
EXPERT_FF = 1024
N_MOD = 6
EPS = 1e-6
N_EVEN = (DEPTH + 1) // 2
N_ODD = DEPTH // 2


def rms_norm(x, g):
    xf = x.astype(jnp.float32)
    y = xf * lax.rsqrt(jnp.mean(xf * xf, axis=-1, keepdims=True) + EPS)
    return (y * g.astype(jnp.float32)).astype(x.dtype)

def layer_norm(x, g, b):
    xf = x.astype(jnp.float32)
    mu = jnp.mean(xf, axis=-1, keepdims=True)
    var = jnp.mean(jnp.square(xf - mu), axis=-1, keepdims=True)
    y = (xf - mu) * lax.rsqrt(var + EPS)
    return (y * g.astype(jnp.float32) + b.astype(jnp.float32)).astype(x.dtype)

def ada_mod(cvec, w, b):
    m = jax.nn.silu(cvec) @ w + b
    return m.reshape(cvec.shape[:-1] + (N_MOD, cvec.shape[-1]))

def modulate(xn, shift, scale):
    return xn * (1 + scale) + shift

def axial_rope_tables(n):
    rows = n // GRID_W
    row = jnp.repeat(jnp.arange(rows, dtype=jnp.float32), GRID_W)
    col = jnp.tile(jnp.arange(GRID_W, dtype=jnp.float32), rows)
    inv = ROPE_THETA ** (-jnp.arange(0, ROPE_AXIS_DIM, 2, dtype=jnp.float32) / ROPE_AXIS_DIM)
    ang = jnp.concatenate([row[:, None] * inv, col[:, None] * inv], axis=-1)
    return jnp.cos(ang)[None, :, None, :], jnp.sin(ang)[None, :, None, :]

def apply_rope(x, cos, sin):
    half = x.shape[-1] // 2
    xf = x.astype(jnp.float32)
    x1, x2 = xf[..., :half], xf[..., half:]
    return jnp.concatenate([x1 * cos - x2 * sin, x2 * cos + x1 * sin], axis=-1).astype(x.dtype)

def depthwise_conv(x, w):
    k = w.shape[0]
    return lax.conv_general_dilated(
        x, w[:, None, :].astype(x.dtype), window_strides=(1,), padding=[(k // 2, k // 2)],
        dimension_numbers=("NWC", "WIO", "NWC"), feature_group_count=x.shape[-1])

def split_kv(kv, k_g):
    bsz, n, _ = kv.shape
    half = KV_WIDTH // 2
    k = kv[..., :half].reshape(bsz, n, N_KV_HEADS, HEAD_DIM)
    v = kv[..., half:].reshape(bsz, n, N_KV_HEADS, HEAD_DIM)
    return rms_norm(k, k_g), v

def block_attention(q, k, v):
    bsz, n, hq, hd = q.shape
    grp = hq // N_KV_HEADS
    nb = n // Q_BLOCK
    qb = q.reshape(bsz, nb, Q_BLOCK, N_KV_HEADS, grp, hd).transpose(1, 0, 2, 3, 4, 5)
    scale = HEAD_DIM ** -0.5

    def one_block(qblk):
        s = jnp.einsum("bqkgd,btkd->bkgqt", qblk, k).astype(jnp.float32) * scale
        p = jax.nn.softmax(s, axis=-1).astype(v.dtype)
        return jnp.einsum("bkgqt,btkd->bqkgd", p, v)

    o = lax.map(one_block, qb)
    return o.transpose(1, 0, 2, 3, 4, 5).reshape(bsz, n, hq * hd)

def context_kv(hcn, w_in, k_g):
    return split_kv(hcn @ w_in[:, ATTN_WIDTH:ATTN_WIDTH + KV_WIDTH], k_g)

def even_mixer(hm, w_in, q_g, k_g, conv_w, conv_b, ln_g, ln_b, w_out, rope, kv_prefix):
    bsz, n, _ = hm.shape
    proj = hm @ w_in
    q = rms_norm(proj[..., :ATTN_WIDTH].reshape(bsz, n, N_Q_HEADS, HEAD_DIM), q_g)
    k, v = split_kv(proj[..., ATTN_WIDTH:ATTN_WIDTH + KV_WIDTH], k_g)
    if rope is not None:
        q = apply_rope(q, *rope)
        k = apply_rope(k, *rope)
    own_kv = (k, v)
    if kv_prefix is not None:
        k = jnp.concatenate([kv_prefix[0], k], axis=1)
        v = jnp.concatenate([kv_prefix[1], v], axis=1)
    attn = block_attention(q, k, v)
    c0 = ATTN_WIDTH + KV_WIDTH
    u = proj[..., c0:c0 + CONV_CH]
    gate = proj[..., c0 + CONV_CH:]
    g = u * jax.nn.sigmoid(gate)
    g = depthwise_conv(g, conv_w) + conv_b
    g = jax.nn.silu(layer_norm(g, ln_g, ln_b))
    return jnp.concatenate([attn, g], axis=-1) @ w_out, own_kv

def short_conv_mixer(hm, w_in, conv_w, w_out):
    proj = hm @ w_in
    d = hm.shape[-1]
    b_gate, c_gate, xv = proj[..., :d], proj[..., d:2 * d], proj[..., 2 * d:]
    y = depthwise_conv(c_gate * xv, conv_w)
    return (b_gate * y) @ w_out

def ec_moe(h, w_r, w_gate, w_up, w_down):
    bsz, n, _ = h.shape
    cap = max(1, EC_CAPACITY * n // N_EXPERTS)
    aff = jax.nn.softmax(jnp.einsum("bnd,de->bne", h, w_r).astype(jnp.float32), axis=-1)
    gates, idx = lax.top_k(jnp.swapaxes(aff, 1, 2), cap)
    bidx = jnp.broadcast_to(jnp.arange(bsz)[:, None, None], idx.shape)
    xs = h[bidx, idx]
    hid = jax.nn.silu(jnp.einsum("becd,edf->becf", xs, w_gate)) * jnp.einsum("becd,edf->becf", xs, w_up)
    ys = jnp.einsum("becf,efd->becd", hid, w_down) * gates[..., None].astype(h.dtype)
    return jnp.zeros_like(h).at[bidx, idx].add(ys)

def first_inputs(seed: int = 0) -> dict:
    key = jax.random.key(seed)
    ks = iter(jax.random.split(key, 32))

    def nrm(shape, s):
        return jax.random.normal(next(ks), shape, jnp.float32) * s

    def gain(shape):
        return 1.0 + nrm(shape, 0.1)

    L, D, E, F = DEPTH, D_MODEL, N_EXPERTS, EXPERT_FF
    return {
        "x": nrm((BATCH, SEQ, D), 1.0),
        "c": nrm((BATCH, D), 1.0),
        "ctx": nrm((BATCH, CTX_LEN, D), 1.0),
        "c_ctx": nrm((D,), 1.0),
        "ada_w": nrm((L, D, N_MOD * D), 0.5 * D ** -0.5),
        "ada_b": nrm((L, N_MOD * D), 0.1),
        "norm1_g": gain((L, D)),
        "norm2_g": gain((L, D)),
        "ev_w_in": nrm((N_EVEN, D, EVEN_IN), D ** -0.5),
        "ev_q_g": gain((N_EVEN, HEAD_DIM)),
        "ev_k_g": gain((N_EVEN, HEAD_DIM)),
        "ev_conv_w": nrm((N_EVEN, CONF_K, CONV_CH), CONF_K ** -0.5),
        "ev_conv_b": nrm((N_EVEN, CONV_CH), 0.02),
        "ev_ln_g": gain((N_EVEN, CONV_CH)),
        "ev_ln_b": nrm((N_EVEN, CONV_CH), 0.02),
        "ev_w_out": nrm((N_EVEN, ATTN_WIDTH + CONV_CH, D), (ATTN_WIDTH + CONV_CH) ** -0.5),
        "sc_w_in": nrm((N_ODD, D, 3 * D), D ** -0.5),
        "sc_conv_w": nrm((N_ODD, SC_K, D), SC_K ** -0.5),
        "sc_w_out": nrm((N_ODD, D, D), D ** -0.5),
        "moe_w_r": nrm((L, D, E), D ** -0.5),
        "moe_w_gate": nrm((L, E, D, F), D ** -0.5),
        "moe_w_up": nrm((L, E, D, F), D ** -0.5),
        "moe_w_down": nrm((L, E, F, D), F ** -0.5),
        "final_g": gain((D,)),
    }

def first_block(x, c, ctx, c_ctx, ada_w, ada_b, norm1_g, norm2_g,
              ev_w_in, ev_q_g, ev_k_g, ev_conv_w, ev_conv_b, ev_ln_g, ev_ln_b, ev_w_out,
              sc_w_in, sc_conv_w, sc_w_out,
              moe_w_r, moe_w_gate, moe_w_up, moe_w_down, final_g):
    rope = axial_rope_tables(x.shape[1])
    h, hc = x, ctx
    for i in range(DEPTH):
        is_even = i % 2 == 0
        ctx_later = any(j % 2 == 0 for j in range(i + 1, DEPTH))
        m = ada_mod(c, ada_w[i], ada_b[i])[:, None]
        hn = modulate(rms_norm(h, norm1_g[i]), m[:, :, 0], m[:, :, 1])
        if is_even or ctx_later:
            mc = ada_mod(c_ctx, ada_w[i], ada_b[i])
            hcn = modulate(rms_norm(hc, norm1_g[i]), mc[0], mc[1])
        if is_even:
            e = i // 2
            prm = (ev_w_in[e], ev_q_g[e], ev_k_g[e], ev_conv_w[e], ev_conv_b[e],
                   ev_ln_g[e], ev_ln_b[e], ev_w_out[e])
            if ctx_later:
                ctx_out, kv_ctx = even_mixer(hcn, *prm, None, None)
                hc = hc + mc[2] * ctx_out
            else:
                kv_ctx = context_kv(hcn, ev_w_in[e], ev_k_g[e])
            lat_out, _ = even_mixer(hn, *prm, rope, kv_ctx)
            h = h + m[:, :, 2] * lat_out
        else:
            o = i // 2
            prm = (sc_w_in[o], sc_conv_w[o], sc_w_out[o])
            h = h + m[:, :, 2] * short_conv_mixer(hn, *prm)
            if ctx_later:
                hc = hc + mc[2] * short_conv_mixer(hcn, *prm)
        moe = (moe_w_r[i], moe_w_gate[i], moe_w_up[i], moe_w_down[i])
        h = h + m[:, :, 5] * ec_moe(modulate(rms_norm(h, norm2_g[i]), m[:, :, 3], m[:, :, 4]), *moe)
        if ctx_later:
            hc = hc + mc[5] * ec_moe(modulate(rms_norm(hc, norm2_g[i]), mc[3], mc[4]), *moe)
    return rms_norm(h, final_g)


DEPTH_2 = 1

CHUNK = 64
MEM_LEN = 256
MIX_WIDTH = D_MODEL
FOX_WIDTH = MIX_WIDTH // 2
FOX_HEAD_DIM = 64
FOX_HEADS = FOX_WIDTH // FOX_HEAD_DIM
GLA_WIDTH = MIX_WIDTH - FOX_WIDTH
GLA_HEADS = 4
GLA_VALUE_DIM = GLA_WIDTH // GLA_HEADS
GLA_KEY_DIM = GLA_VALUE_DIM // 2
GLA_KEY_WIDTH = GLA_HEADS * GLA_KEY_DIM
GLA_GATE_RANK = 16
GLA_TAU = 16.0
XATTN_HEADS = 4
XATTN_HEAD_DIM = D_MODEL // XATTN_HEADS
D_FF = 4 * D_MODEL
IN_SIZES = (FOX_WIDTH, FOX_WIDTH, FOX_WIDTH, FOX_HEADS,
            GLA_KEY_WIDTH, GLA_KEY_WIDTH, GLA_WIDTH, GLA_GATE_RANK, GLA_WIDTH)
IN_WIDTH = sum(IN_SIZES)


def _split_points():
    return [int(v) for v in np.cumsum(np.array(IN_SIZES))[:-1]]

def rms_norm_2(x, g):
    xf = x.astype(jnp.float32)
    y = xf * lax.rsqrt(jnp.mean(xf * xf, axis=-1, keepdims=True) + EPS)
    return (y * g.astype(jnp.float32)).astype(x.dtype)

def fox_attention(q, k, v, log_f):
    B, S, H, D = q.shape
    scale = 1.0 / math.sqrt(D)
    c = jnp.transpose(jnp.cumsum(log_f, axis=1), (0, 2, 1))
    outs = []
    for i in range(S // Q_BLOCK):
        start, end = i * Q_BLOCK, (i + 1) * Q_BLOCK
        qb = q[:, start:end]
        kb = k[:, :end]
        vb = v[:, :end]
        s = jnp.einsum('bqhd,bkhd->bhqk', qb, kb).astype(jnp.float32) * scale
        bias = c[:, :, start:end, None] - c[:, :, None, :end]
        q_pos = start + jnp.arange(Q_BLOCK)
        k_pos = jnp.arange(end)
        mask = k_pos[None, :] <= q_pos[:, None]
        s = jnp.where(mask, s + bias, -jnp.inf)
        p = jax.nn.softmax(s, axis=-1)
        outs.append(jnp.einsum('bhqk,bkhd->bqhd', p.astype(vb.dtype), vb))
    return jnp.concatenate(outs, axis=1)

def gla_chunked(q, k, v, g_log):
    B, S, H, Dk = q.shape
    Dv = v.shape[-1]
    N = S // CHUNK

    def to_chunks(a):
        return jnp.transpose(a.astype(jnp.float32).reshape(B, N, CHUNK, H, a.shape[-1]), (0, 3, 1, 2, 4))

    qc = to_chunks(q) * (Dk ** -0.5)
    kc = to_chunks(k)
    vc = to_chunks(v)
    bc = jnp.cumsum(to_chunks(g_log), axis=3)
    q_dec = qc * jnp.exp(bc)
    k_dec = kc * jnp.exp(-bc)
    A = jnp.einsum('bhnck,bhnsk->bhncs', q_dec, k_dec)
    tril = jnp.tril(jnp.ones((CHUNK, CHUNK), dtype=bool))
    A = jnp.where(tril, A, 0.0)
    o_intra = jnp.einsum('bhncs,bhnsv->bhncv', A, vc)
    b_last = bc[:, :, :, -1:, :]
    dS = jnp.einsum('bhnck,bhncv->bhnkv', kc * jnp.exp(b_last - bc), vc)
    decay = jnp.exp(b_last[:, :, :, 0, :])

    def step(state, inp):
        d, ds = inp
        return d[..., None] * state + ds, state

    init = jnp.zeros((B, H, Dk, Dv), jnp.float32)
    _, s_prev = lax.scan(step, init, (jnp.moveaxis(decay, 2, 0), jnp.moveaxis(dS, 2, 0)))
    s_prev = jnp.moveaxis(s_prev, 0, 2)
    o_inter = jnp.einsum('bhnck,bhnkv->bhncv', q_dec, s_prev)
    o = o_intra + o_inter
    o = jnp.transpose(o, (0, 2, 3, 1, 4)).reshape(B, S, H, Dv)
    return o.astype(v.dtype)

def parallel_mixer(xn, w_in, fox_b_f, fox_q_norm_g, fox_k_norm_g,
                   gla_w_gate2, gla_b_gate, gla_out_norm_g, w_out):
    B, S, _ = xn.shape
    proj = xn @ w_in
    fq, fk, fv, ff, gq, gk, gv, glr, gr = jnp.split(proj, _split_points(), axis=-1)
    fq = rms_norm_2(fq.reshape(B, S, FOX_HEADS, FOX_HEAD_DIM), fox_q_norm_g)
    fk = rms_norm_2(fk.reshape(B, S, FOX_HEADS, FOX_HEAD_DIM), fox_k_norm_g)
    fv = fv.reshape(B, S, FOX_HEADS, FOX_HEAD_DIM)
    log_f = jax.nn.log_sigmoid((ff + fox_b_f).astype(jnp.float32))
    fox_out = fox_attention(fq, fk, fv, log_f).reshape(B, S, FOX_WIDTH)
    g_log = jax.nn.log_sigmoid((glr @ gla_w_gate2 + gla_b_gate).astype(jnp.float32)) / GLA_TAU
    g_log = g_log.reshape(B, S, GLA_HEADS, GLA_KEY_DIM)
    gla_o = gla_chunked(gq.reshape(B, S, GLA_HEADS, GLA_KEY_DIM),
                        gk.reshape(B, S, GLA_HEADS, GLA_KEY_DIM),
                        gv.reshape(B, S, GLA_HEADS, GLA_VALUE_DIM), g_log)
    gla_o = rms_norm_2(gla_o, gla_out_norm_g.reshape(GLA_HEADS, GLA_VALUE_DIM)).reshape(B, S, GLA_WIDTH)
    gla_out = gla_o * jax.nn.silu(gr)
    return jnp.concatenate([fox_out, gla_out], axis=-1) @ w_out

def memory_cross_attention(hn, memn, wq, wkv, q_norm_g, k_norm_g, wo):
    B, S, _ = hn.shape
    M = memn.shape[1]
    q = rms_norm_2((hn @ wq).reshape(B, S, XATTN_HEADS, XATTN_HEAD_DIM), q_norm_g)
    k, v = jnp.split(memn @ wkv, 2, axis=-1)
    k = rms_norm_2(k.reshape(B, M, XATTN_HEADS, XATTN_HEAD_DIM), k_norm_g)
    v = v.reshape(B, M, XATTN_HEADS, XATTN_HEAD_DIM)
    s = jnp.einsum('bshd,bmhd->bhsm', q, k).astype(jnp.float32) / math.sqrt(XATTN_HEAD_DIM)
    p = jax.nn.softmax(s, axis=-1)
    o = jnp.einsum('bhsm,bmhd->bshd', p.astype(v.dtype), v).reshape(B, S, D_MODEL)
    return o @ wo

def second_inputs(seed: int = 0) -> dict:
    key = jax.random.key(seed)
    ks = jax.random.split(key, 24)
    f32 = jnp.float32

    def nrm(k, shape, scale):
        return jax.random.normal(k, shape, f32) * scale

    def gain(k, shape):
        return jnp.ones(shape, f32) + 0.02 * jax.random.normal(k, shape, f32)

    return {
        "x": nrm(ks[0], (BATCH, SEQ, D_MODEL), 1.0),
        "mem": nrm(ks[1], (BATCH, MEM_LEN, D_MODEL), 1.0),
        "norm_mix_g": gain(ks[2], (D_MODEL,)),
        "w_in": nrm(ks[3], (D_MODEL, IN_WIDTH), D_MODEL ** -0.5),
        "fox_b_f": 2.0 + 0.1 * jax.random.normal(ks[4], (FOX_HEADS,), f32),
        "fox_q_norm_g": gain(ks[5], (FOX_HEAD_DIM,)),
        "fox_k_norm_g": gain(ks[6], (FOX_HEAD_DIM,)),
        "gla_w_gate2": nrm(ks[7], (GLA_GATE_RANK, GLA_KEY_WIDTH), GLA_GATE_RANK ** -0.5),
        "gla_b_gate": nrm(ks[8], (GLA_KEY_WIDTH,), 0.02),
        "gla_out_norm_g": gain(ks[9], (GLA_WIDTH,)),
        "w_out": nrm(ks[10], (MIX_WIDTH, D_MODEL), MIX_WIDTH ** -0.5),
        "norm_xattn_g": gain(ks[11], (D_MODEL,)),
        "norm_mem_g": gain(ks[12], (D_MODEL,)),
        "xattn_wq": nrm(ks[13], (D_MODEL, D_MODEL), D_MODEL ** -0.5),
        "xattn_wkv": nrm(ks[14], (D_MODEL, 2 * D_MODEL), D_MODEL ** -0.5),
        "xattn_q_norm_g": gain(ks[15], (XATTN_HEAD_DIM,)),
        "xattn_k_norm_g": gain(ks[16], (XATTN_HEAD_DIM,)),
        "xattn_wo": nrm(ks[17], (D_MODEL, D_MODEL), D_MODEL ** -0.5),
        "norm_mlp_g": gain(ks[18], (D_MODEL,)),
        "mlp_w1": nrm(ks[19], (D_MODEL, D_FF), D_MODEL ** -0.5),
        "mlp_w2": nrm(ks[20], (D_FF, D_MODEL), D_FF ** -0.5),
    }

def second_block(x, mem, norm_mix_g, w_in, fox_b_f, fox_q_norm_g, fox_k_norm_g,
              gla_w_gate2, gla_b_gate, gla_out_norm_g, w_out,
              norm_xattn_g, norm_mem_g, xattn_wq, xattn_wkv, xattn_q_norm_g,
              xattn_k_norm_g, xattn_wo, norm_mlp_g, mlp_w1, mlp_w2):
    h = x
    for _ in range(DEPTH_2):
        h = h + parallel_mixer(rms_norm_2(h, norm_mix_g), w_in, fox_b_f, fox_q_norm_g,
                               fox_k_norm_g, gla_w_gate2, gla_b_gate, gla_out_norm_g, w_out)
        h = h + memory_cross_attention(rms_norm_2(h, norm_xattn_g), rms_norm_2(mem, norm_mem_g),
                                       xattn_wq, xattn_wkv, xattn_q_norm_g, xattn_k_norm_g, xattn_wo)
        u = jax.nn.relu(rms_norm_2(h, norm_mlp_g) @ mlp_w1)
        h = h + (u * u) @ mlp_w2
    return h


def setup_inputs(seed=0):
    out = dict(first_inputs(seed))
    for name, value in second_inputs(seed + 1).items():
        if name != "x":
            out[name + "_2"] = value
    return out


def reference(
    x, c, ctx, c_ctx, ada_w, ada_b, norm1_g, norm2_g, ev_w_in, ev_q_g, ev_k_g, ev_conv_w,
    ev_conv_b, ev_ln_g, ev_ln_b, ev_w_out, sc_w_in, sc_conv_w, sc_w_out, moe_w_r, moe_w_gate,
    moe_w_up, moe_w_down, final_g, mem_2, norm_mix_g_2, w_in_2, fox_b_f_2, fox_q_norm_g_2,
    fox_k_norm_g_2, gla_w_gate2_2, gla_b_gate_2, gla_out_norm_g_2, w_out_2, norm_xattn_g_2,
    norm_mem_g_2, xattn_wq_2, xattn_wkv_2, xattn_q_norm_g_2, xattn_k_norm_g_2, xattn_wo_2,
    norm_mlp_g_2, mlp_w1_2, mlp_w2_2,
):
    x = first_block(
        x, c, ctx, c_ctx, ada_w, ada_b, norm1_g, norm2_g, ev_w_in, ev_q_g, ev_k_g, ev_conv_w,
        ev_conv_b, ev_ln_g, ev_ln_b, ev_w_out, sc_w_in, sc_conv_w, sc_w_out, moe_w_r,
        moe_w_gate, moe_w_up, moe_w_down, final_g,
    )
    return second_block(
        x, mem_2, norm_mix_g_2, w_in_2, fox_b_f_2, fox_q_norm_g_2, fox_k_norm_g_2,
        gla_w_gate2_2, gla_b_gate_2, gla_out_norm_g_2, w_out_2, norm_xattn_g_2, norm_mem_g_2,
        xattn_wq_2, xattn_wkv_2, xattn_q_norm_g_2, xattn_k_norm_g_2, xattn_wo_2, norm_mlp_g_2,
        mlp_w1_2, mlp_w2_2,
    )


_drawn_inputs = setup_inputs


def setup_inputs(seed=0):
    import zlib

    import numpy as np

    out = dict(_drawn_inputs(seed))
    spreads = {}
    factors = {'ev_q_g': 8.0,
     'ev_k_g': 8.0,
     'ev_conv_b': 6.248,
     'ev_ln_b': 8.0,
     'norm_mix_g_2': 3.071,
     'fox_b_f_2': 16.399,
     'fox_q_norm_g_2': 8.0,
     'fox_k_norm_g_2': 8.0,
     'gla_b_gate_2': 8.0,
     'gla_out_norm_g_2': 7.753,
     'norm_xattn_g_2': 8.0,
     'norm_mem_g_2': 8.0,
     'xattn_q_norm_g_2': 8.0,
     'xattn_k_norm_g_2': 8.0,
     'norm_mlp_g_2': 11.577}
    for name, (base, spread) in spreads.items():
        noise = np.random.default_rng([zlib.crc32(name.encode()), seed]).standard_normal(out[name].shape)
        drawn = base * np.exp(spread * noise) if base else spread * noise
        out[name] = jnp.asarray(drawn.astype(out[name].dtype))
    for name, factor in factors.items():
        out[name] = (out[name] * factor).astype(out[name].dtype)
    return out
```

```python
import numpy as np
import concourse.bass as bass
from concourse import mybir
from contextlib import ExitStack

F32 = mybir.dt.float32
I32 = mybir.dt.int32
ACT = mybir.ActivationFunctionType
ALU = mybir.AluOpType
AX = mybir.AxisListType

P = 128
D = 1024
N = 256
NT = N // P
KD = D // P
EPS = 1e-6
HD = 64
NQ, NKV = 8, 2
AW = NQ * HD
CONVK = 31
CT = 4
PADW = N + CONVK - 1
SCK = 3
E, CAP, F = 16, 32, 1024
EG = 4
GROUPS = E // EG
FOXH, GLAH, GDK, GDV, GCH = 8, 4, 64, 128, 64
GLA_TAU = 16.0
XH, XD = 4, 256
SLOTS = 8
SLOT = 4096
NADA = 12
MASKED = -1e30

C_ID, C_FOX, C_COS, C_SIN, C_T, C_IOTA, C_SCAN, C_E4, C_GRP = 0, 128, 256, 320, 384, 385, 417, 673, 801
C_W = 805

NORMS = ["x", "ctx", "moe0", "mix1", "moe1", "final", "mix2", "mem", "xattn", "mlp"]
TRANSPOSED = [n for n in NORMS if n != "final"]


def constants():
    c = np.zeros((P, C_W), np.float32)
    p = np.arange(P)
    c[:, C_ID:C_ID + P] = np.eye(P, dtype=np.float32)
    c[:, C_FOX:C_FOX + P] = np.where(p[None, :] <= p[:, None], 0.0, MASKED)
    half = np.float32(32)
    inv = np.float32(10000.0) ** (-np.arange(0, 32, 2, dtype=np.float32) / half)
    n = np.arange(N)
    ang = np.concatenate([(n // 64).astype(np.float32)[:, None] * inv,
                          (n % 64).astype(np.float32)[:, None] * inv], axis=1).astype(np.float32)
    for t in range(NT):
        c[:, C_COS + 32 * t:C_COS + 32 * t + 32] = np.cos(ang[t * P:(t + 1) * P])
        c[:, C_SIN + 32 * t:C_SIN + 32 * t + 32] = np.sin(ang[t * P:(t + 1) * P])
    c[:, C_T] = p % CAP + 1
    c[:, C_IOTA:C_IOTA + CAP] = np.arange(CAP) + 1
    c[:, C_SCAN:C_SCAN + N] = (n % GCH != 0)
    e = np.arange(E)
    c[0:E, C_E4:C_E4 + P] = (p[None, :] // CAP == e[:, None] % EG)
    c[0:E, C_GRP:C_GRP + GROUPS] = (np.arange(GROUPS)[None, :] == e[:, None] // EG)
    m = ((p[:, None] // GCH == p[None, :] // GCH) & (p[:, None] <= p[None, :])).astype(np.int32)
    return c, m


STREAM = [("ada0a", 4), ("ev_q", 1), ("ev_kv", 1), ("ev_u", 1), ("ev_gate", 1),
          ("ada0b", 4), ("ada0c", 4), ("ada1", 12), ("ev_out", 2), ("moe0", 96),
          ("sc_in", 6), ("sc_out", 2), ("moe1", 96),
          ("w_small", 1), ("w_gqk", 1), ("w_fq", 1), ("w_fk", 1), ("w_fv", 1), ("w_gv", 1), ("w_gr", 1),
          ("w_out", 2), ("wkv", 4), ("wq", 2), ("wo", 2), ("mlp", 16)]
FIRST = {}
_n = 0
for _name, _k in STREAM:
    FIRST[_name] = _n
    _n += _k
PER_GROUP = 3 * KD
assert PER_GROUP % SLOTS == 0


def build(nc, a):
    ctx = ExitStack()
    with ctx:
        def sb(name, shape, dt=F32):
            return ctx.enter_context(nc.sbuf_tensor(name, shape, dt))

        sems = {}

        def sem(name):
            if name not in sems:
                sems[name] = ctx.enter_context(nc.semaphore(name))
            return sems[name]

        ring = sb("ring", [P, SLOTS, SLOT])
        h_t = sb("h", [P, NT * D])
        rows_t = sb("rows", [P, NT * D])
        xT_t = sb("xT", [P, KD * N])
        cst = sb("cst", [P, C_W])
        glam = sb("gla_mask", [P, P], I32)
        gcol = sb("gain_cols", [P, 8, KD])
        mcol = sb("mod_cols", [P, 10, KD])
        acol = sb("scale_cols", [P, 5, KD])
        wr = sb("router_w", [P, 2, KD, E])
        gate_bc = sb("gate_bc", [P, 1280])
        ss = sb("ss", [P, len(NORMS), NT])
        ms = sb("ms", [P, len(NORMS), NT])
        rstd = sb("rstd", [P, len(NORMS), NT])
        mhalf = sb("mhalf", [P, NT])
        cin = sb("c_cols", [P, 2, KD])
        sil = sb("silu_c", [P, KD, 32])
        ones = sb("ones", [P, N])
        lnrow = sb("ln_row", [P, N])
        sm = sb("small", [P, 256])
        scr = sb("scratch", [P, 10496])
        ps = ctx.enter_context(nc.psum_tensor("ps", [P, 8, 512], F32))
        mod_dram = nc.dram_tensor("mod_scratch", (2, 2, 6 * D), F32).ap()

        h = h_t[:, :].rearrange("p (t d) -> p t d", t=NT)
        rows = rows_t[:, :].rearrange("p (t d) -> p t d", t=NT)
        xT = xT_t[:, :].rearrange("p (k n) -> p k n", k=KD)
        ident = cst[:, C_ID:C_ID + P]
        scan_mask = cst[:, C_SCAN:C_SCAN + N]

        def at(off, **dims):
            n = 1
            for v in dims.values():
                n *= v
            v = scr[:, off:off + n]
            if len(dims) == 1:
                return v
            names = " ".join(dims)
            return v.rearrange(f"p ({names}) -> p {names}", **dims)

        mrow = at(0, q=NADA, i=P)
        ctx_rows = at(1536, t=NT, d=D)
        cT = at(3584, k=KD, n=N)
        qk = at(5632, t=NT, h=12, e=HD)
        vall = at(7168, t=4, e=128)
        gpad = at(7680, c=CT, n=PADW)
        sg = cacc = at(8824, c=CT, n=N)
        csq = at(3584, c=CT, n=N)
        cw = at(9848, c=CT, j=34)
        cwrow = at(8824, d=512)
        sq = rows_t[:, 0:1536].rearrange("p (t h e) -> p t h e", t=NT, h=12)
        ra = rows_t[:, 0:640].rearrange("p (t h e) -> p t h e", t=NT, h=10)
        rb = rows_t[:, 640:1280].rearrange("p (t h e) -> p t h e", t=NT, h=10)
        rc = xT_t[:, 0:640].rearrange("p (t h e) -> p t h e", t=NT, h=10)
        rd = xT_t[:, 640:1280].rearrange("p (t h e) -> p t h e", t=NT, h=10)
        kT = at(1536, s=512)
        qT = at(2048, i=4, n=N)
        pexp = at(3584, b=2, s=512)
        pT = at(4608, b=2, s=4, q=P)
        attn = xT_t[:, 0:1024].rearrange("p (t e) -> p t e", t=NT)
        aT = xT_t[:, 1024:2048].rearrange("p (k n) -> p k n", k=4)
        xsT = at(0, k=KD, c=P)
        hid = at(1024, f=F)
        hT = at(2048, k=KD, c=P)
        ym = at(3072, d=D)
        sel_w = at(4096, n=N)
        aff_bc = at(4352, n=N)
        RA = at(4608, g=GROUPS, v=2, n=N)
        onehot = at(6656, t=NT, s=E * CAP)
        affT = at(7680, n=N)
        work = at(7936, n=N)
        rank = at(8192, n=N)
        final_bc = at(8448, d=D)
        aff = at(9472, t=NT, e=E)
        rankT = at(9504, t=NT, e=E)
        smaskE = at(9600, n=N)
        bS = at(0, c=KD, n=N)
        cS = at(2048, c=KD, n=N)
        cx = at(4096, c=KD, n=N + 2)
        yS = at(6160, c=KD, n=N)
        cw1 = at(8208, c=KD, j=SCK)
        cw1row = at(8232, d=D)
        gqT = at(0, r=2, n=N)
        gkT = at(512, r=2, n=N)
        kdec = at(1024, r=2, n=N)
        glog = at(1536, r=2, n=N)
        bcum = at(2048, r=2, n=N)
        ex = at(2560, x=2, r=2, n=N)
        AT = at(2560, t=NT, h=GLAH, c=P)
        gv = at(3584, t=NT, e=512)
        gr = at(4608, t=NT, e=512)
        klrow = at(5632, t=NT, r=2, e=P)
        state = at(6144, r=2, n=3, v=GDV)
        fqk = at(6912, t=NT, h=16, e=HD)
        NB = at(6912, h=FOXH, n=N)
        fv = at(8960, t=NT, e=512)
        fp = at(5632, b=2, s=N)
        fpT = at(9984, b=2, s=N)
        lf = wr[:, :, :, :].rearrange("p l k e -> p (l k e)")
        lf2 = lnrow[:, :]
        glrT = sil[:, :, :].rearrange("p k v -> p (k v)")
        fsq = rows_t[:, :].rearrange("p (t h e) -> p t h e", t=NT, h=16)
        fT = xT_t[:, :].rearrange("p (w r n) -> p w r n", w=2, r=4)
        gsq = at(0, t=NT, e=512)
        go = at(1024, t=NT, e=512)
        mem_rows = at(0, t=NT, d=D)
        memT = at(2048, k=KD, n=N)
        xk = at(4096, t=NT, d=D)
        xv = at(6144, t=NT, d=D)
        xkT = at(8192, k=KD, n=N)
        xq = at(0, t=NT, d=D)
        xqT = at(2048, k=KD, n=N)
        xp = at(0, b=2, s=N)
        xpT = at(512, b=2, s=N)
        xsq = at(4096, t=NT, d=D)
        uT = at(0, b=2, k=4, n=N)
        ur = at(2048, b=2, k=4, n=N)

        class Steps:

            def __init__(self, eng, name):
                self.eng, self.sem, self.n = eng, sem(name), 0

            def mark(self, ins):
                ins.then_inc(self.sem, 1)
                self.n += 1

            def wait(self):
                self.eng.wait_ge(self.sem, self.n)

            def __call__(self, ins):
                self.mark(ins)
                self.wait()

        def arrived(eng, i):
            eng.wait_ge(sem(f"slot{i % SLOTS}_loaded"), 16 * (i // SLOTS + 1))

        def whole(eng, name, j=0):
            eng.wait_ge(sem("chunks_used"), FIRST[name] + j + 1)

        def slot8(i):
            return ring[:, i % SLOTS, :].rearrange("p (k n) -> p k n", k=KD)

        def slot4(i):
            return ring[:, i % SLOTS, :].rearrange("p (e f) -> p e f", e=EG)

        def pb(b):
            return ps[:, b, :]

        def flat(v):
            return v.rearrange("p a b -> p (a b)")

        def by_token(v):
            return v.rearrange("p (t d) -> p t d", t=NT)

        SHIFT = {"x": 0, "ctx": 4, "moe0": 2, "mix1": 6, "moe1": 8}
        SCALE = {"x": 0, "ctx": 1, "moe0": 2, "mix1": 3, "moe1": 4}
        GAIN = {"mix2": 4, "mem": 5, "xattn": 6, "mlp": 7}

        def affine(name):
            if name in SHIFT:
                return acol[:, SCALE[name], :], mcol[:, SHIFT[name], :]
            return gcol[:, GAIN[name], :], None

        NORM_BANKS = {n: (4, 5, 6, 7) for n in TRANSPOSED}
        NORM_BANKS["ctx"] = (0, 1, 2, 3)
        qkg = gate_bc[:, 1024:1152].rearrange("p (w e) -> p w e", w=2)
        foxg = gate_bc[:, 0:128].rearrange("p (w e) -> p w e", w=2)
        glag = gate_bc[:, 128:640]
        xqg, xkg = gate_bc[:, 640:896], gate_bc[:, 896:1152]
        gate2 = at(6912, n=N)[0:16, :]
        FS, FTB, FO = (1, 2, 3, 5), (6, 7), (0, 4)
        GO = ((0, 6), (4, 7))

        block = ctx.enter_context(nc.Block())

        @block.sync
        def _(sp):
            def load(i, dst, src):
                if i >= SLOTS:
                    sp.wait_ge(sem("chunks_used"), i - SLOTS + 1)
                sp.dma_start(dst, src).then_inc(sem(f"slot{i % SLOTS}_loaded"), 16)

            def columns(name, w, count, width=512, rows_by="(p k) n -> p k n", first=0, col0=0):
                v = w.rearrange(rows_by, k=KD)
                for j in range(count):
                    i, c = FIRST[name] + j, col0 + width * (first + j)
                    load(i, slot8(i)[:, :, 0:width], v[:, :, c:c + width])

            def experts(name, l):
                base = FIRST[name]
                gate = a["moe_w_gate"][l].rearrange("(g e) (p k) f -> g k p e f", e=EG, k=KD)
                up = a["moe_w_up"][l].rearrange("(g e) (p k) f -> g k p e f", e=EG, k=KD)
                down = a["moe_w_down"][l].rearrange("(g e) (k p) d -> g k p e d", e=EG, p=P)
                with sp.Fori(0, GROUPS) as g:
                    for c in range(PER_GROUP):
                        w, k = (gate, up, down)[c // KD], c % KD
                        sp.wait_ge(sem("chunks_used"), PER_GROUP * g + (base + c - SLOTS + 1))
                        sp.dma_start(slot4(base + c), w[g, k])\
                            .then_inc(sem(f"slot{(base + c) % SLOTS}_loaded"), 16)

            natural = "(k p) n -> p k n"
            columns("ada0a", a["ada_w"][0], 4)
            evw = a["ev_w_in"][0]
            columns("ev_q", evw, 1)
            columns("ev_kv", evw, 1, width=256, col0=512)
            columns("ev_u", evw, 1, col0=768)
            columns("ev_gate", evw, 1, col0=1280)
            columns("ada0b", a["ada_w"][0], 4, first=4)
            columns("ada0c", a["ada_w"][0], 4, first=8)
            columns("ada1", a["ada_w"][1], 12)
            columns("ev_out", a["ev_w_out"][0], 2, rows_by=natural)
            experts("moe0", 0)
            columns("sc_in", a["sc_w_in"][0], 6)
            columns("sc_out", a["sc_w_out"][0], 2, rows_by=natural)
            experts("moe1", 1)
            w2 = a["w_in_2"]
            i = FIRST["w_small"]
            v = w2.rearrange("(p k) n -> p k n", k=KD)
            sp.wait_ge(sem("chunks_used"), i - SLOTS + 1)
            sp.dma_start(slot8(i)[:, :, 0:8], v[:, :, 1536:1544]).then_inc(sem("forget_cols"), 16)
            sp.dma_start(slot8(i)[:, :, 32:48], v[:, :, 2568:2584]).then_inc(sem(f"slot{i % SLOTS}_loaded"), 16)
            for name, col in (("w_gqk", 1544), ("w_fq", 0), ("w_fk", 512), ("w_fv", 1024), ("w_gv", 2056), ("w_gr", 2584)):
                columns(name, w2, 1, col0=col)
            columns("w_out", a["w_out_2"], 2, rows_by=natural)
            columns("wkv", a["xattn_wkv_2"], 4)
            columns("wq", a["xattn_wq_2"], 2)
            columns("wo", a["xattn_wo_2"], 2, rows_by=natural)
            w1 = a["mlp_w1_2"].rearrange("(p k) f -> p k f", k=KD)
            wd = a["mlp_w2_2"].rearrange("(c k p) d -> c p k d", k=4, p=P)
            for j in range(8):
                i = FIRST["mlp"] + 2 * j
                load(i, slot8(i), w1[:, :, 512 * j:512 * (j + 1)])
                load(i + 1, slot4(i + 1), wd[j])
            for t in range(NT):
                sp.wait_ge(sem("h_ready"), 16 + 2 * t + 2)
                sp.dma_start(a["out"][0, t * P:(t + 1) * P, :], h[:, t, :]).then_inc(sem("stored"), 16)
            sp.wait_ge(sem("stored"), 16 * NT)

        @block.scalar
        def _(act):
            link = Steps(act, "act_steps")

            act.dma_start(cin[:, 0, :], a["c"][0].rearrange("(p k) -> p k", k=KD)).then_inc(sem("c_in"), 16)
            act.dma_start(cin[:, 1, :], a["c_ctx"].rearrange("(p k) -> p k", k=KD)).then_inc(sem("c_in"), 16)
            act.dma_start(h, a["x"][0].rearrange("(t p) d -> p t d", p=P)).then_inc(sem("x_in"), 16)
            act.dma_start(ctx_rows, a["ctx"][0].rearrange("(t p) d -> p t d", p=P)).then_inc(sem("ctx_in"), 16)
            act.dma_start(cst[:, :], a["cst"]).then_inc(sem("cst_in"), 16)
            gains = [a["norm1_g"][0], a["norm1_g"][1], a["norm2_g"][0], a["norm2_g"][1],
                     a["norm_mix_g_2"], a["norm_mem_g_2"], a["norm_xattn_g_2"], a["norm_mlp_g_2"]]
            for j, g in enumerate(gains):
                act.dma_start(gcol[:, j, :], g.rearrange("(p k) -> p k", k=KD)).then_inc(sem("params_in"), 16)
            act.dma_start(cwrow[0:CONVK, :], a["ev_conv_w"][0]).then_inc(sem("params_in"), 16)
            for j, n in enumerate(("ev_conv_b", "ev_ln_g", "ev_ln_b")):
                act.dma_start(cwrow[CONVK + j:CONVK + j + 1, :], a[n]).then_inc(sem("params_in"), 16)
            for j, n in enumerate(("ev_q_g", "ev_k_g")):
                act.dma_start(qkg[:, j, :], a[n][0].partition_broadcast(P)).then_inc(sem("params_in"), 16)
            for l in range(2):
                act.dma_start(wr[:, l], a["moe_w_r"][l].rearrange("(p k) e -> p k e", k=KD)).then_inc(sem("params_in"), 16)
            act.dma_start(glam[:, :], a["cst_i"]).then_inc(sem("params_in"), 16)

            act.wait_ge(sem("c_in"), 32)
            act.wait_ge(sem("sil_zero"), 1)
            nc.scalar.activation(sil[:, :, 0:2], cin[:, :, :].rearrange("p v k -> p k v"), ACT.Silu).then_inc(sem("sil"), 1)

            def squares(name, src, junk):
                u = NORMS.index(name)
                for t in range(NT):
                    nc.scalar.activation(junk[:, t, :], src[:, t, :], ACT.Square,
                                         accum_out=ss[:, u, t:t + 1]).then_inc(sem("norm_ss"), 1)

            def transposed(name, dst):
                v, bank, (scale, shift) = TRANSPOSED.index(name), NORM_BANKS[name], affine(name)
                for b in (1, 3):
                    act.wait_ge(sem("norm_T"), 4 * v + b + 1)
                    for k in (2 * b, 2 * b + 1):
                        src = ps[:, bank[b], 256 * (k % 2):256 * (k % 2) + 256]
                        if shift is None:
                            last = nc.scalar.activation(dst[:, k, :], src, ACT.Copy, scale=scale[:, k:k + 1])
                        else:
                            last = nc.scalar.activation(dst[:, k, :], src, ACT.Identity, scale=scale[:, k:k + 1],
                                                        bias=shift[:, k:k + 1])
                    last.then_inc(sem("xT_ready"), 1)

            xT_rows = by_token(xT_t[:, :])

            act.wait_ge(sem("x_in"), 16)
            squares("x", h, xT_rows)
            act.wait_ge(sem("ctx_in"), 16)
            squares("ctx", ctx_rows, by_token(flat(cT)))
            act.wait_ge(sem("scale_cols"), 1)
            transposed("x", xT)
            transposed("ctx", cT)
            whole(act, "ev_q")
            for t in range(NT):
                nc.scalar.activation(qk[:, t, 0:NQ, :].rearrange("p (i w) e -> p w i e", w=2),
                                     pb(t).rearrange("p (w i e) -> p w i e", w=2, e=HD), ACT.Copy)\
                    .then_inc(sem("ev_rows"), 1)
            whole(act, "ev_kv")
            for w, bank in ((0, 2), (1, 3)):
                for t in range(NT):
                    src = ps[:, bank, 256 * t:256 * t + 256]
                    nc.scalar.activation(qk[:, t, 8 + 2 * w:10 + 2 * w, :],
                                         src[:, 0:128].rearrange("p (h e) -> p h e", e=HD), ACT.Copy)\
                        .then_inc(sem("ev_rows"), 1)
                    nc.scalar.activation(vall[:, 2 - 2 * w + t, :], src[:, 128:256], ACT.Copy).then_inc(sem("ev_rows"), 1)
            whole(act, "ev_gate")
            for j in range(2):
                nc.scalar.activation(flat(sg[:, 2 * j:2 * j + 2, :]), pb(6 + j), ACT.Sigmoid).then_inc(sem("cv_gate"), 1)
            act.wait_ge(sem("inverses"), 1)
            nc.scalar.activation(sm[:, 24:48], sm[:, 24:48], ACT.Sqrt).then_inc(sem("roots"), 1)
            act.wait_ge(sem("ev_qkT_ps"), 1)
            for b in range(2):
                nc.scalar.activation(flat(qT[:, 2 * b:2 * b + 2, :]), pb(b), ACT.Copy).then_inc(sem("ev_qT"), 1)

            def ev_probs_T(m):
                act.wait_ge(sem("ev_pT_ps"), m + 1)
                if m >= 2:
                    act.wait_ge(sem("ev_pv"), m - 1)
                nc.scalar.activation(flat(pT[:, 1]), pb(5), ACT.Copy).then_inc(sem("ev_pT_act"), 1)

            for n in range(NT * NQ):
                act.wait_ge(sem("ev_max"), n + 1)
                if n >= 2:
                    act.wait_ge(sem("ev_pT_ps"), n - 1)
                nc.scalar.activation(pexp[:, n % 2, :], pb(n % 4), ACT.Exp, bias=sm[:, 64 + n:65 + n],
                                     accum_out=sm[:, 96 + n:97 + n]).then_inc(sem("ev_p"), 1)
                if n % 2 == 0 and n >= 2:
                    ev_probs_T(n - 1)
            ev_probs_T(NT * NQ - 1)
            act.wait_ge(sem("cv_centered"), 1)
            nc.scalar.activation(flat(csq), flat(cacc), ACT.Square).then_inc(sem("cv_sq"), 1)
            act.wait_ge(sem("inverses"), 2)
            nc.scalar.activation(lnrow[:, :], lnrow[:, :], ACT.Sqrt).then_inc(sem("roots"), 1)
            act.wait_ge(sem("cv_norm"), 1)
            for c in range(CT):
                nc.scalar.activation(cacc[:, c, :], cacc[:, c, :], ACT.Silu, scale=cw[:, c, 32:33],
                                     bias=cw[:, c, 33:34]).then_inc(sem("cv_out"), 1)
            act.wait_ge(sem("ev_aT_ps"), 2)
            nc.scalar.activation(flat(aT[:, 2:4, :]), pb(5), ACT.Copy).then_inc(sem("ev_aT"), 1)

            def experts(l):
                name, base = f"moe{l}", FIRST[f"moe{l}"]
                scale, shift = affine(name)
                act.wait_ge(sem("h_ready"), 4 * (l + 1))
                squares(name, h, xT_rows)
                transposed(name, xT)
                act.wait_ge(sem("mo_max"), l + 1)
                for t in range(NT):
                    nc.scalar.activation(aff[:, t, :], ps[:, 0, E * t:E * t + E], ACT.Exp, bias=sm[:, 130 + t:131 + t],
                                         accum_out=sm[:, 132 + t:133 + t]).then_inc(sem("mo_exp"), 1)
                with act.Fori(0, GROUPS) as g:
                    n = g + GROUPS * l
                    act.wait_ge(sem("mo_bc"), n + 1)
                    nc.scalar.activation(aff_bc, ps[:, 4, N:2 * N], ACT.Copy).then_inc(sem("mo_affbc"), 1)
                    act.wait_ge(sem("mo_gather"), 2 * n + 2)
                    for k in range(4, KD):
                        last = nc.scalar.activation(xsT[:, k, :], ps[:, 7, P * (k - 4):P * (k - 3)], ACT.Identity,
                                                    scale=scale[:, k:k + 1], bias=shift[:, k:k + 1])
                    last.then_inc(sem("mo_xsT_act"), 1)
                    act.wait_ge(sem("chunks_used"), PER_GROUP * g + (base + KD))
                    act.wait_ge(sem("mo_hT_ps"), 2 * n + 1)
                    nc.scalar.activation(hid, ps[:, 0:2, :].rearrange("p b f -> p (b f)"), ACT.Silu)\
                        .then_inc(sem("mo_silu"), 1)
                    act.wait_ge(sem("mo_hT_ps"), 2 * n + 3)
                    nc.scalar.activation(flat(hT[:, 4:8, :]), pb(7), ACT.Copy).then_inc(sem("mo_hT_act"), 1)

            experts(0)

            act.wait_ge(sem("mo_h"), 4 * GROUPS + 1)
            squares("mix1", h, xT_rows)
            transposed("mix1", xT)
            for j in range(4):
                whole(act, "sc_in", j)
                dst = (bS, cS)[j // 2]
                for b in range(2):
                    c = 4 * (j % 2) + 2 * b
                    last = nc.scalar.activation(flat(dst[:, c:c + 2, :]), pb(2 * j + b), ACT.Copy)
                last.then_inc(sem("sc_bc"), 1)

            experts(1)

            act.wait_ge(sem("mo_h"), 8 * GROUPS + 1)
            squares("final", h, xT_rows)
            act.wait_ge(sem("h_final"), 2)
            squares("mix2", h, xT_rows)
            transposed("mix2", xT)
            whole(act, "w_small")
            nc.scalar.activation(glrT[0:16, :], ps[0:16, 0, N:2 * N], ACT.Copy).then_inc(sem("glr"), 1)
            act.wait_ge(sem("gate_abs"), 1)
            link(nc.scalar.activation(lf2[0:FOXH, :], lf2[0:FOXH, :], ACT.Exp, scale=-1.0))
            nc.scalar.activation(lf2[0:FOXH, :], lf2[0:FOXH, :], ACT.Ln, bias=1.0).then_inc(sem("gate_ln"), 1)
            whole(act, "w_gqk")
            for j, dst in enumerate((gqT, gkT)):
                nc.scalar.activation(flat(dst), pb(1 + j), ACT.Copy).then_inc(sem("gqk"), 1)
            act.wait_ge(sem("gate_abs"), 2)
            link(nc.scalar.activation(ex[:, 0], ex[:, 0], ACT.Exp, scale=-1.0))
            nc.scalar.activation(ex[:, 0], ex[:, 0], ACT.Ln, bias=1.0).then_inc(sem("gate_ln"), 1)
            for w, name in enumerate(("w_fq", "w_fk")):
                whole(act, name)
                for t in range(NT):
                    nc.scalar.activation(fqk[:, t, 8 * w:8 * w + 8, :], pb(4 + 2 * w + t).rearrange("p (h e) -> p h e", e=HD),
                                         ACT.Copy).then_inc(sem("fqk"), 1)
            act.wait_ge(sem("gl_cum"), 1)
            nc.scalar.activation(ex[:, 0], bcum, ACT.Exp)
            nc.scalar.activation(ex[:, 1], bcum, ACT.Exp, scale=-1.0)
            nc.scalar.activation(sm[:, 200:208].rearrange("p (r c) -> p r c", r=2),
                                 bcum.rearrange("p r (c j) -> p r c j", j=GCH)[:, :, :, GCH - 1], ACT.Exp)\
                .then_inc(sem("gl_exp"), 1)
            act.wait_ge(sem("gl_dec"), 1)
            for r in range(2):
                for c in range(4):
                    s = slice(GCH * c, GCH * (c + 1))
                    last = nc.scalar.activation(ex[:, 0, r, s], bcum[:, r, s], ACT.Exp, scale=-1.0,
                                                bias=bcum[:, r, GCH * (c + 1) - 1:GCH * (c + 1)])
            last.then_inc(sem("gl_exp"), 1)
            for name, dst, bank in (("w_fv", fv, 0), ("w_gv", gv, 2)):
                whole(act, name)
                for t in range(NT):
                    nc.scalar.activation(dst[:, t, :], pb(bank + t), ACT.Copy).then_inc(sem("values"), 1)
            act.wait_ge(sem("inverses"), 3)
            nc.scalar.activation(sm[:, 32:64], sm[:, 32:64], ACT.Sqrt).then_inc(sem("roots"), 1)
            whole(act, "w_gr")
            for t in range(NT):
                nc.scalar.activation(gr[:, t, :], pb(6 + t), ACT.Silu).then_inc(sem("gr"), 1)
            for w in range(2):
                act.wait_ge(sem("cols_ps"), 2 * w + 2)
                nc.scalar.activation(flat(fT[:, w, 2:4, :]), pb(1 + 2 * w), ACT.Copy).then_inc(sem("cols"), 1)
            act.wait_ge(sem("inverses"), 4)
            nc.scalar.activation(sm[:, 160:168], sm[:, 160:168], ACT.Sqrt).then_inc(sem("roots"), 1)

            def fox_probs_T(m):
                mk = P * (m // FOXH + 1)
                act.wait_ge(sem("fx_pT_ps"), m + 1)
                if m >= 2:
                    act.wait_ge(sem("fx_pv"), m - 1)
                nc.scalar.activation(fpT[:, 1, 0:mk], ps[:, FTB[1], 0:mk], ACT.Copy).then_inc(sem("fx_pT_act"), 1)

            for n in range(NT * FOXH):
                nk = P * (n // FOXH + 1)
                act.wait_ge(sem("fx_max"), n + 1)
                nc.scalar.activation(fp[:, n % 2, 0:nk], fp[:, n % 2, 0:nk], ACT.Exp, bias=sm[:, 64 + n:65 + n],
                                     accum_out=sm[:, 96 + n:97 + n]).then_inc(sem("fx_p"), 1)
                if n % 2 == 0 and n >= 2:
                    fox_probs_T(n - 1)
            fox_probs_T(NT * FOXH - 1)
            for b in (1, 3):
                act.wait_ge(sem("cols_ps"), 4 + b + 1)
                nc.scalar.activation(flat(xT[:, 2 * b:2 * b + 2, :]), pb(b), ACT.Copy).then_inc(sem("cols"), 1)

            act.wait_ge(sem("mem_in"), 16)
            squares("mem", mem_rows, by_token(flat(memT)))
            transposed("mem", memT)
            for j in range(4):
                whole(act, "wkv", j)
                for t in range(NT):
                    dst = (xk, xv)[j // 2]
                    nc.scalar.activation(dst[:, t, 512 * (j % 2):512 * (j % 2) + 512], pb((2 * j + t + 4) % 8), ACT.Copy)\
                        .then_inc(sem("xkv"), 1)
            act.wait_ge(sem("inverses"), 5)
            nc.scalar.activation(sm[:, 32:40], sm[:, 32:40], ACT.Sqrt).then_inc(sem("roots"), 1)
            for b in (1, 3):
                act.wait_ge(sem("cols_ps"), 8 + b + 1)
                nc.scalar.activation(flat(xkT[:, 2 * b:2 * b + 2, :]), pb(b), ACT.Copy).then_inc(sem("cols"), 1)
            act.wait_ge(sem("h_ready"), 12)
            squares("xattn", h, xT_rows)
            transposed("xattn", xT)
            for j in range(2):
                whole(act, "wq", j)
                for t in range(NT):
                    nc.scalar.activation(xq[:, t, 512 * j:512 * j + 512], pb(2 * j + t), ACT.Copy).then_inc(sem("xq"), 1)
            act.wait_ge(sem("inverses"), 6)
            nc.scalar.activation(sm[:, 48:56], sm[:, 48:56], ACT.Sqrt).then_inc(sem("roots"), 1)
            for b in (1, 3):
                act.wait_ge(sem("cols_ps"), 12 + b + 1)
                nc.scalar.activation(flat(xqT[:, 2 * b:2 * b + 2, :]), pb(4 + b), ACT.Copy).then_inc(sem("cols"), 1)
            for n in range(NT * XH):
                act.wait_ge(sem("xa_max"), n + 1)
                if n >= 2:
                    act.wait_ge(sem("xa_pT_ps"), n - 1)
                nc.scalar.activation(xp[:, n % 2, :], ps[:, n % 2, 0:N], ACT.Exp, bias=sm[:, 64 + n:65 + n],
                                     accum_out=sm[:, 96 + n:97 + n]).then_inc(sem("xa_p"), 1)
            for b in (1, 3):
                act.wait_ge(sem("cols_ps"), 16 + b + 1)
                nc.scalar.activation(flat(xT[:, 2 * b:2 * b + 2, :]), pb(b), ACT.Copy).then_inc(sem("cols"), 1)

            act.wait_ge(sem("h_ready"), 16)
            squares("mlp", h, xT_rows)
            transposed("mlp", xT)
            for j in range(8):
                whole(act, "mlp", 2 * j)
                if j >= 2:
                    act.wait_ge(sem("mlp_uT"), j - 1)
                for b in range(2):
                    last = nc.scalar.activation(flat(ur[:, j % 2, 2 * b:2 * b + 2, :]), pb(4 + 2 * (j % 2) + b), ACT.Relu)
                last.then_inc(sem("mlp_relu"), 1)

        @block.gpsimd
        def _(pool):
            link = Steps(pool, "pool_steps")
            nc.gpsimd.memset(sil[:, :, :], 0.0).then_inc(sem("sil_zero"), 1)
            link.mark(nc.gpsimd.memset(mhalf[:, :], -0.5))
            link(nc.gpsimd.memset(mrow, 0.0))
            nc.gpsimd.memset(ones[:, :], 1.0).then_inc(sem("ones"), 1)

            def ada_bias(l):
                for j in range(4):
                    src = a["ada_b"][l].rearrange("(q j i) -> j q i", j=4, i=P)[j]
                    for v in range(2):
                        pool.dma_start(mrow[32 * j + v:32 * j + v + 1], src.unsqueeze(0)).then_inc(sem("ada_b_in"), 16)

            def store_mod(l, q0, q1, count):
                for j in range(4):
                    dst = mod_dram[l].rearrange("v (q j i) -> j v q i", j=4, i=P)[j][:, q0:q1, :]
                    pool.dma_start(dst, mrow[32 * j:32 * j + 2, q0:q1, :]).then_inc(sem("mod_out"), 16)
                pool.wait_ge(sem("mod_out"), 16 * count)

            def load_mod(slot, l, v, s):
                pool.dma_start(mcol[:, slot, :], mod_dram[l, v, s * D:(s + 1) * D].rearrange("(p k) -> p k", k=KD))\
                    .then_inc(sem("mod_cols"), 16)

            def load_gate(l, s):
                pool.dma_start(gate_bc[:, 0:D], mod_dram[l, 0, s * D:(s + 1) * D].partition_broadcast(P))\
                    .then_inc(sem("gate_in"), 16)

            def rms(name):
                u = NORMS.index(name)
                pool.wait_ge(sem("norm_ss"), 2 * u + 2)
                link(nc.gpsimd.tensor_scalar(ms[:, u, :], ss[:, u, :], 1.0 / D, EPS, ALU.mult, ALU.add))
                nc.gpsimd.tensor_tensor(rstd[:, u, :], ms[:, u, :], mhalf[:, :], ALU.pow).then_inc(sem("norm_rstd"), 1)

            ada_bias(0)
            rms("x")
            rms("ctx")
            pool.wait_ge(sem("ada_rows"), 1)
            store_mod(0, 0, 4, 4)
            for slot, v, s in ((0, 0, 0), (1, 0, 1), (4, 1, 0), (5, 1, 1)):
                load_mod(slot, 0, v, s)
            pool.wait_ge(sem("cw"), 1)
            pool.wait_ge(sem("gpad"), 2)
            tmp = rows_t[:, 1536:2048].rearrange("p (c n) -> p c n", c=2)
            for c in (2, 3):
                link.mark(nc.gpsimd.tensor_scalar(cacc[:, c, :], gpad[:, c, 0:N], cw[:, c, 0:1], cw[:, c, 31:32],
                                                  ALU.mult, ALU.add))
            for k in range(1, CONVK):
                for c in (2, 3):
                    link.mark(nc.gpsimd.tensor_scalar(tmp[:, c - 2, :], gpad[:, c, k:k + N], cw[:, c, k:k + 1], None,
                                                      ALU.mult))
                link.wait()
                for c in (2, 3):
                    ins = nc.gpsimd.tensor_tensor(cacc[:, c, :], cacc[:, c, :], tmp[:, c - 2, :], ALU.add)
                    if k < CONVK - 1:
                        link.mark(ins)
                    else:
                        ins.then_inc(sem("conv_pool"), 1)
                link.wait()
            pool.wait_ge(sem("ada_rows"), 3)
            store_mod(0, 4, 12, 8)
            for slot, s in ((2, 3), (3, 4)):
                load_mod(slot, 0, 0, s)
            load_gate(0, 2)
            ada_bias(1)
            pool.wait_ge(sem("ada_rows"), 6)
            store_mod(1, 0, 12, 12)
            for slot, s in ((6, 0), (7, 1), (8, 3), (9, 4)):
                load_mod(slot, 1, 0, s)
            rms("moe0")
            pool.wait_ge(sem("gate_used"), 4)
            load_gate(0, 5)
            rms("mix1")
            load_gate(1, 2)
            pool.dma_start(cw1row[0:SCK, :], a["sc_conv_w"][0]).then_inc(sem("sc_convw_in"), 16)
            rms("moe1")
            pool.wait_ge(sem("gate_used"), 8)
            load_gate(1, 5)
            pool.wait_ge(sem("mo_lists"), 2)
            pool.dma_start(final_bc, a["final_g"].partition_broadcast(P)).then_inc(sem("final_in"), 16)
            pool.wait_ge(sem("mo_ym"), 4 * GROUPS)
            for n, o, w in (("fox_q_norm_g_2", 0, 64), ("fox_k_norm_g_2", 64, 64), ("gla_out_norm_g_2", 128, 512),
                            ("xattn_q_norm_g_2", 640, 256), ("xattn_k_norm_g_2", 896, 256)):
                pool.dma_start(gate_bc[:, o:o + w], a[n].partition_broadcast(P)).then_inc(sem("gains2_in"), 16)
            pool.dma_start(sm[0:FOXH, 140:141], a["fox_b_f_2"].unsqueeze(1)).then_inc(sem("gate2_in"), 16)
            for r in range(2):
                pool.dma_start(sm[:, 141 + r:142 + r], a["gla_b_gate_2"][P * r:P * (r + 1)].unsqueeze(1))\
                    .then_inc(sem("gate2_in"), 16)
            rms("final")
            pool.dma_start(gate2, a["gla_w_gate2_2"]).then_inc(sem("gate2_in"), 16)
            rms("mix2")
            pool.wait_ge(sem("cols"), 8)
            pool.dma_start(mem_rows, a["mem_2"][0].rearrange("(t p) d -> p t d", p=P)).then_inc(sem("mem_in"), 16)
            for n in ("mem", "xattn", "mlp"):
                rms(n)
            for j in range(8):
                pool.wait_ge(sem("mlp_relu"), j + 1)
                if j >= 2:
                    pool.wait_ge(sem("chunks_used"), FIRST["mlp"] + 2 * (j - 2) + 2)
                nc.gpsimd.tensor_tensor(uT[:, j % 2], ur[:, j % 2], ur[:, j % 2], ALU.mult).then_inc(sem("mlp_uT"), 1)

        @block.vector
        def _(dve):
            link = Steps(dve, "dve_steps")

            def normed(name, src, dst):
                u = NORMS.index(name)
                dve.wait_ge(sem("norm_rstd"), u + 1)
                for t in range(NT):
                    nc.vector.tensor_scalar(dst[:, t, :], src[:, t, :], rstd[:, u, t:t + 1], None, ALU.mult)\
                        .then_inc(sem("norm_rows"), 1)

            def transposed(name, dst):
                v, bank, (scale, shift) = TRANSPOSED.index(name), NORM_BANKS[name], affine(name)
                for b in (0, 2):
                    dve.wait_ge(sem("norm_T"), 4 * v + b + 1)
                    for k in (2 * b, 2 * b + 1):
                        src = ps[:, bank[b], 256 * (k % 2):256 * (k % 2) + 256]
                        if shift is None:
                            last = nc.vector.tensor_scalar(dst[:, k, :], src, scale[:, k:k + 1], None, ALU.mult)
                        else:
                            last = nc.vector.tensor_scalar(dst[:, k, :], src, scale[:, k:k + 1], shift[:, k:k + 1],
                                                           ALU.mult, ALU.add)
                    last.then_inc(sem("xT_ready"), 1)

            def ada_rows(name, j0, bank, q0):
                whole(dve, name, j0 + 3)
                nc.vector.tensor_tensor(mrow[:, q0:q0 + 4, :], mrow[:, q0:q0 + 4, :],
                                        pb(bank).rearrange("p (q i) -> p q i", i=P), ALU.add).then_inc(sem("ada_rows"), 1)

            def scale_col(name, col, gain):
                return nc.vector.scalar_tensor_tensor(acol[:, SCALE[name], :], mcol[:, col, :], 1.0, gcol[:, gain, :],
                                                      ALU.add, ALU.mult)

            def add_gated(n, name, banks):
                for j in range(2):
                    whole(dve, name, j)
                    s = slice(512 * j, 512 * j + 512)
                    for t in range(NT):
                        i = 2 * j + t
                        nc.vector.tensor_tensor(rows[:, t, s], pb(banks[i]), gate_bc[:, s], ALU.mult)\
                            .then_inc(sem("gate_used"), 1)
                    for t in range(NT):
                        dve.wait_ge(sem("gate_used"), 4 * n + 2 * j + t + 1)
                        nc.vector.tensor_tensor(h[:, t, s], h[:, t, s], rows[:, t, s], ALU.add).then_inc(sem("h_ready"), 1)

            def add_plain(name, banks, first=0):
                for j in range(2):
                    whole(dve, name, first + j)
                    for t in range(NT):
                        s = slice(512 * j, 512 * j + 512)
                        nc.vector.tensor_tensor(h[:, t, s], h[:, t, s], pb(banks[2 * j + t]), ALU.add)\
                            .then_inc(sem("h_ready"), 1)

            normed("x", h, rows)
            normed("ctx", ctx_rows, ctx_rows)
            dve.wait_ge(sem("ada_b_in"), 8 * 16)
            ada_rows("ada0a", 0, 0, 0)
            dve.wait_ge(sem("params_in"), 17 * 16)
            dve.wait_ge(sem("mod_cols"), 4 * 16)
            scale_col("x", 1, 0)
            scale_col("ctx", 5, 0).then_inc(sem("scale_cols"), 1)
            dve.wait_ge(sem("scale_cols"), 1)
            transposed("x", xT)
            transposed("ctx", cT)
            dve.wait_ge(sem("cw_ps"), 1)
            nc.vector.tensor_copy(flat(cw), ps[:, 4, 0:CT * 34]).then_inc(sem("cw"), 1)
            dve.wait_ge(sem("params_in"), 17 * 16)
            link.mark(nc.vector.tensor_scalar(qkg[:, 0, :], qkg[:, 0, :], float(HD) ** -0.5, None, ALU.mult))
            edge = CONVK // 2
            link.mark(nc.vector.memset(gpad[:, :, 0:edge], 0.0))
            link(nc.vector.memset(gpad[:, :, edge + N:PADW], 0.0))
            whole(dve, "ev_u")
            for j in range(2):
                dve.wait_ge(sem("cv_gate"), j + 1)
                nc.vector.tensor_tensor(gpad[:, 2 * j:2 * j + 2, edge:edge + N],
                                        pb(4 + j).rearrange("p (c n) -> p c n", c=2), sg[:, 2 * j:2 * j + 2, :], ALU.mult)\
                    .then_inc(sem("gpad"), 1)
            dve.wait_ge(sem("ev_rows"), 10)
            link(nc.vector.tensor_tensor(sq, qk, qk, ALU.mult))
            link(nc.vector.tensor_reduce(sm[:, 0:24].rearrange("p (t h) -> p t h", t=NT), sq, AX.X, ALU.add))
            link(nc.vector.tensor_scalar(sm[:, 0:24], sm[:, 0:24], 1.0 / HD, EPS, ALU.mult, ALU.add))
            nc.vector.reciprocal(sm[:, 24:48], sm[:, 0:24]).then_inc(sem("inverses"), 1)
            dve.wait_ge(sem("roots"), 1)
            hr = sm[:, 24:48].rearrange("p (t h) -> p t h", t=NT).unsqueeze(3).broadcast_to([P, NT, 12, HD])
            link(nc.vector.tensor_tensor(qk, qk, hr, ALU.mult))
            for t in range(NT):
                link.mark(nc.vector.tensor_tensor(qk[:, t, 0:8, :], qk[:, t, 0:8, :],
                                                  qkg[:, 0:1, :].broadcast_to([P, 8, HD]), ALU.mult))
                link.mark(nc.vector.tensor_tensor(qk[:, t, 8:12, :], qk[:, t, 8:12, :],
                                                  qkg[:, 1:2, :].broadcast_to([P, 4, HD]), ALU.mult))
            link.wait()
            for t in range(NT):
                cos = cst[:, C_COS + 32 * t:C_COS + 32 * t + 32].unsqueeze(1).broadcast_to([P, 10, 32])
                sin = cst[:, C_SIN + 32 * t:C_SIN + 32 * t + 32].unsqueeze(1).broadcast_to([P, 10, 32])
                x1, x2 = qk[:, t, 0:10, 0:32], qk[:, t, 0:10, 32:64]
                link.mark(nc.vector.tensor_tensor(ra[:, t], x1, cos, ALU.mult))
                link.mark(nc.vector.tensor_tensor(rb[:, t], x2, sin, ALU.mult))
                link.mark(nc.vector.tensor_tensor(rc[:, t], x2, cos, ALU.mult))
                link(nc.vector.tensor_tensor(rd[:, t], x1, sin, ALU.mult))
                nc.vector.tensor_tensor(x1, ra[:, t], rb[:, t], ALU.subtract).then_inc(sem("ev_rope"), 1)
                nc.vector.tensor_tensor(x2, rc[:, t], rd[:, t], ALU.add).then_inc(sem("ev_rope"), 1)
            ada_rows("ada0b", 0, 3, 4)
            dve.wait_ge(sem("ev_qkT_ps"), 2)
            nc.vector.tensor_copy(kT, pb(2)).then_inc(sem("ev_kT"), 1)

            taps_left = [(k, c) for k in range(CONVK) for c in range(2)]

            def taps(n):
                for _ in range(min(n, len(taps_left))):
                    k, c = taps_left.pop(0)
                    if k:
                        dve.wait_ge(sem("conv_dve"), 2 * (k - 1) + c + 1)
                        ins = nc.vector.scalar_tensor_tensor(cacc[:, c, :], gpad[:, c, k:k + N], cw[:, c, k:k + 1],
                                                             cacc[:, c, :], ALU.mult, ALU.add)
                    else:
                        ins = nc.vector.tensor_scalar(cacc[:, c, :], gpad[:, c, 0:N], cw[:, c, 0:1], cw[:, c, 31:32],
                                                      ALU.mult, ALU.add)
                    ins.then_inc(sem("conv_dve"), 1)

            dve.wait_ge(sem("cw"), 1)
            dve.wait_ge(sem("gpad"), 2)
            for n in range(NT * NQ):
                if n == NQ:
                    ada_rows("ada0c", 0, 7, 8)
                dve.wait_ge(sem("ev_s"), n + 1)
                nc.vector.tensor_reduce(sm[:, 64 + n:65 + n], pb(n % 4), AX.X, ALU.max, negate=True)\
                    .then_inc(sem("ev_max"), 1)
                taps(4)
                if n % 2 == 1:
                    dve.wait_ge(sem("ev_pT_ps"), n)
                    if n >= 3:
                        dve.wait_ge(sem("ev_pv"), n - 2)
                    nc.vector.tensor_copy(flat(pT[:, 0]), pb(4)).then_inc(sem("ev_pT_dve"), 1)
            taps(len(taps_left))
            for t in range(NT):
                dve.wait_ge(sem("ev_pv"), NQ * (t + 1))
                link(nc.vector.reciprocal(sm[:, 112 + 8 * t:120 + 8 * t], sm[:, 96 + 8 * t:104 + 8 * t]))
                for w in range(2):
                    nc.vector.tensor_tensor(attn[:, t, 256 * w:256 * w + 256].rearrange("p (i e) -> p i e", e=HD),
                                            pb(6 + t).rearrange("p (i w e) -> p w i e", w=2, e=HD)[:, w],
                                            sm[:, 112 + 8 * t:120 + 8 * t].rearrange("p (i w) -> p w i", w=2)[:, w]
                                            .unsqueeze(2).broadcast_to([P, 4, HD]), ALU.mult)\
                        .then_inc(sem("ev_attn"), 1)
            dve.wait_ge(sem("ada_b_in"), 16 * 16)
            for j in range(3):
                ada_rows("ada1", 4 * j, (6, 0, 1)[j], 4 * j)
            dve.wait_ge(sem("conv_dve"), 2 * CONVK)
            dve.wait_ge(sem("cv_sum"), 1)
            mu = lnrow[:, :].unsqueeze(1).broadcast_to([P, CT, N])
            link(nc.vector.tensor_scalar(lnrow[:, :], ps[:, 2, 0:N], 1.0 / 512, None, ALU.mult))
            nc.vector.tensor_tensor(cacc, cacc, mu, ALU.subtract).then_inc(sem("cv_centered"), 1)
            dve.wait_ge(sem("cv_sum"), 2)
            link(nc.vector.tensor_scalar(lnrow[:, :], ps[:, 3, 0:N], 1.0 / 512, EPS, ALU.mult, ALU.add))
            nc.vector.reciprocal(lnrow[:, :], lnrow[:, :]).then_inc(sem("inverses"), 1)
            dve.wait_ge(sem("roots"), 2)
            nc.vector.tensor_tensor(cacc, cacc, mu, ALU.mult).then_inc(sem("cv_norm"), 1)
            dve.wait_ge(sem("ev_aT_ps"), 1)
            nc.vector.tensor_copy(flat(aT[:, 0:2, :]), pb(4)).then_inc(sem("ev_aT"), 1)
            dve.wait_ge(sem("mod_cols"), 10 * 16)
            scale_col("moe0", 3, 2)
            scale_col("mix1", 7, 1)
            scale_col("moe1", 9, 3).then_inc(sem("scale_cols"), 1)
            dve.wait_ge(sem("gate_in"), 16)
            add_gated(0, "ev_out", (6, 7, 0, 1))
            dve.wait_ge(sem("scale_cols"), 2)

            def experts(l):
                name, base = f"moe{l}", FIRST[f"moe{l}"]
                scale, shift = affine(name)
                dve.wait_ge(sem("h_ready"), 4 * (l + 1))
                normed(name, h, rows)
                transposed(name, xT)
                dve.wait_ge(sem("mo_logits"), l + 1)
                nc.vector.tensor_reduce(sm[:, 130:132], ps[:, 0, 0:NT * E].rearrange("p (t e) -> p t e", t=NT), AX.X,
                                        ALU.max, negate=True).then_inc(sem("mo_max"), 1)
                dve.wait_ge(sem("mo_exp"), 2 * l + 2)
                link(nc.vector.reciprocal(sm[:, 134:136], sm[:, 132:134]))
                nc.vector.tensor_tensor(aff, aff, sm[:, 134:136].unsqueeze(2).broadcast_to([P, NT, E]), ALU.mult)\
                    .then_inc(sem("mo_aff"), 1)
                dve.wait_ge(sem("mo_affT_ps"), l + 1)
                link.mark(nc.vector.tensor_copy(affT[0:E, :], ps[0:E, 1, 0:N]))
                link(nc.vector.tensor_copy(work[0:E, :], ps[0:E, 1, 0:N]))
                for _ in range(CAP // 8):
                    link(nc.vector.max(sm[0:E, 144:152], work[0:E, :]))
                    link(nc.vector.match_replace(work[0:E, :], sm[0:E, 144:152], work[0:E, :], -1.0))
                link(nc.vector.tensor_scalar(smaskE[0:E, :], work[0:E, :], 0.0, None, ALU.is_lt))
                link(nc.vector.tensor_tensor_scan(rank[0:E, :], ones[0:E, :], smaskE[0:E, :], 0.0, ALU.mult, ALU.add))
                nc.vector.tensor_tensor(rank[0:E, :], rank[0:E, :], smaskE[0:E, :], ALU.mult).then_inc(sem("mo_rank"), 1)
                dve.wait_ge(sem("mo_rank"), l + 1)
                grp = cst[0:E, C_GRP:C_GRP + GROUPS].unsqueeze(2).broadcast_to([E, GROUPS, N])
                for v, src in ((0, rank), (1, affT)):
                    ins = nc.vector.tensor_tensor(RA[0:E, :, v, :], src[0:E, :].unsqueeze(1).broadcast_to([E, GROUPS, N]),
                                                  grp, ALU.mult)
                    if l == v == 0:
                        ins.then_inc(sem("mo_h"), 1)
                dve.wait_ge(sem("mo_rankT_ps"), l + 1)
                link(nc.vector.tensor_copy(flat(rankT), ps[:, 2, 0:NT * E]))
                iota = cst[:, C_IOTA:C_IOTA + CAP].unsqueeze(1).broadcast_to([P, E, CAP])
                for t in range(NT):
                    last = nc.vector.tensor_tensor(onehot[:, t, :].rearrange("p (e c) -> p e c", c=CAP), iota,
                                                   rankT[:, t, :].unsqueeze(2).broadcast_to([P, E, CAP]), ALU.is_equal)
                last.then_inc(sem("mo_lists"), 1)
                dve.wait_ge(sem("gate_in"), 32 * (l + 1))
                with dve.Fori(0, GROUPS) as g:
                    n = g + GROUPS * l
                    dve.wait_ge(sem("mo_gather"), 2 * n + 1)
                    for k in range(4):
                        last = nc.vector.tensor_scalar(xsT[:, k, :], ps[:, 6, P * k:P * (k + 1)], scale[:, k:k + 1],
                                                       shift[:, k:k + 1], ALU.mult, ALU.add)
                    last.then_inc(sem("mo_xsT_dve"), 1)
                    dve.wait_ge(sem("mo_affbc"), n + 1)
                    dve.wait_ge(sem("mo_comb"), 4 * n + 1)
                    nc.vector.scalar_tensor_tensor(sel_w, ps[:, 4, 0:N], cst[:, C_T:C_T + 1], aff_bc, ALU.is_equal, ALU.mult)\
                        .then_inc(sem("mo_sel"), 1)
                    dve.wait_ge(sem("mo_silu"), n + 1)
                    dve.wait_ge(sem("chunks_used"), PER_GROUP * g + (base + 2 * KD))
                    nc.vector.tensor_tensor(hid, hid, ps[:, 2:4, :].rearrange("p b f -> p (b f)"), ALU.mult)\
                        .then_inc(sem("mo_hid"), 1)
                    dve.wait_ge(sem("mo_hT_ps"), 2 * n + 2)
                    nc.vector.tensor_copy(flat(hT[:, 0:4, :]), pb(6)).then_inc(sem("mo_hT_dve"), 1)
                    dve.wait_ge(sem("chunks_used"), PER_GROUP * g + (base + 3 * KD))
                    for j in range(2):
                        nc.vector.tensor_tensor(ym[:, 512 * j:512 * j + 512], pb(4 + j), gate_bc[:, 512 * j:512 * j + 512],
                                                ALU.mult).then_inc(sem("mo_ym"), 1)
                    dve.wait_ge(sem("mo_h"), 4 * n + 1)
                    for i in range(4):
                        dve.wait_ge(sem("mo_comb"), 4 * n + i + 2)
                        t, s = i // 2, slice(512 * (i % 2), 512 * (i % 2) + 512)
                        nc.vector.tensor_tensor(h[:, t, s], h[:, t, s], pb((6, 7, 4, 5)[i]), ALU.add).then_inc(sem("mo_h"), 1)
                dve.wait_ge(sem("mo_h"), 4 * GROUPS * (l + 1) + 1)

            experts(0)

            normed("mix1", h, rows)
            transposed("mix1", xT)
            link.mark(nc.vector.memset(cx[:, :, 0:1], 0.0))
            link.mark(nc.vector.memset(cx[:, :, N + 1:N + 2], 0.0))
            dve.wait_ge(sem("sc_cw_ps"), 1)
            link(nc.vector.tensor_copy(flat(cw1), ps[:, 4, 0:KD * SCK]))
            nc.vector.tensor_copy(sm[:, 0:1], cw1[:, 0, 0:1]).then_inc(sem("sc_cw"), 1)
            for j in range(2):
                dve.wait_ge(sem("sc_bc"), 3 + j)
                whole(dve, "sc_in", 4 + j)
                for b in range(2):
                    c = 4 * j + 2 * b
                    link.mark(nc.vector.tensor_tensor(cx[:, c:c + 2, 1:N + 1], pb(2 * j + b).rearrange("p (c n) -> p c n", c=2),
                                                      cS[:, c:c + 2, :], ALU.mult))
                link.wait()
                for c in range(4 * j, 4 * j + 4):
                    link.mark(nc.vector.tensor_scalar(yS[:, c, :], cx[:, c, 0:N], cw1[:, c, 0:1], None, ALU.mult))
                for k in range(1, SCK):
                    link.wait()
                    for c in range(4 * j, 4 * j + 4):
                        link.mark(nc.vector.scalar_tensor_tensor(yS[:, c, :], cx[:, c, k:k + N], cw1[:, c, k:k + 1],
                                                                 yS[:, c, :], ALU.mult, ALU.add))
                link.wait()
                s = slice(4 * j, 4 * j + 4)
                nc.vector.tensor_tensor(yS[:, s, :], yS[:, s, :], bS[:, s, :], ALU.mult).then_inc(sem("sc_y"), 1)
            dve.wait_ge(sem("gate_in"), 48)
            add_gated(1, "sc_out", (4, 5, 6, 7))

            experts(1)

            normed("final", h, rows)
            dve.wait_ge(sem("final_in"), 16)
            dve.wait_ge(sem("norm_rows"), 2 * NORMS.index("final") + 2)
            for t in range(NT):
                nc.vector.tensor_tensor(h[:, t, :], rows[:, t, :], final_bc, ALU.mult).then_inc(sem("h_final"), 1)
            dve.wait_ge(sem("h_final"), 2)
            normed("mix2", h, rows)
            transposed("mix2", xT)
            dve.wait_ge(sem("gate2_in"), 4 * 16)
            whole(dve, "w_small")
            dve.wait_ge(sem("glr"), 1)
            lfr, lf2r = lf[0:FOXH, :], lf2[0:FOXH, :]
            link(nc.vector.tensor_scalar(lfr, ps[0:FOXH, 0, 0:N], sm[0:FOXH, 140:141], None, ALU.add))
            nc.vector.scalar_tensor_tensor(lf2r, lfr, -1.0, lfr, ALU.mult, ALU.max).then_inc(sem("gate_abs"), 1)
            dve.wait_ge(sem("gl_ps"), 1)
            for r in range(2):
                link.mark(nc.vector.tensor_scalar(glog[:, r, :], ps[:, 3, N * r:N * (r + 1)], sm[:, 141 + r:142 + r], None,
                                                  ALU.add))
            link.wait()
            nc.vector.scalar_tensor_tensor(flat(ex[:, 0]), flat(glog), -1.0, flat(glog), ALU.mult, ALU.max).then_inc(sem("gate_abs"), 1)
            dve.wait_ge(sem("gate_ln"), 1)
            link(nc.vector.scalar_tensor_tensor(lfr, lfr, 0.0, lf2r, ALU.min, ALU.subtract))
            nc.vector.tensor_tensor_scan(lf2r, ones[0:FOXH, :], lfr, 0.0, ALU.mult, ALU.add).then_inc(sem("lf_cum"), 1)
            dve.wait_ge(sem("gate_ln"), 2)
            link(nc.vector.scalar_tensor_tensor(flat(glog), flat(glog), 0.0, flat(ex[:, 0]), ALU.min, ALU.subtract))
            link(nc.vector.tensor_scalar(glog, glog, 1.0 / GLA_TAU, None, ALU.mult))
            for r in range(2):
                last = nc.vector.tensor_tensor_scan(bcum[:, r, :], scan_mask, glog[:, r, :], 0.0, ALU.mult, ALU.add)
            last.then_inc(sem("gl_cum"), 1)
            dve.wait_ge(sem("gqk"), 2)
            dve.wait_ge(sem("gl_exp"), 1)
            nc.vector.scalar_tensor_tensor(flat(gqT), flat(gqT), float(GDK) ** -0.5, flat(ex[:, 0]), ALU.mult, ALU.mult)
            nc.vector.tensor_tensor(kdec, gkT, ex[:, 1], ALU.mult).then_inc(sem("gl_dec"), 1)
            dve.wait_ge(sem("fqk"), 4)
            link(nc.vector.tensor_tensor(fsq, fqk, fqk, ALU.mult))
            link(nc.vector.tensor_reduce(sm[:, 0:32].rearrange("p (t h) -> p t h", t=NT), fsq, AX.X, ALU.add))
            link(nc.vector.tensor_scalar(sm[:, 0:32], sm[:, 0:32], 1.0 / HD, EPS, ALU.mult, ALU.add))
            nc.vector.reciprocal(sm[:, 32:64], sm[:, 0:32]).then_inc(sem("inverses"), 1)
            dve.wait_ge(sem("gl_exp"), 2)
            dve.wait_ge(sem("gl_dec"), 1)
            nc.vector.tensor_tensor(gkT, gkT, ex[:, 0], ALU.mult).then_inc(sem("gl_klast"), 1)
            dve.wait_ge(sem("gains2_in"), 5 * 16)
            link(nc.vector.tensor_scalar(foxg[:, 0, :], foxg[:, 0, :], float(HD) ** -0.5, None, ALU.mult))
            dve.wait_ge(sem("roots"), 3)
            fr = sm[:, 32:64].rearrange("p (t h) -> p t h", t=NT).unsqueeze(3).broadcast_to([P, NT, 16, HD])
            link(nc.vector.tensor_tensor(fqk, fqk, fr, ALU.mult))
            for t in range(NT):
                for w in range(2):
                    last = nc.vector.tensor_tensor(fqk[:, t, 8 * w:8 * w + 8, :], fqk[:, t, 8 * w:8 * w + 8, :],
                                                   foxg[:, w:w + 1, :].broadcast_to([P, 8, HD]), ALU.mult)
            last.then_inc(sem("fqk_normed"), 1)
            dve.wait_ge(sem("gl_klast"), 1)
            link(nc.vector.memset(AT, 0.0))
            for w in range(2):
                dve.wait_ge(sem("cols_ps"), 2 * w + 1)
                nc.vector.tensor_copy(flat(fT[:, w, 0:2, :]), pb(2 * w)).then_inc(sem("cols"), 1)
            dve.wait_ge(sem("kl_ps"), 1)
            nc.vector.tensor_copy(klrow.rearrange("p t r e -> p (t r e)"), pb(4)).then_inc(sem("klrow"), 1)
            dve.wait_ge(sem("params_in"), 17 * 16)
            for w in range(2):
                dve.wait_ge(sem("A_ps"), w + 1)
                for t in range(NT):
                    last = nc.vector.copy_predicated(AT[:, t].rearrange("p (r w) c -> p w r c", w=2)[:, w],
                                                     glam[:, :].unsqueeze(1).broadcast_to([P, 2, P]),
                                                     pb(5 + w)[:, 256 * t:256 * t + 256].rearrange("p (r c) -> p r c", r=2))
                last.then_inc(sem("AT"), 1)
            dve.wait_ge(sem("dS_ps"), 2)
            decay = sm[:, 200:208].rearrange("p (r c) -> p r c", r=2)
            dS02 = pb(7).rearrange("p (r c v) -> p r c v", r=2, c=2)
            dS1 = pb(4)[:, 0:N].rearrange("p (r v) -> p r v", r=2)
            link(nc.vector.tensor_copy(state[:, :, 0, :], dS02[:, :, 0, :]))
            for r in range(2):
                link(nc.vector.scalar_tensor_tensor(state[:, r, 1, :], state[:, r, 0, :], decay[:, r, 1:2], dS1[:, r, :],
                                                    ALU.mult, ALU.add))
            for r in range(2):
                last = nc.vector.scalar_tensor_tensor(state[:, r, 2, :], state[:, r, 1, :], decay[:, r, 2:3],
                                                      dS02[:, r, 1, :], ALU.mult, ALU.add)
            last.then_inc(sem("states"), 1)
            dve.wait_ge(sem("ccol_ps"), 1)
            ccol = sm[:, 184:200]
            nc.vector.tensor_copy(ccol, ps[:, 0, 0:16]).then_inc(sem("ccol"), 1)
            for j, b in enumerate((1, 2, 3, 5)):
                dve.wait_ge(sem("nb_ps"), j + 1)
                nc.vector.tensor_scalar(flat(NB[:, 2 * j:2 * j + 2, :]), pb(b), -1.0, None, ALU.mult).then_inc(sem("nb"), 1)
            for t in range(NT):
                dve.wait_ge(sem("go_ps"), t + 1)
                for w in range(2):
                    link.mark(nc.vector.tensor_copy(go[:, t, :].rearrange("p (r w v) -> p w r v", w=2, v=GDV)[:, w],
                                                    pb(GO[t][w])[:, 0:N].rearrange("p (r v) -> p r v", v=GDV)))
            link.wait()
            nc.vector.tensor_copy(sm[:, 208:209], go[:, 1, 0:1]).then_inc(sem("go_sb"), 1)
            gh = go.rearrange("p t (h v) -> p t h v", v=GDV)
            link(nc.vector.tensor_tensor(gsq, go, go, ALU.mult))
            link(nc.vector.tensor_reduce(sm[:, 152:160].rearrange("p (t h) -> p t h", t=NT),
                                         gsq.rearrange("p t (h v) -> p t h v", v=GDV), AX.X, ALU.add))
            link(nc.vector.tensor_scalar(sm[:, 152:160], sm[:, 152:160], 1.0 / GDV, EPS, ALU.mult, ALU.add))
            nc.vector.reciprocal(sm[:, 160:168], sm[:, 152:160]).then_inc(sem("inverses"), 1)
            dve.wait_ge(sem("roots"), 4)
            link(nc.vector.tensor_tensor(gh, gh, sm[:, 160:168].rearrange("p (t h) -> p t h", t=NT).unsqueeze(3)
                                         .broadcast_to([P, NT, GLAH, GDV]), ALU.mult))
            link(nc.vector.tensor_tensor(go, go, glag.unsqueeze(1).broadcast_to([P, NT, 512]), ALU.mult))
            dve.wait_ge(sem("gr"), 2)
            nc.vector.tensor_tensor(rows[:, :, 512:1024], go, gr, ALU.mult).then_inc(sem("mix_rows"), 1)
            dve.wait_ge(sem("nb"), 4)
            dve.wait_ge(sem("ccol"), 1)
            for n in range(NT * FOXH):
                t, hd, nk = n // FOXH, n % FOXH, P * (n // FOXH + 1)
                x = fp[:, n % 2, 0:nk]
                dve.wait_ge(sem("fx_s"), n + 1)
                if n >= 2:
                    dve.wait_ge(sem("fx_pT_ps"), n - 1)
                link(nc.vector.scalar_tensor_tensor(x, ps[:, FS[n % 4], 0:nk], ccol[:, 8 * t + hd:8 * t + hd + 1],
                                                    NB[:, hd, 0:nk], ALU.add, ALU.add))
                link(nc.vector.tensor_tensor(x[:, nk - P:nk], x[:, nk - P:nk], cst[:, C_FOX:C_FOX + P], ALU.add))
                nc.vector.tensor_reduce(sm[:, 64 + n:65 + n], x, AX.X, ALU.max, negate=True).then_inc(sem("fx_max"), 1)
                if n % 2 == 1:
                    dve.wait_ge(sem("fx_pT_ps"), n)
                    mk = P * ((n - 1) // FOXH + 1)
                    if n >= 3:
                        dve.wait_ge(sem("fx_pv"), n - 2)
                    nc.vector.tensor_copy(fpT[:, 0, 0:mk], ps[:, FTB[0], 0:mk]).then_inc(sem("fx_pT_dve"), 1)
            for t in range(NT):
                dve.wait_ge(sem("fx_pv"), FOXH * (t + 1))
                link(nc.vector.reciprocal(sm[:, 112 + 8 * t:120 + 8 * t], sm[:, 96 + 8 * t:104 + 8 * t]))
                nc.vector.tensor_tensor(rows[:, t, 0:512].rearrange("p (h e) -> p h e", e=HD),
                                        pb(FO[t]).rearrange("p (h e) -> p h e", e=HD),
                                        sm[:, 112 + 8 * t:120 + 8 * t].unsqueeze(2).broadcast_to([P, FOXH, HD]), ALU.mult)\
                    .then_inc(sem("mix_rows"), 1)
            for b in (0, 2):
                dve.wait_ge(sem("cols_ps"), 4 + b + 1)
                nc.vector.tensor_copy(flat(xT[:, 2 * b:2 * b + 2, :]), pb(b)).then_inc(sem("cols"), 1)
            add_plain("w_out", (4, 5, 6, 7))

            normed("mem", mem_rows, rows)
            transposed("mem", memT)
            def head_norm(x, tmp, c0, c1, nth, gain):
                x4 = x.rearrange("p t (h e) -> p t h e", e=XD)
                t4 = tmp.rearrange("p t (h e) -> p t h e", e=XD)
                link(nc.vector.tensor_tensor(tmp, x, x, ALU.mult))
                link(nc.vector.tensor_reduce(sm[:, c0:c0 + 8].rearrange("p (t h) -> p t h", t=NT), t4, AX.X, ALU.add))
                link(nc.vector.tensor_scalar(sm[:, c0:c0 + 8], sm[:, c0:c0 + 8], 1.0 / XD, EPS, ALU.mult, ALU.add))
                nc.vector.reciprocal(sm[:, c1:c1 + 8], sm[:, c0:c0 + 8]).then_inc(sem("inverses"), 1)
                dve.wait_ge(sem("roots"), nth)
                for t in range(NT):
                    for hd in range(XH):
                        last = nc.vector.scalar_tensor_tensor(x4[:, t, hd, :], x4[:, t, hd, :],
                                                              sm[:, c1 + 4 * t + hd:c1 + 4 * t + hd + 1], gain,
                                                              ALU.mult, ALU.mult)
                return last

            dve.wait_ge(sem("xkv"), 4)
            dve.wait_ge(sem("norm_T"), 4 * TRANSPOSED.index("mem") + 4)
            head_norm(xk, rows, 0, 32, 5, xkg).then_inc(sem("xk_normed"), 1)
            for b in (0, 2):
                dve.wait_ge(sem("cols_ps"), 8 + b + 1)
                nc.vector.tensor_copy(flat(xkT[:, 2 * b:2 * b + 2, :]), pb(b)).then_inc(sem("cols"), 1)
            dve.wait_ge(sem("h_ready"), 12)
            dve.wait_ge(sem("xk_normed"), 1)
            normed("xattn", h, rows)
            transposed("xattn", xT)
            link(nc.vector.tensor_scalar(xqg, xqg, float(XD) ** -0.5, None, ALU.mult))
            dve.wait_ge(sem("xq"), 4)
            dve.wait_ge(sem("cols_ps"), 8 + 4)
            head_norm(xq, xsq, 16, 48, 6, xqg).then_inc(sem("xq_normed"), 1)
            for b in (0, 2):
                dve.wait_ge(sem("cols_ps"), 12 + b + 1)
                nc.vector.tensor_copy(flat(xqT[:, 2 * b:2 * b + 2, :]), pb(4 + b)).then_inc(sem("cols"), 1)
            for n in range(NT * XH + 1):
                if n < NT * XH:
                    dve.wait_ge(sem("xa_s"), n + 1)
                    nc.vector.tensor_reduce(sm[:, 64 + n:65 + n], ps[:, n % 2, 0:N], AX.X, ALU.max, negate=True)\
                        .then_inc(sem("xa_max"), 1)
                if n >= 1:
                    m = n - 1
                    dve.wait_ge(sem("xa_pT_ps"), m + 1)
                    if m >= 2:
                        dve.wait_ge(sem("xa_pv"), m - 1)
                    nc.vector.tensor_copy(xpT[:, m % 2, :], ps[:, 2 + m % 2, 0:N]).then_inc(sem("xa_pT"), 1)
            dve.wait_ge(sem("xa_pv"), NT * XH)
            link(nc.vector.reciprocal(sm[:, 112:120], sm[:, 96:104]))
            for t in range(NT):
                for b in range(2):
                    nc.vector.tensor_tensor(rows[:, t, 512 * b:512 * b + 512].rearrange("p (h e) -> p h e", e=XD),
                                            pb(4 + 2 * t + b).rearrange("p (h e) -> p h e", e=XD),
                                            sm[:, 112 + 4 * t + 2 * b:114 + 4 * t + 2 * b].unsqueeze(2)
                                            .broadcast_to([P, 2, XD]), ALU.mult).then_inc(sem("xo"), 1)
            for b in (0, 2):
                dve.wait_ge(sem("cols_ps"), 16 + b + 1)
                nc.vector.tensor_copy(flat(xT[:, 2 * b:2 * b + 2, :]), pb(b)).then_inc(sem("cols"), 1)
            add_plain("wo", (4, 5, 6, 7))

            dve.wait_ge(sem("h_ready"), 16)
            normed("mlp", h, rows)
            transposed("mlp", xT)
            whole(dve, "mlp", 15)
            for t in range(NT):
                for j in range(2):
                    s = slice(512 * j, 512 * j + 512)
                    nc.vector.tensor_tensor(h[:, t, s], h[:, t, s], pb(2 * t + j), ALU.add).then_inc(sem("h_ready"), 1)

        @block.tensor
        def _(pe):
            mm = nc.tensor.matmul

            def used(ins):
                ins.then_inc(sem("chunks_used"), 1)

            def ada(name, j0, bank):
                for q in range(4):
                    i = FIRST[name] + j0 + q
                    arrived(pe, i)
                    for k in range(KD):
                        for j in range(4):
                            last = mm(ps[32 * j:32 * j + 32, bank, P * q:P * (q + 1)], sil[:, k, :],
                                      slot8(i)[:, k, P * j:P * (j + 1)], start=(k == 0), stop=(k == KD - 1))
                    used(last)

            def transposes(name, src):
                u, v, bank = NORMS.index(name), TRANSPOSED.index(name), NORM_BANKS[name]
                view = src.rearrange("p t (q k) -> p t k q", k=KD)
                pe.wait_ge(sem("norm_rows"), 2 * u + 2)
                for k in range(KD):
                    for t in range(NT):
                        last = nc.tensor.transpose(ps[:, bank[k // 2], 256 * (k % 2) + P * t:256 * (k % 2) + P * (t + 1)],
                                                   view[:, t, k, :], ident)
                    if k % 2:
                        last.then_inc(sem("norm_T"), 1)

            def normed_columns(name):
                pe.wait_ge(sem("xT_ready"), 4 * TRANSPOSED.index(name) + 4)

            def to_rows(i, lhs, banks, width=512, col=0):
                for t in range(NT):
                    for k in range(KD):
                        last = mm(ps[:, banks[t], col:col + width], lhs[:, k, P * t:P * (t + 1)], slot8(i)[:, k, 0:width],
                                  start=(k == 0), stop=(k == KD - 1))
                return last

            def to_columns(i, rhs, banks):
                for c in range(4):
                    for k in range(KD):
                        last = mm(ps[:, banks[c // 2], N * (c % 2):N * (c % 2 + 1)], slot8(i)[:, k, P * c:P * (c + 1)],
                                  rhs[:, k, :], start=(k == 0), stop=(k == KD - 1))
                return last

            def row_transposes(src, banks):
                for k in range(KD):
                    for t in range(NT):
                        last = nc.tensor.transpose(ps[:, banks[k // 2], N * (k % 2) + P * t:N * (k % 2) + P * (t + 1)],
                                                   src[:, t, P * k:P * (k + 1)], ident)
                    if k % 2:
                        last.then_inc(sem("cols_ps"), 1)

            pe.wait_ge(sem("sil"), 1)
            ada("ada0a", 0, 0)
            pe.wait_ge(sem("cst_in"), 16)
            transposes("x", rows)
            pe.wait_ge(sem("ada_rows"), 1)
            transposes("ctx", ctx_rows)
            normed_columns("x")
            normed_columns("ctx")
            pe.wait_ge(sem("params_in"), 17 * 16)
            for c in range(CT):
                last = nc.tensor.transpose(ps[:, 4, 34 * c:34 * c + 34], cwrow[0:34, P * c:P * (c + 1)], ident[0:34, 0:34])
            last.then_inc(sem("cw_ps"), 1)
            i = FIRST["ev_q"]
            arrived(pe, i)
            used(to_rows(i, xT, (0, 1)))
            i = FIRST["ev_kv"]
            arrived(pe, i)
            for bank, lhs in ((2, xT), (3, cT)):
                for t in range(NT):
                    for k in range(KD):
                        last = mm(ps[:, bank, 256 * t:256 * t + 256], lhs[:, k, P * t:P * (t + 1)], slot8(i)[:, k, 0:256],
                                  start=(k == 0), stop=(k == KD - 1))
            used(last)
            pe.wait_ge(sem("cw"), 1)
            for name, banks in (("ev_u", (4, 5)), ("ev_gate", (6, 7))):
                i = FIRST[name]
                arrived(pe, i)
                used(to_columns(i, xT, banks))
            pe.wait_ge(sem("ev_rows"), 10)
            ada("ada0b", 0, 3)
            pe.wait_ge(sem("ev_rope"), 4)
            for i in range(4):
                for t in range(NT):
                    last = nc.tensor.transpose(ps[:, i // 2, N * (i % 2) + P * t:N * (i % 2) + P * (t + 1)],
                                               qk[:, t, 2 * i:2 * i + 2, :].rearrange("p h e -> p (h e)"), ident)
            last.then_inc(sem("ev_qkT_ps"), 1)
            for s in range(4):
                last = nc.tensor.transpose(ps[:, 2, P * s:P * (s + 1)],
                                           qk[:, s % 2, 10 - 2 * (s // 2):12 - 2 * (s // 2), :].rearrange("p h e -> p (h e)"),
                                           ident)
            last.then_inc(sem("ev_qkT_ps"), 1)
            pe.wait_ge(sem("ev_qT"), 2)
            pe.wait_ge(sem("ev_kT"), 1)
            pe.wait_ge(sem("ada_rows"), 2)

            def ev_scores(m):
                t, i = m // 4, m % 4
                for w in range(2):
                    n = 2 * m + w
                    if n >= 4:
                        pe.wait_ge(sem("ev_p"), n - 3)
                    mm(pb(n % 4), qT[64 * w:64 * w + 64, i, P * t:P * (t + 1)], kT[64 * w:64 * w + 64, :],
                       start=True, stop=True).then_inc(sem("ev_s"), 1)

            def ev_transposed(n):
                pe.wait_ge(sem("ev_p"), n + 1)
                if n >= 2:
                    pe.wait_ge(sem(("ev_pT_dve", "ev_pT_act")[n % 2]), n // 2)
                for s in range(4):
                    last = nc.tensor.transpose(ps[:, 4 + n % 2, P * s:P * (s + 1)], pexp[:, n % 2, P * s:P * (s + 1)], ident)
                last.then_inc(sem("ev_pT_ps"), 1)

            def ev_values(n):
                t, i, w = n // 8, n % 8 // 2, n % 2
                pe.wait_ge(sem(("ev_pT_dve", "ev_pT_act")[w]), n // 2 + 1)
                for s in range(4):
                    last = mm(ps[:, 6 + t, 64 * (n % 8):64 * (n % 8) + 64], pT[:, w, s, :], vall[:, s, 64 * w:64 * w + 64],
                              start=(s == 0), stop=(s == 3))
                last.then_inc(sem("ev_pv"), 1)

            pe.wait_ge(sem("gpad"), 2)
            pe.wait_ge(sem("cv_gate"), 2)
            ev_scores(0)
            for n in range(NT * NQ):
                if n == NQ:
                    ada("ada0c", 0, 7)
                    pe.wait_ge(sem("ada_rows"), 3)
                if n % 2 == 0 and n // 2 + 1 < NT * NQ // 2:
                    ev_scores(n // 2 + 1)
                ev_transposed(n)
                if n:
                    ev_values(n - 1)
            ev_values(NT * NQ - 1)
            pe.wait_ge(sem("ev_attn"), 2)
            ada("ada1", 0, 6)
            ada("ada1", 4, 0)
            ada("ada1", 8, 1)
            pe.wait_ge(sem("conv_dve"), 2 * CONVK)
            pe.wait_ge(sem("conv_pool"), 2)
            pe.wait_ge(sem("ones"), 1)
            for bank, src in ((2, cacc), (3, csq)):
                if bank == 3:
                    pe.wait_ge(sem("cv_sq"), 1)
                for c in range(CT):
                    last = mm(ps[:, bank, 0:N], ones[:, 0:P], src[:, c, :], start=(c == 0), stop=(c == CT - 1))
                last.then_inc(sem("cv_sum"), 1)
            pe.wait_ge(sem("ev_attn"), 4)
            pe.wait_ge(sem("ev_pT_dve"), 8)
            pe.wait_ge(sem("ev_pT_act"), 8)
            for k in range(4):
                for t in range(NT):
                    last = nc.tensor.transpose(ps[:, 4 + k // 2, N * (k % 2) + P * t:N * (k % 2) + P * (t + 1)],
                                               attn[:, t, P * k:P * (k + 1)], ident)
                if k % 2:
                    last.then_inc(sem("ev_aT_ps"), 1)
            pe.wait_ge(sem("ev_aT"), 2)
            pe.wait_ge(sem("cv_out"), 4)
            pe.wait_ge(sem("ada_rows"), 6)
            for j in range(2):
                i = FIRST["ev_out"] + j
                arrived(pe, i)
                for t in range(NT):
                    for k in range(KD):
                        src = aT[:, k, P * t:P * (t + 1)] if k < 4 else cacc[:, k - 4, P * t:P * (t + 1)]
                        last = mm(pb(((6, 7), (0, 1))[j][t]), src, slot8(i)[:, k, :], start=(k == 0), stop=(k == KD - 1))
                used(last)

            def experts(l):
                name, base = f"moe{l}", FIRST[f"moe{l}"]
                pe.wait_ge(sem("h_ready"), 4 * (l + 1))
                transposes(name, rows)
                normed_columns(name)
                pe.wait_ge(sem("params_in"), 17 * 16)
                for t in range(NT):
                    for k in range(KD):
                        last = mm(ps[:, 0, E * t:E * (t + 1)], xT[:, k, P * t:P * (t + 1)], wr[:, l, k, :],
                                  start=(k == 0), stop=(k == KD - 1))
                last.then_inc(sem("mo_logits"), 1)
                pe.wait_ge(sem("mo_aff"), l + 1)
                for t in range(NT):
                    last = nc.tensor.transpose(ps[0:E, 1, P * t:P * (t + 1)], aff[:, t, :], ident)
                    if l == t == 0:
                        last.then_inc(sem("mo_comb"), 1)
                last.then_inc(sem("mo_affT_ps"), 1)
                pe.wait_ge(sem("mo_rank"), l + 1)
                for t in range(NT):
                    last = nc.tensor.transpose(ps[:, 2, E * t:E * (t + 1)], rank[0:E, P * t:P * (t + 1)], ident[0:E, 0:E])
                    if l == t == 0:
                        last.then_inc(sem("mo_hT_ps"), 1)
                last.then_inc(sem("mo_rankT_ps"), 1)
                pe.wait_ge(sem("mo_lists"), l + 1)
                hm = rows.rearrange("p t (q k) -> p t k q", k=KD)
                with pe.Fori(0, GROUPS) as g:
                    n = g + GROUPS * l

                    def chunk(c):
                        i = base + c
                        pe.wait_ge(sem(f"slot{i % SLOTS}_loaded"), 16 * (PER_GROUP // SLOTS) * g + 16 * (i // SLOTS + 1))
                        return slot4(i)

                    def product(c0, banks, src):
                        for k in range(KD):
                            w = chunk(c0 + k)
                            for half in range(2):
                                for j in range(EG):
                                    last = mm(ps[32 * j:32 * j + 32, banks[half], :], src[:, k, CAP * j:CAP * (j + 1)],
                                              w[:, j, 512 * half:512 * half + 512], start=(k == 0), stop=(k == KD - 1))
                            used(last)

                    pe.wait_ge(sem("mo_h"), 4 * n + 1)
                    for k in range(KD):
                        for t in range(NT):
                            last = mm(ps[:, 6 + k // 4, P * (k % 4):P * (k % 4 + 1)], hm[:, t, k, :],
                                      onehot[:, t, bass.ds(g * P, P)], start=(t == 0), stop=(t == NT - 1))
                        if k % 4 == 3:
                            last.then_inc(sem("mo_gather"), 1)
                    mm(pb(4), cst[0:E, C_E4:C_E4 + P], RA[0:E].rearrange("e g v n -> e (g v n)")[:, bass.ds(g * 2 * N, 2 * N)],
                       start=True, stop=True).then_inc(sem("mo_bc"), 1)
                    pe.wait_ge(sem("mo_xsT_dve"), n + 1)
                    pe.wait_ge(sem("mo_xsT_act"), n + 1)
                    product(0, (0, 1), xsT)
                    product(KD, (2, 3), xsT)
                    pe.wait_ge(sem("mo_hid"), n + 1)
                    for k in range(KD):
                        last = nc.tensor.transpose(ps[:, 6 + k // 4, P * (k % 4):P * (k % 4 + 1)], hid[:, P * k:P * (k + 1)],
                                                   ident)
                        if k % 4 == 3:
                            last.then_inc(sem("mo_hT_ps"), 1)
                    pe.wait_ge(sem("mo_hT_dve"), n + 1)
                    pe.wait_ge(sem("mo_hT_act"), n + 1)
                    pe.wait_ge(sem("mo_sel"), n + 1)
                    product(2 * KD, (4, 5), hT)
                    pe.wait_ge(sem("mo_ym"), 2 * n + 2)
                    for i in range(4):
                        t, half = i // 2, i % 2
                        mm(pb((6, 7, 4, 5)[i]), sel_w[:, P * t:P * (t + 1)], ym[:, 512 * half:512 * half + 512],
                           start=True, stop=True).then_inc(sem("mo_comb"), 1)
                pe.wait_ge(sem("mo_h"), 4 * GROUPS * (l + 1) + 1)

            experts(0)

            transposes("mix1", rows)
            normed_columns("mix1")
            pe.wait_ge(sem("sc_convw_in"), 16)
            for c in range(KD):
                last = nc.tensor.transpose(ps[:, 4, SCK * c:SCK * (c + 1)], cw1row[0:SCK, P * c:P * (c + 1)],
                                           ident[0:SCK, 0:SCK])
            last.then_inc(sem("sc_cw_ps"), 1)
            for j in range(6):
                i = FIRST["sc_in"] + j
                arrived(pe, i)
                if j == 2:
                    pe.wait_ge(sem("sc_cw"), 1)
                if j >= 4:
                    pe.wait_ge(sem("sc_bc"), j - 3)
                used(to_columns(i, xT, (2 * j % 8, 2 * j % 8 + 1)))
            pe.wait_ge(sem("sc_y"), 2)
            pe.wait_ge(sem("sc_bc"), 4)
            for j in range(2):
                i = FIRST["sc_out"] + j
                arrived(pe, i)
                used(to_rows(i, yS, (4 + 2 * j, 5 + 2 * j)))

            experts(1)

            transposes("mix2", rows)
            normed_columns("mix2")
            i = FIRST["w_small"]
            arrived(pe, i)
            pe.wait_ge(sem("forget_cols"), 16)
            for c0, m, col in ((0, FOXH, 0), (32, 16, N)):
                for k in range(KD):
                    last = mm(ps[0:m, 0, col:col + N], slot8(i)[:, k, c0:c0 + m], xT[:, k, :],
                              start=(k == 0), stop=(k == KD - 1))
            used(last)
            i = FIRST["w_gqk"]
            arrived(pe, i)
            used(to_columns(i, xT, (1, 2)))
            pe.wait_ge(sem("glr"), 1)
            pe.wait_ge(sem("gate2_in"), 4 * 16)
            for r in range(2):
                last = mm(ps[:, 3, N * r:N * (r + 1)], gate2[:, P * r:P * (r + 1)], glrT[0:16, :], start=True, stop=True)
            last.then_inc(sem("gl_ps"), 1)
            for name, banks in (("w_fq", (4, 5)), ("w_fk", (6, 7)), ("w_fv", (0, 1)), ("w_gv", (2, 3)), ("w_gr", (6, 7))):
                i = FIRST[name]
                arrived(pe, i)
                if name == "w_fv":
                    pe.wait_ge(sem("gate_abs"), 1)
                    pe.wait_ge(sem("gqk"), 2)
                if name == "w_gv":
                    pe.wait_ge(sem("gate_abs"), 2)
                if name == "w_gr":
                    pe.wait_ge(sem("fqk"), 4)
                used(to_rows(i, xT, banks))
            pe.wait_ge(sem("values"), 4)
            pe.wait_ge(sem("fqk_normed"), 1)
            for w in range(2):
                for r in range(4):
                    for t in range(NT):
                        last = nc.tensor.transpose(ps[:, 2 * w + r // 2, N * (r % 2) + P * t:N * (r % 2) + P * (t + 1)],
                                                   fqk[:, t, 8 * w + 2 * r:8 * w + 2 * r + 2, :].rearrange("p h e -> p (h e)"),
                                                   ident)
                    if r % 2:
                        last.then_inc(sem("cols_ps"), 1)
            pe.wait_ge(sem("gl_klast"), 1)
            for t in range(NT):
                for r in range(2):
                    last = nc.tensor.transpose(ps[:, 4, P * (2 * t + r):P * (2 * t + r + 1)], gkT[:, r, P * t:P * (t + 1)], ident)
            last.then_inc(sem("kl_ps"), 1)
            pe.wait_ge(sem("gr"), 2)
            for w in range(2):
                for t in range(NT):
                    for r in range(2):
                        s = slice(64 * w, 64 * w + 64)
                        last = mm(ps[:, 5 + w, P * (2 * t + r):P * (2 * t + r + 1)], kdec[s, r, P * t:P * (t + 1)],
                                  gqT[s, r, P * t:P * (t + 1)], start=True, stop=True)
                last.then_inc(sem("A_ps"), 1)
            pe.wait_ge(sem("klrow"), 1)
            for chunks, bank in (((0, 2), 7), ((1,), 4)):
                for c in chunks:
                    s, t = slice(GCH * (c % 2), GCH * (c % 2) + GCH), c // 2
                    for hd in range(GLAH):
                        r, w = hd // 2, hd % 2
                        col = GDV * (2 * r + c // 2) if bank == 7 else GDV * r
                        last = mm(ps[64 * w:64 * w + 64, bank, col:col + GDV], klrow[s, t, r, 64 * w:64 * w + 64],
                                  gv[s, t, GDV * hd:GDV * (hd + 1)], start=True, stop=True)
                last.then_inc(sem("dS_ps"), 1)
            pe.wait_ge(sem("cols"), 4)
            pe.wait_ge(sem("lf_cum"), 1)
            for t in range(NT):
                last = nc.tensor.transpose(ps[:, 0, FOXH * t:FOXH * (t + 1)], lf2[0:FOXH, P * t:P * (t + 1)],
                                           ident[0:FOXH, 0:FOXH])
            last.then_inc(sem("ccol_ps"), 1)
            for j, b in enumerate((1, 2, 3, 5)):
                if b == 5:
                    pe.wait_ge(sem("AT"), 2)
                for w in range(2):
                    hd = 2 * j + w
                    last = mm(ps[:, b, N * w:N * (w + 1)], ident[0:FOXH, hd:hd + 1].broadcast_to([FOXH, P]), lf2[0:FOXH, :],
                              start=True, stop=True)
                last.then_inc(sem("nb_ps"), 1)
            pe.wait_ge(sem("states"), 1)
            pe.wait_ge(sem("ccol"), 1)
            pe.wait_ge(sem("AT"), 2)
            for t in range(NT):
                for hd in range(GLAH):
                    r, w = hd // 2, hd % 2
                    for c in (2 * t, 2 * t + 1):
                        o = slice(GCH * (c % 2), GCH * (c % 2) + GCH)
                        out = ps[o, GO[t][w], GDV * r:GDV * (r + 1)]
                        last = mm(out, AT[:, t, hd, o], gv[:, t, GDV * hd:GDV * (hd + 1)], start=True, stop=(c == 0))
                        if c:
                            last = mm(out, gqT[64 * w:64 * w + 64, r, GCH * c:GCH * (c + 1)],
                                      state[64 * w:64 * w + 64, r, c - 1, :], start=False, stop=True)
                last.then_inc(sem("go_ps"), 1)

            def fox_scores(m):
                t, r = m // 4, m % 4
                for w in range(2):
                    n = 2 * m + w
                    if n >= 4:
                        pe.wait_ge(sem("fx_max"), n - 3)
                    s, nk = slice(64 * w, 64 * w + 64), P * (t + 1)
                    mm(ps[:, FS[n % 4], 0:nk], fT[s, 0, r, P * t:P * (t + 1)], fT[s, 1, r, 0:nk],
                       start=True, stop=True).then_inc(sem("fx_s"), 1)

            def fox_transposed(n):
                pe.wait_ge(sem("fx_p"), n + 1)
                if n >= 2:
                    pe.wait_ge(sem(("fx_pT_dve", "fx_pT_act")[n % 2]), n // 2)
                for s in range(n // FOXH + 1):
                    last = nc.tensor.transpose(ps[:, FTB[n % 2], P * s:P * (s + 1)], fp[:, n % 2, P * s:P * (s + 1)], ident)
                last.then_inc(sem("fx_pT_ps"), 1)

            def fox_values(n):
                t, hd = n // FOXH, n % FOXH
                pe.wait_ge(sem(("fx_pT_dve", "fx_pT_act")[n % 2]), n // 2 + 1)
                for s in range(t + 1):
                    last = mm(ps[:, FO[t], HD * hd:HD * (hd + 1)], fpT[:, n % 2, P * s:P * (s + 1)],
                              fv[:, s, HD * hd:HD * (hd + 1)], start=(s == 0), stop=(s == t))
                last.then_inc(sem("fx_pv"), 1)

            pe.wait_ge(sem("nb"), 4)
            pe.wait_ge(sem("AT"), 2)
            pe.wait_ge(sem("go_sb"), 1)
            fox_scores(0)
            for n in range(NT * FOXH):
                if n % 2 == 0 and n // 2 + 1 < NT * FOXH // 2:
                    fox_scores(n // 2 + 1)
                fox_transposed(n)
                if n:
                    fox_values(n - 1)
            fox_values(NT * FOXH - 1)
            pe.wait_ge(sem("mix_rows"), 3)
            row_transposes(rows, (0, 1, 2, 3))
            pe.wait_ge(sem("cols"), 8)
            for j in range(2):
                i = FIRST["w_out"] + j
                arrived(pe, i)
                used(to_rows(i, xT, (4 + 2 * j, 5 + 2 * j)))

            pe.wait_ge(sem("h_ready"), 12)
            transposes("mem", rows)
            normed_columns("mem")
            for j in range(4):
                i = FIRST["wkv"] + j
                arrived(pe, i)
                banks = ((2 * j + 4) % 8, (2 * j + 5) % 8)
                used(to_rows(i, memT, banks))
            pe.wait_ge(sem("xk_normed"), 1)
            pe.wait_ge(sem("xkv"), 8)
            row_transposes(xk, (0, 1, 2, 3))
            transposes("xattn", rows)
            normed_columns("xattn")
            pe.wait_ge(sem("cols"), 12)
            for j in range(2):
                i = FIRST["wq"] + j
                arrived(pe, i)
                used(to_rows(i, xT, (2 * j, 2 * j + 1)))
            pe.wait_ge(sem("xq_normed"), 1)
            row_transposes(xq, (4, 5, 6, 7))
            pe.wait_ge(sem("cols"), 16)

            def x_scores(n):
                t, hd = n // XH, n % XH
                if n >= 2:
                    pe.wait_ge(sem("xa_p"), n - 1)
                for kk in range(2):
                    last = mm(ps[:, n % 2, 0:N], xqT[:, 2 * hd + kk, P * t:P * (t + 1)], xkT[:, 2 * hd + kk, :],
                              start=(kk == 0), stop=(kk == 1))
                last.then_inc(sem("xa_s"), 1)

            def x_transposed(n):
                pe.wait_ge(sem("xa_p"), n + 1)
                if n >= 2:
                    pe.wait_ge(sem("xa_pT"), n - 1)
                for s in range(2):
                    last = nc.tensor.transpose(ps[:, 2 + n % 2, P * s:P * (s + 1)], xp[:, n % 2, P * s:P * (s + 1)], ident)
                last.then_inc(sem("xa_pT_ps"), 1)

            def x_values(n):
                t, hd = n // XH, n % XH
                pe.wait_ge(sem("xa_pT"), n + 1)
                for s in range(2):
                    last = mm(ps[:, 4 + 2 * t + hd // 2, XD * (hd % 2):XD * (hd % 2) + XD], xpT[:, n % 2, P * s:P * (s + 1)],
                              xv[:, s, XD * hd:XD * (hd + 1)], start=(s == 0), stop=(s == 1))
                last.then_inc(sem("xa_pv"), 1)

            x_scores(0)
            for n in range(NT * XH):
                if n + 1 < NT * XH:
                    x_scores(n + 1)
                x_transposed(n)
                if n:
                    x_values(n - 1)
            x_values(NT * XH - 1)
            pe.wait_ge(sem("xo"), 4)
            row_transposes(rows, (0, 1, 2, 3))
            pe.wait_ge(sem("cols"), 20)
            for j in range(2):
                i = FIRST["wo"] + j
                arrived(pe, i)
                used(to_rows(i, xT, (4 + 2 * j, 5 + 2 * j)))

            pe.wait_ge(sem("h_ready"), 16)
            transposes("mlp", rows)
            normed_columns("mlp")

            def up(j):
                i = FIRST["mlp"] + 2 * j
                arrived(pe, i)
                if j >= 2:
                    pe.wait_ge(sem("mlp_relu"), j - 1)
                return to_columns(i, xT, (4 + 2 * (j % 2), 5 + 2 * (j % 2)))

            def down(j):
                i = FIRST["mlp"] + 2 * j + 1
                arrived(pe, i)
                pe.wait_ge(sem("mlp_uT"), j + 1)
                for k in range(4):
                    for t in range(NT):
                        for half in range(2):
                            last = mm(pb(2 * t + half), uT[:, j % 2, k, P * t:P * (t + 1)],
                                      slot4(i)[:, k, 512 * half:512 * half + 512],
                                      start=(j == 0 and k == 0), stop=(j == 7 and k == 3))
                return last

            for j in range(8):
                used(up(j))
                used(down(j))


_WEIGHTS = ['x', 'c', 'ctx', 'c_ctx', 'ada_w', 'ada_b', 'norm1_g', 'norm2_g', 'ev_w_in', 'ev_q_g', 'ev_k_g', 'ev_conv_w',
            'ev_conv_b', 'ev_ln_g', 'ev_ln_b', 'ev_w_out', 'sc_w_in', 'sc_conv_w', 'sc_w_out', 'moe_w_r', 'moe_w_gate',
            'moe_w_up', 'moe_w_down', 'final_g', 'mem_2', 'norm_mix_g_2', 'w_in_2', 'fox_b_f_2', 'fox_q_norm_g_2',
            'fox_k_norm_g_2', 'gla_w_gate2_2', 'gla_b_gate_2', 'gla_out_norm_g_2', 'w_out_2', 'norm_xattn_g_2',
            'norm_mem_g_2', 'xattn_wq_2', 'xattn_wkv_2', 'xattn_q_norm_g_2', 'xattn_k_norm_g_2', 'xattn_wo_2',
            'norm_mlp_g_2', 'mlp_w1_2', 'mlp_w2_2']


def kernel(**inputs):
    import concourse.bacc as bacc
    from concourse.bass_utils import run_bass_kernel_spmd

    nc = bacc.Bacc("TRN2", target_bir_lowering=False, num_devices=1)
    arrays = {n: np.ascontiguousarray(inputs[n]) for n in _WEIGHTS}
    arrays["cst"], arrays["cst_i"] = constants()
    a = {n: nc.dram_tensor(f"in_{n}", v.shape, mybir.dt.from_np(v.dtype), kind="ExternalInput").ap()
         for n, v in arrays.items()}
    a["out"] = nc.dram_tensor("out", (1, N, D), F32, kind="ExternalOutput").ap()
    build(nc, a)
    r = run_bass_kernel_spmd(nc, [{f"in_{n}": v for n, v in arrays.items()}], core_ids=[0])
    return r.results[0]["out"]
```

```python
import numpy as np
import concourse.bass as bass
from concourse import mybir
from contextlib import ExitStack

F32 = mybir.dt.float32
I32 = mybir.dt.int32
F32R = mybir.dt.float32r
ACT = mybir.ActivationFunctionType
ALU = mybir.AluOpType
AX = mybir.AxisListType

P = 128
D = 1024
N = 256
NT = N // P
KD = D // P
EPS = 1e-6
HD = 64
NQ, NKV = 8, 2
AW = NQ * HD
CONVK = 31
CT = 4
PADW = N + CONVK - 1
SCK = 3
E, CAP, F = 16, 32, 1024
EG = 4
GROUPS = E // EG
FOXH, GLAH, GDK, GDV, GCH = 8, 4, 64, 128, 64
GLA_TAU = 16.0
XH, XD = 4, 256
SLOTS = 8
SLOT = 4096
MASKED = -1e30

C_ID, C_FOX, C_COS, C_SIN, C_T, C_IOTA, C_SCAN, C_E4, C_GRP = 0, 128, 256, 320, 384, 385, 417, 673, 801
C_W = 805

ADA = ["ada0a", "ada0b", "ada0c", "ada1a", "ada1b", "ada1c"]
NORMS = ["x", "ctx", "moe0", "mem", "mix1", "moe1", "final", "mix2", "xattn", "mlp"]
TRANSPOSED = [n for n in NORMS if n != "final"]


def constants():
    c = np.zeros((P, C_W), np.float32)
    p = np.arange(P)
    c[:, C_ID:C_ID + P] = np.eye(P, dtype=np.float32)
    c[:, C_FOX:C_FOX + P] = np.where(p[None, :] <= p[:, None], 0.0, MASKED)
    half = np.float32(32)
    inv = np.float32(10000.0) ** (-np.arange(0, 32, 2, dtype=np.float32) / half)
    n = np.arange(N)
    ang = np.concatenate([(n // 64).astype(np.float32)[:, None] * inv,
                          (n % 64).astype(np.float32)[:, None] * inv], axis=1).astype(np.float32)
    for t in range(NT):
        c[:, C_COS + 32 * t:C_COS + 32 * t + 32] = np.cos(ang[t * P:(t + 1) * P])
        c[:, C_SIN + 32 * t:C_SIN + 32 * t + 32] = np.sin(ang[t * P:(t + 1) * P])
    c[:, C_T] = p % CAP + 1
    c[:, C_IOTA:C_IOTA + CAP] = np.arange(CAP) + 1
    c[:, C_SCAN:C_SCAN + N] = (n % GCH != 0)
    e = np.arange(E)
    c[0:E, C_E4:C_E4 + P] = (p[None, :] // CAP == e[:, None] % EG)
    c[0:E, C_GRP:C_GRP + GROUPS] = (np.arange(GROUPS)[None, :] == e[:, None] // EG)
    m = ((p[:, None] // GCH == p[None, :] // GCH) & (p[:, None] <= p[None, :])).astype(np.int32)
    return c, m


STREAM = [("ada0a", 4), ("ev_q", 1), ("ev_kv", 1), ("ev_u", 1), ("ev_gate", 1),
          ("ada0b", 4), ("ada0c", 4), ("ada1a", 4), ("ada1b", 4), ("ada1c", 4), ("ev_out", 2), ("moe0", 48), ("wkv", 4), ("moe0b", 48),
          ("sc_in", 6), ("sc_out", 2), ("moe1", 96),
          ("w_small", 1), ("w_gqk", 1), ("w_fq", 1), ("w_fk", 1), ("w_fv", 1), ("w_gv", 1), ("w_gr", 1),
          ("w_out", 2), ("wq", 2), ("wo", 2), ("mlp", 16)]
FIRST = {}
_n = 0
for _name, _k in STREAM:
    FIRST[_name] = _n
    _n += _k
PER_GROUP = 3 * KD
assert PER_GROUP % SLOTS == 0
LOOPS = [(0, 0, 2, FIRST["moe0"]), (0, 2, GROUPS, FIRST["moe0b"] - 2 * PER_GROUP), (1, 0, GROUPS, FIRST["moe1"])]


def build(nc, a):
    ctx = ExitStack()
    with ctx:
        place = {}

        def sb(name, shape, dt=F32):
            place[name] = -(-nc.sbuf_base // 32) * 32
            return ctx.enter_context(nc.sbuf_tensor(name, shape, dt))

        def parts_of(name, floats, first=0):
            return nc.alloc_sbuf_tensor_at(f"{name}_parts_{first}", [P, floats], F32R, offset=place[name] + 4 * first)[:, :]

        sems = {}

        def sem(name):
            if name not in sems:
                sems[name] = ctx.enter_context(nc.semaphore(name))
            return sems[name]

        ring = sb("ring", [P, SLOTS, SLOT])
        h_t = sb("h", [P, NT * D])
        rows_t = sb("rows", [P, NT * D])
        xT_t = sb("xT", [P, KD * N])
        cst = sb("cst", [P, C_W])
        glam = sb("gla_mask", [P, P], I32)
        gcol = sb("gain_cols", [P, 8 + SCK, KD])
        mcol = sb("mod_cols", [P, 10, KD])
        acol = sb("scale_cols", [P, 5, KD])
        wr = sb("router_w", [P, 2, KD, E])
        gate_bc = sb("gate_bc", [P, 1280])
        ss = sb("ss", [P, len(NORMS), NT])
        ms = sb("ms", [P, len(NORMS), NT])
        rstd = sb("rstd", [P, len(NORMS), NT])
        mhalf = sb("mhalf", [P, NT])
        sil = sb("silu_c", [P, KD, 32])
        ones = sb("ones", [P, N])
        lnrow = sb("ln_row", [P, N])
        sm = sb("small", [P, 256])
        scr = sb("scratch", [P, 10496])
        ps = ctx.enter_context(nc.psum_tensor("ps", [P, 8, 512], F32))
        memk_dram = nc.dram_tensor("memory_keys", (P, KD * N), F32).ap()
        memv_dram = nc.dram_tensor("memory_values", (P, NT * D), F32).ap()
        gate_dram = nc.dram_tensor("gate_scratch", (2, 2, D), F32).ap()

        h = h_t[:, :].rearrange("p (t d) -> p t d", t=NT)
        rows = rows_t[:, :].rearrange("p (t d) -> p t d", t=NT)
        xT = xT_t[:, :].rearrange("p (k n) -> p k n", k=KD)
        ident = cst[:, C_ID:C_ID + P]
        scan_mask = cst[:, C_SCAN:C_SCAN + N]

        def at(off, **dims):
            n = 1
            for v in dims.values():
                n *= v
            v = scr[:, off:off + n]
            if len(dims) == 1:
                return v
            names = " ".join(dims)
            return v.rearrange(f"p ({names}) -> p {names}", **dims)

        mrow = at(0, b=3, q=4, i=P)
        ctx_rows = at(1536, t=NT, d=D)
        cT = at(3584, k=KD, n=N)
        qk = at(5632, t=NT, h=12, e=HD)
        vall = at(7168, t=4, e=128)
        gpad = at(7680, c=CT, n=PADW)
        sg = cacc = at(8824, c=CT, n=N)
        csq = at(5632, c=CT, n=N)
        cw = at(9848, c=CT, j=34)
        cwrow = at(8824, d=512)
        grow = at(9336, i=P)
        crow = at(9464, i=P)
        ada_b = at(9984, i=512)
        sq = rows_t[:, 0:1536].rearrange("p (t h e) -> p t h e", t=NT, h=12)
        ra = rows_t[:, 0:640].rearrange("p (t h e) -> p t h e", t=NT, h=10)
        rb = rows_t[:, 640:1280].rearrange("p (t h e) -> p t h e", t=NT, h=10)
        rc = at(3584, t=NT, h=10, e=32)
        rd = at(4224, t=NT, h=10, e=32)
        kT = at(1536, s=512)
        qT = at(2048, i=4, n=N)
        pexp = at(3584, b=2, s=512)
        pT = at(4608, b=2, s=4, q=P)
        attn = xT_t[:, 0:1024].rearrange("p (t e) -> p t e", t=NT)
        aT = xT_t[:, 1024:2048].rearrange("p (k n) -> p k n", k=4)
        xsT = at(0, k=KD, c=P)
        hid = at(1024, f=F)
        hT = at(2048, k=KD, c=P)
        ym = at(3072, d=D)
        sel_w = at(4096, n=N)
        aff_bc = at(4352, n=N)
        RA = at(4608, g=GROUPS, v=2, n=N)
        onehot = at(6656, t=NT, s=E * CAP)
        affT = at(7680, n=N)
        work = at(7936, n=N)
        rank = at(8192, n=N)
        final_bc = at(8448, d=D)
        aff = at(9472, t=NT, e=E)
        rankT = at(9504, t=NT, e=E)
        smaskE = at(9600, n=N)
        bS = at(0, c=KD, n=N)
        cS = at(2048, c=KD, n=N)
        cx = at(4096, c=KD, n=N + 2)
        yS = at(6160, c=KD, n=N)
        gqT = at(0, r=2, n=N)
        gkT = at(512, r=2, n=N)
        kdec = at(1024, r=2, n=N)
        glog = at(1536, r=2, n=N)
        bcum = at(2048, r=2, n=N)
        ex = at(2560, x=2, r=2, n=N)
        AT = at(2560, t=NT, h=GLAH, c=P)
        gv = at(3584, t=NT, e=512)
        gr = at(4608, t=NT, e=512)
        klrow = at(5632, t=NT, r=2, e=P)
        state = at(6144, r=2, n=3, v=GDV)
        fqk = at(6912, t=NT, h=16, e=HD)
        NB = at(6912, h=FOXH, n=N)
        fv = at(8960, t=NT, e=512)
        fp = at(5632, b=2, s=N)
        fpT = at(9984, b=2, s=N)
        lf = wr[:, :, :, :].rearrange("p l k e -> p (l k e)")
        lf2 = lnrow[:, :]
        glrT = sil[:, :, :].rearrange("p k v -> p (k v)")
        fsq = rows_t[:, :].rearrange("p (t h e) -> p t h e", t=NT, h=16)
        fT = xT_t[:, :].rearrange("p (w r n) -> p w r n", w=2, r=4)
        gsq = at(0, t=NT, e=512)
        go = at(1024, t=NT, e=512)
        mem_rows = by_rows = xT_t[:, :].rearrange("p (t d) -> p t d", t=NT)
        xk = at(0, t=NT, d=D)
        memT = at(2048, k=KD, n=N)
        memkT = at(2048, k=KD, n=N)
        memv = by_rows
        xv = at(6144, t=NT, d=D)
        xkT = at(8192, k=KD, n=N)
        xq = at(0, t=NT, d=D)
        xqT = at(2048, k=KD, n=N)
        xp = at(0, b=2, s=N)
        xpT = at(512, b=2, s=N)
        xsq = at(4096, t=NT, d=D)
        ring_r = [parts_of("ring", SLOT, SLOT * i) for i in range(SLOTS)]
        xT_r = parts_of("xT", KD * N).rearrange("p (k n) -> p k n", k=KD)

        uT = at(0, b=2, k=4, n=N)
        uT_lo = parts_of("scratch", 2048, 0).rearrange("p (b k n) -> p b k n", b=2, k=4)
        uT_hi = parts_of("scratch", 2048, 2048).rearrange("p (b k n) -> p b k n", b=2, k=4)
        xT_hi = parts_of("scratch", 2048, 4096).rearrange("p (k n) -> p k n", k=KD)
        w_hi = [parts_of("scratch", 2048, 6144), parts_of("scratch", 2048, 8192), parts_of("rows", 2048)]

        class Steps:

            def __init__(self, eng, name):
                self.eng, self.sem, self.n = eng, sem(name), 0

            def mark(self, ins):
                ins.then_inc(self.sem, 1)
                self.n += 1

            def wait(self):
                self.eng.wait_ge(self.sem, self.n)

            def __call__(self, ins):
                self.mark(ins)
                self.wait()

        def arrived(eng, i):
            eng.wait_ge(sem(f"slot{i % SLOTS}_loaded"), 16 * (i // SLOTS + 1))

        def whole(eng, name, j=0):
            eng.wait_ge(sem("chunks_used"), FIRST[name] + j + 1)

        def slot8(i):
            return ring[:, i % SLOTS, :].rearrange("p (k n) -> p k n", k=KD)

        def slot2(i):
            return ring[:, i % SLOTS, :].rearrange("p (k n) -> p k n", k=2)

        def slot4(i):
            return ring[:, i % SLOTS, :].rearrange("p (e f) -> p e f", e=EG)

        def pb(b):
            return ps[:, b, :]

        def flat(v):
            return v.rearrange("p a b -> p (a b)")

        def by_token(v):
            return v.rearrange("p (t d) -> p t d", t=NT)

        MODS = {"x": 1, "ctx": 1, "moe0": 3, "mix1": 4, "moe1": 6}
        SHIFT = {"x": 0, "ctx": 4, "moe0": 2, "mix1": 6, "moe1": 8}
        SCALE = {"x": 0, "ctx": 1, "moe0": 2, "mix1": 3, "moe1": 4}
        GAIN = {"mix2": 4, "mem": 5, "xattn": 6, "mlp": 7}

        def affine(name):
            if name in SHIFT:
                return acol[:, SCALE[name], :], mcol[:, SHIFT[name], :]
            return gcol[:, GAIN[name], :], None

        NORM_BANKS = {n: (4, 5, 6, 7) for n in TRANSPOSED}
        NORM_BANKS["ctx"] = (0, 1, 2, 3)
        qkg = gate_bc[:, 1024:1152].rearrange("p (w e) -> p w e", w=2)
        foxg = gate_bc[:, 0:128].rearrange("p (w e) -> p w e", w=2)
        glag = gate_bc[:, 128:640]
        xqg, xkg = gate_bc[:, 640:896], gate_bc[:, 1024:1280]
        gate2 = at(6912, n=N)[0:16, :]
        FS, FTB, FO = (1, 2, 3, 5), (6, 7), (0, 4)
        GAINS = (8 + SCK) * KD
        cw1 = gcol[:, 8:8 + SCK, :].rearrange("p j c -> p c j")
        PARAMS = 10
        LN_AT = 12
        GO = ((0, 6), (4, 7))

        MLP = [("up", 0)]
        for j in range(8):
            MLP += [("up", j + 1)] * (j < 7) + [("down", j)]

        def mlp_halves(kind, j):
            m = MLP.index((kind, j))
            i = FIRST["mlp"] + m
            whole_chunk, lo_chunk = ring[:, i % SLOTS, :], ring_r[i % SLOTS]
            for half in range(2):
                hi = w_hi[(2 * m + half) % 3]
                if kind == "up":
                    w, lo = (v.rearrange("p (k n) -> p k n", k=KD)[:, :, 256 * half:256 * half + 256]
                             for v in (whole_chunk, lo_chunk))
                    hi = hi.rearrange("p (k n) -> p k n", k=KD)
                else:
                    w, lo = (v.rearrange("p (k n) -> p k n", k=4)[:, 2 * half:2 * half + 2, :]
                             for v in (whole_chunk, lo_chunk))
                    hi = hi.rearrange("p (k n) -> p k n", k=2)
                yield 2 * m + half, i, w, lo, hi

        block = ctx.enter_context(nc.Block())

        @block.sync
        def _(sp):
            def load(i, dst, src):
                if i >= SLOTS:
                    sp.wait_ge(sem("chunks_used"), i - SLOTS + 1)
                sp.dma_start(dst, src).then_inc(sem(f"slot{i % SLOTS}_loaded"), 16)

            def columns(name, w, count, width=512, col0=0):
                v = w.rearrange("(k p) n -> p k n", k=KD)
                for j in range(count):
                    i, c = FIRST[name] + j, col0 + width * j
                    load(i, slot8(i)[:, :, 0:width], v[:, :, c:c + width])

            def modulations(g, chunks=(0, 1, 2, 3)):
                v = a["ada_w"][g // 3].rearrange("(c k p) n -> c p k n", c=4, p=P)
                for c in chunks:
                    i = FIRST[ADA[g]] + c
                    load(i, slot2(i), v[c, :, :, 2 * D * (g % 3):2 * D * (g % 3 + 1)])

            def experts(loop):
                l, g0, g1, base = loop
                gate = a["moe_w_gate"][l].rearrange("(g e) (k p) f -> g k p e f", e=EG, k=KD)
                up = a["moe_w_up"][l].rearrange("(g e) (k p) f -> g k p e f", e=EG, k=KD)
                down = a["moe_w_down"][l].rearrange("(g e) (k p) d -> g k p e d", e=EG, p=P)
                with sp.Fori(g0, g1) as g:
                    for c in range(PER_GROUP):
                        w, k = (gate, up, down)[c // KD], c % KD
                        sp.wait_ge(sem("chunks_used"), PER_GROUP * g + (base + c - SLOTS + 1))
                        sp.dma_start(slot4(base + c), w[g, k])\
                            .then_inc(sem(f"slot{(base + c) % SLOTS}_loaded"), 16)

            for v, c in enumerate((a["c"][0], a["c_ctx"])):
                sp.dma_start(crow[KD * v:KD * (v + 1), :], c.rearrange("(k p) -> k p", k=KD)).then_inc(sem("c_in"), 16)
            sp.dma_start(ident, a["cst"][:, C_ID:C_ID + P]).then_inc(sem("c_in"), 16)
            first = 0
            for g in (a["norm1_g"], a["norm2_g"], a["norm_mix_g_2"].unsqueeze(0), a["norm_mem_g_2"].unsqueeze(0),
                      a["norm_xattn_g_2"].unsqueeze(0), a["norm_mlp_g_2"].unsqueeze(0), a["sc_conv_w"][0]):
                n = KD * g.shape[0]
                sp.dma_start(grow[first:first + n, :], g.rearrange("l (k p) -> (l k) p", k=KD)).then_inc(sem("gains_in"), 16)
                first += n
            sp.wait_ge(sem("cleared"), 2)
            sp.dma_start(ada_b[0:24, :], a["ada_b"].rearrange("l (q n) -> (l q) n", n=512)).then_inc(sem("ada_b_in"), 16)
            modulations(0, (0, 1))
            sp.dma_start(h, a["x"][0].rearrange("(t p) d -> p t d", p=P)).then_inc(sem("x_in"), 16)
            modulations(0, (2, 3))
            sp.dma_start(ctx_rows, a["ctx"][0].rearrange("(t p) d -> p t d", p=P)).then_inc(sem("ctx_in"), 16)
            evw = a["ev_w_in"][0]
            columns("ev_q", evw, 1)
            columns("ev_kv", evw, 1, width=256, col0=512)
            columns("ev_u", evw, 1, col0=768)
            columns("ev_gate", evw, 1, col0=1280)
            for g in range(1, len(ADA)):
                modulations(g)
            columns("ev_out", a["ev_w_out"][0], 2)
            experts(LOOPS[0])
            columns("wkv", a["xattn_wkv_2"], 4)
            experts(LOOPS[1])
            columns("sc_in", a["sc_w_in"][0], 6)
            columns("sc_out", a["sc_w_out"][0], 2)
            experts(LOOPS[2])
            w2 = a["w_in_2"]
            i = FIRST["w_small"]
            v = w2.rearrange("(k p) n -> p k n", k=KD)
            sp.wait_ge(sem("chunks_used"), i - SLOTS + 1)
            sp.dma_start(slot8(i)[:, :, 0:8], v[:, :, 1536:1544]).then_inc(sem("forget_cols"), 16)
            sp.dma_start(slot8(i)[:, :, 32:48], v[:, :, 2568:2584]).then_inc(sem(f"slot{i % SLOTS}_loaded"), 16)
            for name, col in (("w_gqk", 1544), ("w_fq", 0), ("w_fk", 512), ("w_fv", 1024), ("w_gv", 2056), ("w_gr", 2584)):
                columns(name, w2, 1, col0=col)
            columns("w_out", a["w_out_2"], 2)
            columns("wq", a["xattn_wq_2"], 2)
            columns("wo", a["xattn_wo_2"], 2)
            w1 = a["mlp_w1_2"].rearrange("(k p) f -> p k f", k=KD)
            wd = a["mlp_w2_2"].rearrange("(c k p) d -> c p k d", k=4, p=P)
            for m, (kind, j) in enumerate(MLP):
                i = FIRST["mlp"] + m
                if m < SLOTS:
                    sp.wait_ge(sem("chunks_used"), i - SLOTS + 1)
                else:
                    sp.wait_ge(sem("w_halves_used"), 2 * (m - SLOTS) + 2)
                dst, src = (slot8(i), w1[:, :, 512 * j:512 * (j + 1)]) if kind == "up" else (slot4(i), wd[j])
                sp.dma_start(dst, src).then_inc(sem(f"slot{i % SLOTS}_loaded"), 16)
            for t in range(NT):
                sp.wait_ge(sem("h_ready"), 16 + 2 * t + 2)
                sp.dma_start(a["out"][0, t * P:(t + 1) * P, :], h[:, t, :]).then_inc(sem("stored"), 16)
            sp.wait_ge(sem("stored"), 16 * NT)

        @block.scalar
        def _(act):
            link = Steps(act, "act_steps")

            act.dma_start(cwrow[0:CONVK, :], a["ev_conv_w"][0]).then_inc(sem("params_in"), 16)
            for j, n in enumerate(("ev_conv_b", "ev_ln_g", "ev_ln_b")):
                act.dma_start(cwrow[CONVK + j:CONVK + j + 1, :], a[n]).then_inc(sem("params_in"), 16)
            for j, n in enumerate(("ev_q_g", "ev_k_g")):
                act.dma_start(qkg[:, j, :], a[n][0].partition_broadcast(P)).then_inc(sem("params_in"), 16)
            act.dma_start(cst[:, C_FOX:], a["cst"][:, C_FOX:]).then_inc(sem("params_in"), 16)
            for l in range(2):
                act.dma_start(wr[:, l], a["moe_w_r"][l].rearrange("(k p) e -> p k e", k=KD)).then_inc(sem("params_in"), 16)
            act.dma_start(glam[:, :], a["cst_i"]).then_inc(sem("params_in"), 16)

            act.wait_ge(sem("c_ps"), 1)
            act.wait_ge(sem("cleared"), 1)
            nc.scalar.activation(sil[:, :, 0:2], ps[:, 2, 0:2 * KD].rearrange("p (v k) -> p k v", v=2), ACT.Silu)\
                .then_inc(sem("sil"), 1)

            def squares(name, src, junk):
                u = NORMS.index(name)
                for t in range(NT):
                    nc.scalar.activation(junk[:, t, :], src[:, t, :], ACT.Square,
                                         accum_out=ss[:, u, t:t + 1]).then_inc(sem("norm_ss"), 1)

            def transposed(name, dst):
                v, bank, (scale, shift) = TRANSPOSED.index(name), NORM_BANKS[name], affine(name)
                if name in MODS:
                    act.wait_ge(sem("mod_cols"), MODS[name])
                for b in (1, 3):
                    act.wait_ge(sem("norm_T"), 4 * v + b + 1)
                    for k in (2 * b, 2 * b + 1):
                        src = ps[:, bank[b], 256 * (k % 2):256 * (k % 2) + 256]
                        if shift is None:
                            last = nc.scalar.activation(dst[:, k, :], src, ACT.Copy, scale=scale[:, k:k + 1])
                        else:
                            last = nc.scalar.activation(dst[:, k, :], src, ACT.Identity, scale=scale[:, k:k + 1],
                                                        bias=shift[:, k:k + 1])
                    last.then_inc(sem("xT_ready"), 1)

            xT_rows = by_token(xT_t[:, :])

            act.wait_ge(sem("x_in"), 16)
            squares("x", h, xT_rows)
            act.wait_ge(sem("ctx_in"), 16)
            squares("ctx", ctx_rows, by_token(flat(cT)))
            transposed("x", xT)
            transposed("ctx", cT)
            whole(act, "ev_q")
            for t in range(NT):
                nc.scalar.activation(qk[:, t, 0:NQ, :].rearrange("p (i w) e -> p w i e", w=2),
                                     pb(t).rearrange("p (w i e) -> p w i e", w=2, e=HD), ACT.Copy)\
                    .then_inc(sem("ev_rows"), 1)
            whole(act, "ev_kv")
            for w, bank in ((0, 2), (1, 3)):
                for t in range(NT):
                    src = ps[:, bank, 256 * t:256 * t + 256]
                    nc.scalar.activation(qk[:, t, 8 + 2 * w:10 + 2 * w, :],
                                         src[:, 0:128].rearrange("p (h e) -> p h e", e=HD), ACT.Copy)\
                        .then_inc(sem("ev_rows"), 1)
                    nc.scalar.activation(vall[:, 2 - 2 * w + t, :], src[:, 128:256], ACT.Copy).then_inc(sem("ev_rows"), 1)
            act.wait_ge(sem("inverses"), 1)
            nc.scalar.activation(sm[:, 24:48], sm[:, 24:48], ACT.Sqrt).then_inc(sem("roots"), 1)
            whole(act, "ev_gate")
            for j in range(2):
                nc.scalar.activation(flat(sg[:, 2 * j:2 * j + 2, :]), pb(6 + j), ACT.Sigmoid).then_inc(sem("cv_gate"), 1)
            act.wait_ge(sem("ev_qkT_ps"), 1)
            for b in range(2):
                nc.scalar.activation(flat(qT[:, 2 * b:2 * b + 2, :]), pb(b), ACT.Copy).then_inc(sem("ev_qT"), 1)

            def ev_probs_T(m):
                act.wait_ge(sem("ev_pT_ps"), m + 1)
                if m >= 2:
                    act.wait_ge(sem("ev_pv"), m - 1)
                nc.scalar.activation(flat(pT[:, 1]), pb(5), ACT.Copy).then_inc(sem("ev_pT_act"), 1)

            for n in range(NT * NQ):
                act.wait_ge(sem("ev_max"), n + 1)
                if n >= 2:
                    act.wait_ge(sem("ev_pT_ps"), n - 1)
                nc.scalar.activation(pexp[:, n % 2, :], pb(n % 3), ACT.Exp, bias=sm[:, 64 + n:65 + n],
                                     accum_out=sm[:, 96 + n:97 + n]).then_inc(sem("ev_p"), 1)
                if n % 2 == 0 and n >= 2:
                    ev_probs_T(n - 1)
                if n == LN_AT:
                    act.wait_ge(sem("cv_centered"), 1)
                    nc.scalar.activation(flat(csq), flat(cacc), ACT.Square).then_inc(sem("cv_sq"), 1)
                if n == LN_AT + 1:
                    act.wait_ge(sem("inverses"), 2)
                    nc.scalar.activation(lnrow[:, :], lnrow[:, :], ACT.Sqrt).then_inc(sem("roots"), 1)
            ev_probs_T(NT * NQ - 1)
            act.wait_ge(sem("cv_norm"), 1)
            for c in range(CT):
                nc.scalar.activation(cacc[:, c, :], cacc[:, c, :], ACT.Silu, scale=cw[:, c, 32:33],
                                     bias=cw[:, c, 33:34]).then_inc(sem("cv_out"), 1)
            act.wait_ge(sem("ev_aT_ps"), 2)
            nc.scalar.activation(flat(aT[:, 2:4, :]), pb(5), ACT.Copy).then_inc(sem("ev_aT"), 1)

            def route(l):
                name = f"moe{l}"
                act.wait_ge(sem("h_ready"), 4 * (l + 1))
                squares(name, h, xT_rows)
                transposed(name, xT)
                act.wait_ge(sem("mo_max"), l + 1)
                for t in range(NT):
                    nc.scalar.activation(aff[:, t, :], ps[:, 0, E * t:E * t + E], ACT.Exp, bias=sm[:, 130 + t:131 + t],
                                         accum_out=sm[:, 132 + t:133 + t]).then_inc(sem("mo_exp"), 1)

            def experts(loop):
                l, g0, g1, base = loop
                scale, shift = affine(f"moe{l}")
                with act.Fori(g0, g1) as g:
                    n = g + GROUPS * l
                    act.wait_ge(sem("mo_bc"), n + 1)
                    nc.scalar.activation(aff_bc, ps[:, 4, N:2 * N], ACT.Copy).then_inc(sem("mo_affbc"), 1)
                    act.wait_ge(sem("mo_gather"), 2 * n + 2)
                    for k in range(4, KD):
                        last = nc.scalar.activation(xsT[:, k, :], ps[:, 7, P * (k - 4):P * (k - 3)], ACT.Identity,
                                                    scale=scale[:, k:k + 1], bias=shift[:, k:k + 1])
                    last.then_inc(sem("mo_xsT_act"), 1)
                    act.wait_ge(sem("chunks_used"), PER_GROUP * g + (base + KD))
                    act.wait_ge(sem("mo_hT_ps"), 2 * n + 1)
                    nc.scalar.activation(hid, ps[:, 0:2, :].rearrange("p b f -> p (b f)"), ACT.Silu)\
                        .then_inc(sem("mo_silu"), 1)
                    act.wait_ge(sem("mo_hT_ps"), 2 * n + 3)
                    if g0:
                        act.wait_ge(sem("mem_out"), 32)
                    nc.scalar.activation(flat(hT[:, 4:8, :]), pb(7), ACT.Copy).then_inc(sem("mo_hT_act"), 1)

            route(0)
            experts(LOOPS[0])
            act.wait_ge(sem("mem_in"), 32)
            act.wait_ge(sem("mo_h"), 4 * 2 + 1)
            squares("mem", mem_rows, xk)
            transposed("mem", memT)
            for j in range(4):
                whole(act, "wkv", j)
                for t in range(NT):
                    src, half = pb((2 * j + t + 4) % 8), slice(512 * (j % 2), 512 * (j % 2) + 512)
                    nc.scalar.activation((xk, memv)[j // 2][:, t, half], src, ACT.Copy).then_inc(sem("xkv"), 1)
                    if j < 2:
                        for w in range(2):
                            u, done = XH * t + 2 * j + w, 4 * j + 2 * t + w
                            if done:
                                act.wait_ge(sem("xk_ss"), done)
                            nc.scalar.activation(lnrow[:, :], src[:, XD * w:XD * (w + 1)], ACT.Square,
                                                 accum_out=sm[:, u:u + 1]).then_inc(sem("xk_ss"), 1)
                if j == 2:
                    act.wait_ge(sem("inverses"), 3)
                    nc.scalar.activation(sm[:, 32:40], sm[:, 32:40], ACT.Sqrt).then_inc(sem("roots"), 1)
            for b in (1, 3):
                act.wait_ge(sem("cols_ps"), b + 1)
                nc.scalar.activation(flat(memkT[:, 2 * b:2 * b + 2, :]), pb(4 + b), ACT.Copy).then_inc(sem("cols"), 1)
            experts(LOOPS[1])

            act.wait_ge(sem("mo_h"), 4 * GROUPS + 1)
            squares("mix1", h, xT_rows)
            transposed("mix1", xT)
            for j in range(4):
                whole(act, "sc_in", j)
                dst = (bS, cS)[j // 2]
                for b in range(2):
                    c = 4 * (j % 2) + 2 * b
                    last = nc.scalar.activation(flat(dst[:, c:c + 2, :]), pb(2 * j + b), ACT.Copy)
                last.then_inc(sem("sc_bc"), 1)

            route(1)
            experts(LOOPS[2])

            act.wait_ge(sem("mo_h"), 8 * GROUPS + 1)
            squares("final", h, xT_rows)
            act.wait_ge(sem("h_final"), 2)
            squares("mix2", h, xT_rows)
            transposed("mix2", xT)
            whole(act, "w_small")
            nc.scalar.activation(glrT[0:16, :], ps[0:16, 0, N:2 * N], ACT.Copy).then_inc(sem("glr"), 1)
            act.wait_ge(sem("gate_abs"), 1)
            link(nc.scalar.activation(lf2[0:FOXH, :], lf2[0:FOXH, :], ACT.Exp, scale=-1.0))
            nc.scalar.activation(lf2[0:FOXH, :], lf2[0:FOXH, :], ACT.Ln, bias=1.0).then_inc(sem("gate_ln"), 1)
            whole(act, "w_gqk")
            for j, dst in enumerate((gqT, gkT)):
                nc.scalar.activation(flat(dst), pb(1 + j), ACT.Copy).then_inc(sem("gqk"), 1)
            act.wait_ge(sem("gate_abs"), 2)
            link(nc.scalar.activation(ex[:, 0], ex[:, 0], ACT.Exp, scale=-1.0))
            nc.scalar.activation(ex[:, 0], ex[:, 0], ACT.Ln, bias=1.0).then_inc(sem("gate_ln"), 1)
            for w, name in enumerate(("w_fq", "w_fk")):
                whole(act, name)
                for t in range(NT):
                    nc.scalar.activation(fqk[:, t, 8 * w:8 * w + 8, :], pb(4 + 2 * w + t).rearrange("p (h e) -> p h e", e=HD),
                                         ACT.Copy).then_inc(sem("fqk"), 1)
            act.wait_ge(sem("gl_cum"), 1)
            nc.scalar.activation(ex[:, 0], bcum, ACT.Exp)
            nc.scalar.activation(ex[:, 1], bcum, ACT.Exp, scale=-1.0)
            nc.scalar.activation(sm[:, 200:208].rearrange("p (r c) -> p r c", r=2),
                                 bcum.rearrange("p r (c j) -> p r c j", j=GCH)[:, :, :, GCH - 1], ACT.Exp)\
                .then_inc(sem("gl_exp"), 1)
            act.wait_ge(sem("gl_dec"), 1)
            for r in range(2):
                for c in range(4):
                    s = slice(GCH * c, GCH * (c + 1))
                    last = nc.scalar.activation(ex[:, 0, r, s], bcum[:, r, s], ACT.Exp, scale=-1.0,
                                                bias=bcum[:, r, GCH * (c + 1) - 1:GCH * (c + 1)])
            last.then_inc(sem("gl_exp"), 1)
            for name, dst, bank in (("w_fv", fv, 0), ("w_gv", gv, 2)):
                whole(act, name)
                for t in range(NT):
                    nc.scalar.activation(dst[:, t, :], pb(bank + t), ACT.Copy).then_inc(sem("values"), 1)
            act.wait_ge(sem("inverses"), 4)
            nc.scalar.activation(sm[:, 32:64], sm[:, 32:64], ACT.Sqrt).then_inc(sem("roots"), 1)
            whole(act, "w_gr")
            for t in range(NT):
                nc.scalar.activation(gr[:, t, :], pb(6 + t), ACT.Silu).then_inc(sem("gr"), 1)
            for w in range(2):
                act.wait_ge(sem("cols_ps"), 4 + 2 * w + 2)
                nc.scalar.activation(flat(fT[:, w, 2:4, :]), pb(1 + 2 * w), ACT.Copy).then_inc(sem("cols"), 1)
            act.wait_ge(sem("inverses"), 5)
            nc.scalar.activation(sm[:, 160:168], sm[:, 160:168], ACT.Sqrt).then_inc(sem("roots"), 1)

            def fox_probs_T(m):
                mk = P * (m // FOXH + 1)
                act.wait_ge(sem("fx_pT_ps"), m + 1)
                if m >= 2:
                    act.wait_ge(sem("fx_pv"), m - 1)
                nc.scalar.activation(fpT[:, 1, 0:mk], ps[:, FTB[1], 0:mk], ACT.Copy).then_inc(sem("fx_pT_act"), 1)

            for n in range(NT * FOXH):
                nk = P * (n // FOXH + 1)
                act.wait_ge(sem("fx_max"), n + 1)
                nc.scalar.activation(fp[:, n % 2, 0:nk], fp[:, n % 2, 0:nk], ACT.Exp, bias=sm[:, 64 + n:65 + n],
                                     accum_out=sm[:, 96 + n:97 + n]).then_inc(sem("fx_p"), 1)
                if n % 2 == 0 and n >= 2:
                    fox_probs_T(n - 1)
            fox_probs_T(NT * FOXH - 1)
            for b in (1, 3):
                act.wait_ge(sem("cols_ps"), 8 + b + 1)
                nc.scalar.activation(flat(xT[:, 2 * b:2 * b + 2, :]), pb(b), ACT.Copy).then_inc(sem("cols"), 1)

            act.wait_ge(sem("h_ready"), 12)
            squares("xattn", h, xT_rows)
            transposed("xattn", xT)
            for j in range(2):
                whole(act, "wq", j)
                for t in range(NT):
                    nc.scalar.activation(xq[:, t, 512 * j:512 * j + 512], pb(2 * j + t), ACT.Copy).then_inc(sem("xq"), 1)
            act.wait_ge(sem("inverses"), 6)
            nc.scalar.activation(sm[:, 48:56], sm[:, 48:56], ACT.Sqrt).then_inc(sem("roots"), 1)
            for b in (1, 3):
                act.wait_ge(sem("cols_ps"), 12 + b + 1)
                nc.scalar.activation(flat(xqT[:, 2 * b:2 * b + 2, :]), pb(4 + b), ACT.Copy).then_inc(sem("cols"), 1)
            for n in range(NT * XH):
                act.wait_ge(sem("xa_max"), n + 1)
                if n >= 2:
                    act.wait_ge(sem("xa_pT_ps"), n - 1)
                nc.scalar.activation(xp[:, n % 2, :], ps[:, n % 2, 0:N], ACT.Exp, bias=sm[:, 64 + n:65 + n],
                                     accum_out=sm[:, 96 + n:97 + n]).then_inc(sem("xa_p"), 1)
            for b in (1, 3):
                act.wait_ge(sem("cols_ps"), 16 + b + 1)
                nc.scalar.activation(flat(xT[:, 2 * b:2 * b + 2, :]), pb(b), ACT.Copy).then_inc(sem("cols"), 1)

            def w_high(kind, j, halves=(0, 1)):
                for half, (n, i, w, lo, hi) in enumerate(mlp_halves(kind, j)):
                    if half in halves:
                        arrived(act, i)
                        if n >= 3:
                            act.wait_ge(sem("w_halves_used"), n - 2)
                        nc.scalar.activation(hi, w, ACT.Copy).then_inc(sem("w_high"), 1)

            act.wait_ge(sem("xa_pv"), NT * XH)
            w_high("up", 0)
            act.wait_ge(sem("h_ready"), 16)
            squares("mlp", h, xT_rows)
            transposed("mlp", xT)
            act.wait_ge(sem("xT_ready"), 4 * TRANSPOSED.index("mlp") + 4)
            nc.scalar.activation(xT_hi, xT, ACT.Copy).then_inc(sem("mlp_high"), 1)
            w_high("up", 1)
            for j in range(8):
                act.wait_ge(sem("w_halves_used"), 2 * MLP.index(("up", j)) + 2)
                if j >= 2:
                    act.wait_ge(sem("w_halves_used"), 2 * MLP.index(("down", j - 2)) + 2)
                for b in range(2):
                    last = nc.scalar.activation(flat(uT[:, j % 2, 2 * b:2 * b + 2, :]), pb(4 + 2 * (j % 2) + b), ACT.Relu)
                last.then_inc(sem("mlp_relu"), 1)
                w_high("down", j, (0,))
                act.wait_ge(sem("mlp_u"), j + 1)
                nc.scalar.activation(uT_hi[:, j % 2], uT[:, j % 2], ACT.Copy).then_inc(sem("mlp_high"), 1)
                w_high("down", j, (1,))
                if j + 2 < 8:
                    w_high("up", j + 2)

        @block.gpsimd
        def _(pool):
            link = Steps(pool, "pool_steps")
            nc.gpsimd.memset(sil[:, :, :], 0.0).then_inc(sem("cleared"), 1)
            nc.gpsimd.memset(ada_b, 0.0).then_inc(sem("cleared"), 1)
            link(nc.gpsimd.memset(mhalf[:, :], -0.5))
            nc.gpsimd.memset(ones[:, :], 1.0).then_inc(sem("cleared"), 1)
            def store_gate(g):
                pool.wait_ge(sem("ada_rows"), g + 1)
                l, s = g // 3, g % 3 - 1
                for j in range(2):
                    r = 32 * (2 * s + j)
                    pool.dma_start(gate_dram[l, s:s + 1, 512 * j:512 * (j + 1)], flat(mrow[r:r + 1, g % 3]))\
                        .then_inc(sem(f"gate{g}_out"), 16)

            def load_gate(l, s):
                pool.wait_ge(sem(f"gate{3 * l + s + 1}_out"), 2 * 16)
                pool.dma_start(gate_bc[:, 0:D], gate_dram[l, s].partition_broadcast(P)).then_inc(sem("gate_in"), 16)

            def rms(name):
                u = NORMS.index(name)
                pool.wait_ge(sem("norm_ss"), 2 * u + 2)
                link(nc.gpsimd.tensor_scalar(ms[:, u, :], ss[:, u, :], 1.0 / D, EPS, ALU.mult, ALU.add))
                nc.gpsimd.tensor_tensor(rstd[:, u, :], ms[:, u, :], mhalf[:, :], ALU.pow).then_inc(sem("norm_rstd"), 1)

            rms("x")
            rms("ctx")
            store_gate(1)
            load_gate(0, 0)
            for g in (2, 4, 5):
                store_gate(g)
            rms("moe0")
            pool.wait_ge(sem("gate_used"), 4)
            for g in (4, 5):
                pool.wait_ge(sem(f"gate{g}_out"), 2 * 16)
            load_gate(0, 1)
            pool.dma_start(xkg, a["xattn_k_norm_g_2"].partition_broadcast(P)).then_inc(sem("mem_in"), 16)
            pool.wait_ge(sem("mo_logits"), 1)
            pool.dma_start(mem_rows, a["mem_2"][0].rearrange("(t p) d -> p t d", p=P)).then_inc(sem("mem_in"), 16)
            rms("mem")
            pool.wait_ge(sem("xkv"), 8)
            pool.dma_start(memv_dram.rearrange("p (t d) -> p t d", t=NT), memv).then_inc(sem("mem_out"), 16)
            pool.wait_ge(sem("cols"), 4)
            pool.dma_start(memk_dram.rearrange("p (k n) -> p k n", k=KD), memkT).then_inc(sem("mem_out"), 16)
            rms("mix1")
            load_gate(1, 0)
            rms("moe1")
            pool.wait_ge(sem("gate_used"), 8)
            load_gate(1, 1)
            pool.wait_ge(sem("mo_lists"), 2)
            pool.dma_start(final_bc, a["final_g"].partition_broadcast(P)).then_inc(sem("final_in"), 16)
            pool.wait_ge(sem("mo_ym"), 4 * GROUPS)
            for n, o, w in (("fox_q_norm_g_2", 0, 64), ("fox_k_norm_g_2", 64, 64), ("gla_out_norm_g_2", 128, 512),
                            ("xattn_q_norm_g_2", 640, 256)):
                pool.dma_start(gate_bc[:, o:o + w], a[n].partition_broadcast(P)).then_inc(sem("gains2_in"), 16)
            pool.dma_start(sm[0:FOXH, 140:141], a["fox_b_f_2"].unsqueeze(1)).then_inc(sem("gate2_in"), 16)
            for r in range(2):
                pool.dma_start(sm[:, 141 + r:142 + r], a["gla_b_gate_2"][P * r:P * (r + 1)].unsqueeze(1))\
                    .then_inc(sem("gate2_in"), 16)
            rms("final")
            pool.dma_start(gate2, a["gla_w_gate2_2"]).then_inc(sem("gate2_in"), 16)
            rms("mix2")
            pool.wait_ge(sem("mem_out"), 32)
            pool.wait_ge(sem("cols"), 12)
            pool.dma_start(xkT, memk_dram.rearrange("p (k n) -> p k n", k=KD)).then_inc(sem("memkv_in"), 16)
            pool.dma_start(xv, memv_dram.rearrange("p (t d) -> p t d", t=NT)).then_inc(sem("memkv_in"), 16)
            for n in ("xattn", "mlp"):
                rms(n)

        @block.vector
        def _(dve):
            link = Steps(dve, "dve_steps")

            def normed(name, src, dst):
                u = NORMS.index(name)
                dve.wait_ge(sem("norm_rstd"), u + 1)
                for t in range(NT):
                    nc.vector.tensor_scalar(dst[:, t, :], src[:, t, :], rstd[:, u, t:t + 1], None, ALU.mult)\
                        .then_inc(sem("norm_rows"), 1)

            def transposed(name, dst):
                v, bank, (scale, shift) = TRANSPOSED.index(name), NORM_BANKS[name], affine(name)
                if name in MODS:
                    dve.wait_ge(sem("mod_cols"), MODS[name])
                for b in (0, 2):
                    dve.wait_ge(sem("norm_T"), 4 * v + b + 1)
                    for k in (2 * b, 2 * b + 1):
                        src = ps[:, bank[b], 256 * (k % 2):256 * (k % 2) + 256]
                        if shift is None:
                            last = nc.vector.tensor_scalar(dst[:, k, :], src, scale[:, k:k + 1], None, ALU.mult)
                        else:
                            last = nc.vector.tensor_scalar(dst[:, k, :], src, scale[:, k:k + 1], shift[:, k:k + 1],
                                                           ALU.mult, ALU.add)
                    last.then_inc(sem("xT_ready"), 1)

            def ada_rows(g, bank):
                whole(dve, ADA[g], 3)
                if g == 3:
                    dve.wait_ge(sem("mod_T"), 1)
                if g > 3:
                    dve.wait_ge(sem(f"gate{g - 3}_out"), 2 * 16)
                nc.vector.tensor_copy(flat(mrow[:, g % 3]), pb(bank)).then_inc(sem("ada_rows"), 1)

            def mod_cols(g, bank):
                dve.wait_ge(sem("mod_T"), g + 1)
                v = pb(bank).rearrange("p (b s j c) -> p s j b c", b=4, s=2, c=32)

                def k_order(x):
                    return x.rearrange("p (j b) -> p j b", b=4)

                def shift(name, s, cond=0):
                    return nc.vector.tensor_copy(k_order(mcol[:, SHIFT[name], :]), v[:, s, :, :, cond])

                def scale(name, s, gain, cond=0):
                    return nc.vector.scalar_tensor_tensor(k_order(acol[:, SCALE[name], :]), v[:, s, :, :, cond], 1.0,
                                                          k_order(gcol[:, gain, :]), ALU.add, ALU.mult)
                if g == 0:
                    shift("ctx", 0, 1)
                    scale("ctx", 1, 0, 1)
                if g % 3 == 0:
                    shift(("x", "mix1")[g // 3], 0)
                    last = scale(("x", "mix1")[g // 3], 1, g // 3)
                elif g % 3 == 1:
                    last = shift(("moe0", "moe1")[g // 3], 1)
                else:
                    last = scale(("moe0", "moe1")[g // 3], 0, 2 + g // 3)
                last.then_inc(sem("mod_cols"), 1)

            def add_gated(n, name, banks):
                for j in range(2):
                    whole(dve, name, j)
                    s = slice(512 * j, 512 * j + 512)
                    for t in range(NT):
                        i = 2 * j + t
                        nc.vector.tensor_tensor(rows[:, t, s], pb(banks[i]), gate_bc[:, s], ALU.mult)\
                            .then_inc(sem("gate_used"), 1)
                    for t in range(NT):
                        dve.wait_ge(sem("gate_used"), 4 * n + 2 * j + t + 1)
                        nc.vector.tensor_tensor(h[:, t, s], h[:, t, s], rows[:, t, s], ALU.add).then_inc(sem("h_ready"), 1)

            def add_plain(name, banks, first=0):
                for j in range(2):
                    whole(dve, name, first + j)
                    for t in range(NT):
                        s = slice(512 * j, 512 * j + 512)
                        nc.vector.tensor_tensor(h[:, t, s], h[:, t, s], pb(banks[2 * j + t]), ALU.add)\
                            .then_inc(sem("h_ready"), 1)

            dve.wait_ge(sem("gains_ps"), 1)
            nc.vector.tensor_copy(flat(gcol[:, :, :]), ps[:, 1, 0:GAINS]).then_inc(sem("gain_cols"), 1)
            normed("x", h, rows)
            normed("ctx", ctx_rows, ctx_rows)
            ada_rows(0, 0)
            dve.wait_ge(sem("gain_cols"), 1)
            mod_cols(0, 0)
            transposed("x", xT)
            transposed("ctx", cT)
            dve.wait_ge(sem("cw_ps"), 1)
            nc.vector.tensor_copy(flat(cw), ps[:, 4, 0:CT * 34]).then_inc(sem("cw"), 1)
            dve.wait_ge(sem("params_in"), PARAMS * 16)
            link.mark(nc.vector.tensor_scalar(qkg[:, 0, :], qkg[:, 0, :], float(HD) ** -0.5, None, ALU.mult))
            edge = CONVK // 2
            link.mark(nc.vector.memset(gpad[:, :, 0:edge], 0.0))
            link(nc.vector.memset(gpad[:, :, edge + N:PADW], 0.0))
            dve.wait_ge(sem("ev_rows"), 10)
            link(nc.vector.tensor_tensor(sq, qk, qk, ALU.mult))
            link(nc.vector.tensor_reduce(sm[:, 0:24].rearrange("p (t h) -> p t h", t=NT), sq, AX.X, ALU.add))
            link(nc.vector.tensor_scalar(sm[:, 0:24], sm[:, 0:24], 1.0 / HD, EPS, ALU.mult, ALU.add))
            nc.vector.reciprocal(sm[:, 24:48], sm[:, 0:24]).then_inc(sem("inverses"), 1)
            dve.wait_ge(sem("roots"), 1)
            hr = sm[:, 24:48].rearrange("p (t h) -> p t h", t=NT).unsqueeze(3).broadcast_to([P, NT, 12, HD])
            link(nc.vector.tensor_tensor(qk, qk, hr, ALU.mult))
            for t in range(NT):
                link.mark(nc.vector.tensor_tensor(qk[:, t, 0:8, :], qk[:, t, 0:8, :],
                                                  qkg[:, 0:1, :].broadcast_to([P, 8, HD]), ALU.mult))
                link.mark(nc.vector.tensor_tensor(qk[:, t, 8:12, :], qk[:, t, 8:12, :],
                                                  qkg[:, 1:2, :].broadcast_to([P, 4, HD]), ALU.mult))
            link.wait()
            for t in range(NT):
                cos = cst[:, C_COS + 32 * t:C_COS + 32 * t + 32].unsqueeze(1).broadcast_to([P, 10, 32])
                sin = cst[:, C_SIN + 32 * t:C_SIN + 32 * t + 32].unsqueeze(1).broadcast_to([P, 10, 32])
                x1, x2 = qk[:, t, 0:10, 0:32], qk[:, t, 0:10, 32:64]
                link.mark(nc.vector.tensor_tensor(ra[:, t], x1, cos, ALU.mult))
                link.mark(nc.vector.tensor_tensor(rb[:, t], x2, sin, ALU.mult))
                link.mark(nc.vector.tensor_tensor(rc[:, t], x2, cos, ALU.mult))
                link(nc.vector.tensor_tensor(rd[:, t], x1, sin, ALU.mult))
                nc.vector.tensor_tensor(x1, ra[:, t], rb[:, t], ALU.subtract).then_inc(sem("ev_rope"), 1)
                nc.vector.tensor_tensor(x2, rc[:, t], rd[:, t], ALU.add).then_inc(sem("ev_rope"), 1)
            whole(dve, "ev_u")
            for j in range(2):
                dve.wait_ge(sem("cv_gate"), j + 1)
                nc.vector.tensor_tensor(gpad[:, 2 * j:2 * j + 2, edge:edge + N],
                                        pb(4 + j).rearrange("p (c n) -> p c n", c=2), sg[:, 2 * j:2 * j + 2, :], ALU.mult)\
                    .then_inc(sem("gpad"), 1)
            ada_rows(1, 3)
            dve.wait_ge(sem("ev_qkT_ps"), 2)
            nc.vector.tensor_copy(kT, pb(2)).then_inc(sem("ev_kT"), 1)
            mod_cols(1, 3)

            taps_left = [(k, c) for k in range(CONVK) for c in range(CT)]

            def taps(n):
                for _ in range(min(n, len(taps_left))):
                    k, c = taps_left.pop(0)
                    if k:
                        dve.wait_ge(sem("conv"), CT * (k - 1) + c + 1)
                        ins = nc.vector.scalar_tensor_tensor(cacc[:, c, :], gpad[:, c, k:k + N], cw[:, c, k:k + 1],
                                                             cacc[:, c, :], ALU.mult, ALU.add)
                    else:
                        ins = nc.vector.tensor_scalar(cacc[:, c, :], gpad[:, c, 0:N], cw[:, c, 0:1], cw[:, c, 31:32],
                                                      ALU.mult, ALU.add)
                    ins.then_inc(sem("conv"), 1)

            def attn_rows(t):
                dve.wait_ge(sem("ev_pv"), NQ * (t + 1))
                link(nc.vector.reciprocal(sm[:, 112 + 8 * t:120 + 8 * t], sm[:, 96 + 8 * t:104 + 8 * t]))
                for w in range(2):
                    nc.vector.tensor_tensor(attn[:, t, 256 * w:256 * w + 256].rearrange("p (i e) -> p i e", e=HD),
                                            pb(6 + t).rearrange("p (i w e) -> p w i e", w=2, e=HD)[:, w],
                                            sm[:, 112 + 8 * t:120 + 8 * t].rearrange("p (i w) -> p w i", w=2)[:, w]
                                            .unsqueeze(2).broadcast_to([P, 4, HD]), ALU.mult)\
                        .then_inc(sem("ev_attn"), 1)

            mu = lnrow[:, :].unsqueeze(1).broadcast_to([P, CT, N])

            def ln_center():
                dve.wait_ge(sem("cv_sum"), 1)
                link(nc.vector.tensor_scalar(lnrow[:, :], ps[:, 6, 0:N], 1.0 / 512, None, ALU.mult))
                nc.vector.tensor_tensor(cacc, cacc, mu, ALU.subtract).then_inc(sem("cv_centered"), 1)

            def ln_inverse():
                dve.wait_ge(sem("cv_sum"), 2)
                link(nc.vector.tensor_scalar(lnrow[:, :], ps[:, 6, N:2 * N], 1.0 / 512, EPS, ALU.mult, ALU.add))
                nc.vector.reciprocal(lnrow[:, :], lnrow[:, :]).then_inc(sem("inverses"), 1)

            def ln_scale():
                dve.wait_ge(sem("roots"), 2)
                nc.vector.tensor_tensor(cacc, cacc, mu, ALU.mult).then_inc(sem("cv_norm"), 1)

            dve.wait_ge(sem("cw"), 1)
            dve.wait_ge(sem("gpad"), 2)
            for n in range(NT * NQ):
                dve.wait_ge(sem("ev_s"), n + 1)
                nc.vector.tensor_reduce(sm[:, 64 + n:65 + n], pb(n % 3), AX.X, ALU.max, negate=True)\
                    .then_inc(sem("ev_max"), 1)
                if n % 2 == 1:
                    dve.wait_ge(sem("ev_pT_ps"), n)
                    if n >= 3:
                        dve.wait_ge(sem("ev_pv"), n - 2)
                    nc.vector.tensor_copy(flat(pT[:, 0]), pb(4)).then_inc(sem("ev_pT_dve"), 1)
                if n % 4 == 0 and n:
                    ada_rows(1 + n // 4, 3)
                taps(12)
                if n % 4 == 0 and n:
                    mod_cols(1 + n // 4, 3)
                if n == NQ + 1:
                    attn_rows(0)
                if n == LN_AT:
                    ln_center()
                if n == LN_AT + 1:
                    ln_inverse()
                if n == LN_AT + 2:
                    ln_scale()
            ada_rows(5, 3)
            attn_rows(1)
            dve.wait_ge(sem("ev_aT_ps"), 1)
            nc.vector.tensor_copy(flat(aT[:, 0:2, :]), pb(4)).then_inc(sem("ev_aT"), 1)
            mod_cols(5, 3)
            dve.wait_ge(sem("gate_in"), 16)
            add_gated(0, "ev_out", (6, 7, 0, 1))

            def route(l):
                name = f"moe{l}"
                dve.wait_ge(sem("h_ready"), 4 * (l + 1))
                normed(name, h, rows)
                transposed(name, xT)
                dve.wait_ge(sem("mo_logits"), l + 1)
                nc.vector.tensor_reduce(sm[:, 130:132], ps[:, 0, 0:NT * E].rearrange("p (t e) -> p t e", t=NT), AX.X,
                                        ALU.max, negate=True).then_inc(sem("mo_max"), 1)
                dve.wait_ge(sem("mo_exp"), 2 * l + 2)
                link(nc.vector.reciprocal(sm[:, 134:136], sm[:, 132:134]))
                nc.vector.tensor_tensor(aff, aff, sm[:, 134:136].unsqueeze(2).broadcast_to([P, NT, E]), ALU.mult)\
                    .then_inc(sem("mo_aff"), 1)
                dve.wait_ge(sem("mo_affT_ps"), l + 1)
                link.mark(nc.vector.tensor_copy(affT[0:E, :], ps[0:E, 1, 0:N]))
                link(nc.vector.tensor_copy(work[0:E, :], ps[0:E, 1, 0:N]))
                for _ in range(CAP // 8):
                    link(nc.vector.max(sm[0:E, 144:152], work[0:E, :]))
                    link(nc.vector.match_replace(work[0:E, :], sm[0:E, 144:152], work[0:E, :], -1.0))
                link(nc.vector.tensor_scalar(smaskE[0:E, :], work[0:E, :], 0.0, None, ALU.is_lt))
                link(nc.vector.tensor_tensor_scan(rank[0:E, :], ones[0:E, :], smaskE[0:E, :], 0.0, ALU.mult, ALU.add))
                nc.vector.tensor_tensor(rank[0:E, :], rank[0:E, :], smaskE[0:E, :], ALU.mult).then_inc(sem("mo_rank"), 1)
                dve.wait_ge(sem("mo_rank"), l + 1)
                grp = cst[0:E, C_GRP:C_GRP + GROUPS].unsqueeze(2).broadcast_to([E, GROUPS, N])
                for v, src in ((0, rank), (1, affT)):
                    ins = nc.vector.tensor_tensor(RA[0:E, :, v, :], src[0:E, :].unsqueeze(1).broadcast_to([E, GROUPS, N]),
                                                  grp, ALU.mult)
                    if l == v == 0:
                        ins.then_inc(sem("mo_h"), 1)
                dve.wait_ge(sem("mo_rankT_ps"), l + 1)
                dve.wait_ge(sem("gate_in"), 32 * (l + 1))
                link(nc.vector.tensor_copy(flat(rankT), ps[:, 2, 0:NT * E]))
                iota = cst[:, C_IOTA:C_IOTA + CAP].unsqueeze(1).broadcast_to([P, E, CAP])
                for t in range(NT):
                    last = nc.vector.tensor_tensor(onehot[:, t, :].rearrange("p (e c) -> p e c", c=CAP), iota,
                                                   rankT[:, t, :].unsqueeze(2).broadcast_to([P, E, CAP]), ALU.is_equal)
                last.then_inc(sem("mo_lists"), 1)

            def experts(loop):
                l, g0, g1, base = loop
                scale, shift = affine(f"moe{l}")
                with dve.Fori(g0, g1) as g:
                    n = g + GROUPS * l
                    dve.wait_ge(sem("mo_gather"), 2 * n + 1)
                    for k in range(4):
                        last = nc.vector.tensor_scalar(xsT[:, k, :], ps[:, 6, P * k:P * (k + 1)], scale[:, k:k + 1],
                                                       shift[:, k:k + 1], ALU.mult, ALU.add)
                    last.then_inc(sem("mo_xsT_dve"), 1)
                    dve.wait_ge(sem("mo_affbc"), n + 1)
                    dve.wait_ge(sem("mo_comb"), 4 * n + 1)
                    nc.vector.scalar_tensor_tensor(sel_w, ps[:, 4, 0:N], cst[:, C_T:C_T + 1], aff_bc, ALU.is_equal, ALU.mult)\
                        .then_inc(sem("mo_sel"), 1)
                    dve.wait_ge(sem("mo_silu"), n + 1)
                    dve.wait_ge(sem("chunks_used"), PER_GROUP * g + (base + 2 * KD))
                    nc.vector.tensor_tensor(hid, hid, ps[:, 2:4, :].rearrange("p b f -> p (b f)"), ALU.mult)\
                        .then_inc(sem("mo_hid"), 1)
                    dve.wait_ge(sem("mo_hT_ps"), 2 * n + 2)
                    if g0:
                        dve.wait_ge(sem("mem_out"), 32)
                    nc.vector.tensor_copy(flat(hT[:, 0:4, :]), pb(6)).then_inc(sem("mo_hT_dve"), 1)
                    dve.wait_ge(sem("chunks_used"), PER_GROUP * g + (base + 3 * KD))
                    for j in range(2):
                        nc.vector.tensor_tensor(ym[:, 512 * j:512 * j + 512], pb(4 + j), gate_bc[:, 512 * j:512 * j + 512],
                                                ALU.mult).then_inc(sem("mo_ym"), 1)
                    dve.wait_ge(sem("mo_h"), 4 * n + 1)
                    for i in range(4):
                        dve.wait_ge(sem("mo_comb"), 4 * n + i + 2)
                        t, s = i // 2, slice(512 * (i % 2), 512 * (i % 2) + 512)
                        nc.vector.tensor_tensor(h[:, t, s], h[:, t, s], pb((6, 7, 4, 5)[i]), ALU.add).then_inc(sem("mo_h"), 1)
                dve.wait_ge(sem("mo_h"), 4 * (GROUPS * l + g1) + 1)

            route(0)
            experts(LOOPS[0])
            normed("mem", mem_rows, mem_rows)
            transposed("mem", memT)
            dve.wait_ge(sem("xk_ss"), 2 * XH)
            dve.wait_ge(sem("mem_in"), 32)
            link(nc.vector.tensor_scalar(sm[:, 0:8], sm[:, 0:8], 1.0 / XD, EPS, ALU.mult, ALU.add))
            nc.vector.reciprocal(sm[:, 32:40], sm[:, 0:8]).then_inc(sem("inverses"), 1)
            dve.wait_ge(sem("roots"), 3)
            for t in range(NT):
                for hd in range(XH):
                    x = xk[:, t, XD * hd:XD * (hd + 1)]
                    last = nc.vector.scalar_tensor_tensor(x, x, sm[:, 32 + XH * t + hd:33 + XH * t + hd], xkg,
                                                          ALU.mult, ALU.mult)
            last.then_inc(sem("xk_normed"), 1)
            for b in (0, 2):
                dve.wait_ge(sem("cols_ps"), b + 1)
                nc.vector.tensor_copy(flat(memkT[:, 2 * b:2 * b + 2, :]), pb(4 + b)).then_inc(sem("cols"), 1)
            experts(LOOPS[1])

            normed("mix1", h, rows)
            transposed("mix1", xT)
            link.mark(nc.vector.memset(cx[:, :, 0:1], 0.0))
            link.mark(nc.vector.memset(cx[:, :, N + 1:N + 2], 0.0))
            for j in range(2):
                dve.wait_ge(sem("sc_bc"), 3 + j)
                whole(dve, "sc_in", 4 + j)
                for b in range(2):
                    c = 4 * j + 2 * b
                    link.mark(nc.vector.tensor_tensor(cx[:, c:c + 2, 1:N + 1], pb(2 * j + b).rearrange("p (c n) -> p c n", c=2),
                                                      cS[:, c:c + 2, :], ALU.mult))
                link.wait()
                for c in range(4 * j, 4 * j + 4):
                    link.mark(nc.vector.tensor_scalar(yS[:, c, :], cx[:, c, 0:N], cw1[:, c, 0:1], None, ALU.mult))
                for k in range(1, SCK):
                    link.wait()
                    for c in range(4 * j, 4 * j + 4):
                        link.mark(nc.vector.scalar_tensor_tensor(yS[:, c, :], cx[:, c, k:k + N], cw1[:, c, k:k + 1],
                                                                 yS[:, c, :], ALU.mult, ALU.add))
                link.wait()
                s = slice(4 * j, 4 * j + 4)
                nc.vector.tensor_tensor(yS[:, s, :], yS[:, s, :], bS[:, s, :], ALU.mult).then_inc(sem("sc_y"), 1)
            dve.wait_ge(sem("gate_in"), 48)
            add_gated(1, "sc_out", (4, 5, 6, 7))

            route(1)
            experts(LOOPS[2])

            normed("final", h, rows)
            dve.wait_ge(sem("final_in"), 16)
            dve.wait_ge(sem("norm_rows"), 2 * NORMS.index("final") + 2)
            for t in range(NT):
                nc.vector.tensor_tensor(h[:, t, :], rows[:, t, :], final_bc, ALU.mult).then_inc(sem("h_final"), 1)
            dve.wait_ge(sem("h_final"), 2)
            normed("mix2", h, rows)
            transposed("mix2", xT)
            dve.wait_ge(sem("gate2_in"), 4 * 16)
            whole(dve, "w_small")
            dve.wait_ge(sem("glr"), 1)
            lfr, lf2r = lf[0:FOXH, :], lf2[0:FOXH, :]
            link(nc.vector.tensor_scalar(lfr, ps[0:FOXH, 0, 0:N], sm[0:FOXH, 140:141], None, ALU.add))
            nc.vector.scalar_tensor_tensor(lf2r, lfr, -1.0, lfr, ALU.mult, ALU.max).then_inc(sem("gate_abs"), 1)
            dve.wait_ge(sem("gl_ps"), 1)
            for r in range(2):
                link.mark(nc.vector.tensor_scalar(glog[:, r, :], ps[:, 3, N * r:N * (r + 1)], sm[:, 141 + r:142 + r], None,
                                                  ALU.add))
            link.wait()
            nc.vector.scalar_tensor_tensor(flat(ex[:, 0]), flat(glog), -1.0, flat(glog), ALU.mult, ALU.max).then_inc(sem("gate_abs"), 1)
            dve.wait_ge(sem("gate_ln"), 1)
            link(nc.vector.scalar_tensor_tensor(lfr, lfr, 0.0, lf2r, ALU.min, ALU.subtract))
            nc.vector.tensor_tensor_scan(lf2r, ones[0:FOXH, :], lfr, 0.0, ALU.mult, ALU.add).then_inc(sem("lf_cum"), 1)
            dve.wait_ge(sem("gate_ln"), 2)
            link(nc.vector.scalar_tensor_tensor(flat(glog), flat(glog), 0.0, flat(ex[:, 0]), ALU.min, ALU.subtract))
            link(nc.vector.tensor_scalar(glog, glog, 1.0 / GLA_TAU, None, ALU.mult))
            for r in range(2):
                last = nc.vector.tensor_tensor_scan(bcum[:, r, :], scan_mask, glog[:, r, :], 0.0, ALU.mult, ALU.add)
            last.then_inc(sem("gl_cum"), 1)
            dve.wait_ge(sem("gqk"), 2)
            dve.wait_ge(sem("gl_exp"), 1)
            nc.vector.scalar_tensor_tensor(flat(gqT), flat(gqT), float(GDK) ** -0.5, flat(ex[:, 0]), ALU.mult, ALU.mult)
            nc.vector.tensor_tensor(kdec, gkT, ex[:, 1], ALU.mult).then_inc(sem("gl_dec"), 1)
            dve.wait_ge(sem("fqk"), 4)
            link(nc.vector.tensor_tensor(fsq, fqk, fqk, ALU.mult))
            link(nc.vector.tensor_reduce(sm[:, 0:32].rearrange("p (t h) -> p t h", t=NT), fsq, AX.X, ALU.add))
            link(nc.vector.tensor_scalar(sm[:, 0:32], sm[:, 0:32], 1.0 / HD, EPS, ALU.mult, ALU.add))
            nc.vector.reciprocal(sm[:, 32:64], sm[:, 0:32]).then_inc(sem("inverses"), 1)
            dve.wait_ge(sem("gl_exp"), 2)
            dve.wait_ge(sem("gl_dec"), 1)
            nc.vector.tensor_tensor(gkT, gkT, ex[:, 0], ALU.mult).then_inc(sem("gl_klast"), 1)
            dve.wait_ge(sem("gains2_in"), 4 * 16)
            link(nc.vector.tensor_scalar(foxg[:, 0, :], foxg[:, 0, :], float(HD) ** -0.5, None, ALU.mult))
            dve.wait_ge(sem("roots"), 4)
            fr = sm[:, 32:64].rearrange("p (t h) -> p t h", t=NT).unsqueeze(3).broadcast_to([P, NT, 16, HD])
            link(nc.vector.tensor_tensor(fqk, fqk, fr, ALU.mult))
            for t in range(NT):
                for w in range(2):
                    last = nc.vector.tensor_tensor(fqk[:, t, 8 * w:8 * w + 8, :], fqk[:, t, 8 * w:8 * w + 8, :],
                                                   foxg[:, w:w + 1, :].broadcast_to([P, 8, HD]), ALU.mult)
            last.then_inc(sem("fqk_normed"), 1)
            dve.wait_ge(sem("gl_klast"), 1)
            link(nc.vector.memset(AT, 0.0))
            for w in range(2):
                dve.wait_ge(sem("cols_ps"), 4 + 2 * w + 1)
                nc.vector.tensor_copy(flat(fT[:, w, 0:2, :]), pb(2 * w)).then_inc(sem("cols"), 1)
            dve.wait_ge(sem("kl_ps"), 1)
            nc.vector.tensor_copy(klrow.rearrange("p t r e -> p (t r e)"), pb(4)).then_inc(sem("klrow"), 1)
            dve.wait_ge(sem("params_in"), PARAMS * 16)
            for w in range(2):
                dve.wait_ge(sem("A_ps"), w + 1)
                for t in range(NT):
                    last = nc.vector.copy_predicated(AT[:, t].rearrange("p (r w) c -> p w r c", w=2)[:, w],
                                                     glam[:, :].unsqueeze(1).broadcast_to([P, 2, P]),
                                                     pb(5 + w)[:, 256 * t:256 * t + 256].rearrange("p (r c) -> p r c", r=2))
                last.then_inc(sem("AT"), 1)
            dve.wait_ge(sem("dS_ps"), 2)
            decay = sm[:, 200:208].rearrange("p (r c) -> p r c", r=2)
            dS02 = pb(7).rearrange("p (r c v) -> p r c v", r=2, c=2)
            dS1 = pb(4)[:, 0:N].rearrange("p (r v) -> p r v", r=2)
            link(nc.vector.tensor_copy(state[:, :, 0, :], dS02[:, :, 0, :]))
            for r in range(2):
                link(nc.vector.scalar_tensor_tensor(state[:, r, 1, :], state[:, r, 0, :], decay[:, r, 1:2], dS1[:, r, :],
                                                    ALU.mult, ALU.add))
            for r in range(2):
                last = nc.vector.scalar_tensor_tensor(state[:, r, 2, :], state[:, r, 1, :], decay[:, r, 2:3],
                                                      dS02[:, r, 1, :], ALU.mult, ALU.add)
            last.then_inc(sem("states"), 1)
            dve.wait_ge(sem("ccol_ps"), 1)
            ccol = sm[:, 184:200]
            nc.vector.tensor_copy(ccol, ps[:, 0, 0:16]).then_inc(sem("ccol"), 1)
            for j, b in enumerate((1, 2, 3, 5)):
                dve.wait_ge(sem("nb_ps"), j + 1)
                nc.vector.tensor_scalar(flat(NB[:, 2 * j:2 * j + 2, :]), pb(b), -1.0, None, ALU.mult).then_inc(sem("nb"), 1)
            for t in range(NT):
                dve.wait_ge(sem("go_ps"), t + 1)
                for w in range(2):
                    link.mark(nc.vector.tensor_copy(go[:, t, :].rearrange("p (r w v) -> p w r v", w=2, v=GDV)[:, w],
                                                    pb(GO[t][w])[:, 0:N].rearrange("p (r v) -> p r v", v=GDV)))
            link.wait()
            nc.vector.tensor_copy(sm[:, 208:209], go[:, 1, 0:1]).then_inc(sem("go_sb"), 1)
            gh = go.rearrange("p t (h v) -> p t h v", v=GDV)
            link(nc.vector.tensor_tensor(gsq, go, go, ALU.mult))
            link(nc.vector.tensor_reduce(sm[:, 152:160].rearrange("p (t h) -> p t h", t=NT),
                                         gsq.rearrange("p t (h v) -> p t h v", v=GDV), AX.X, ALU.add))
            link(nc.vector.tensor_scalar(sm[:, 152:160], sm[:, 152:160], 1.0 / GDV, EPS, ALU.mult, ALU.add))
            nc.vector.reciprocal(sm[:, 160:168], sm[:, 152:160]).then_inc(sem("inverses"), 1)
            dve.wait_ge(sem("roots"), 5)
            link(nc.vector.tensor_tensor(gh, gh, sm[:, 160:168].rearrange("p (t h) -> p t h", t=NT).unsqueeze(3)
                                         .broadcast_to([P, NT, GLAH, GDV]), ALU.mult))
            link(nc.vector.tensor_tensor(go, go, glag.unsqueeze(1).broadcast_to([P, NT, 512]), ALU.mult))
            dve.wait_ge(sem("gr"), 2)
            nc.vector.tensor_tensor(rows[:, :, 512:1024], go, gr, ALU.mult).then_inc(sem("mix_rows"), 1)
            dve.wait_ge(sem("nb"), 4)
            dve.wait_ge(sem("ccol"), 1)
            for n in range(NT * FOXH):
                t, hd, nk = n // FOXH, n % FOXH, P * (n // FOXH + 1)
                x = fp[:, n % 2, 0:nk]
                dve.wait_ge(sem("fx_s"), n + 1)
                if n >= 2:
                    dve.wait_ge(sem("fx_pT_ps"), n - 1)
                link(nc.vector.scalar_tensor_tensor(x, ps[:, FS[n % 4], 0:nk], ccol[:, 8 * t + hd:8 * t + hd + 1],
                                                    NB[:, hd, 0:nk], ALU.add, ALU.add))
                link(nc.vector.tensor_tensor(x[:, nk - P:nk], x[:, nk - P:nk], cst[:, C_FOX:C_FOX + P], ALU.add))
                nc.vector.tensor_reduce(sm[:, 64 + n:65 + n], x, AX.X, ALU.max, negate=True).then_inc(sem("fx_max"), 1)
                if n % 2 == 1:
                    dve.wait_ge(sem("fx_pT_ps"), n)
                    mk = P * ((n - 1) // FOXH + 1)
                    if n >= 3:
                        dve.wait_ge(sem("fx_pv"), n - 2)
                    nc.vector.tensor_copy(fpT[:, 0, 0:mk], ps[:, FTB[0], 0:mk]).then_inc(sem("fx_pT_dve"), 1)
            for t in range(NT):
                dve.wait_ge(sem("fx_pv"), FOXH * (t + 1))
                link(nc.vector.reciprocal(sm[:, 112 + 8 * t:120 + 8 * t], sm[:, 96 + 8 * t:104 + 8 * t]))
                nc.vector.tensor_tensor(rows[:, t, 0:512].rearrange("p (h e) -> p h e", e=HD),
                                        pb(FO[t]).rearrange("p (h e) -> p h e", e=HD),
                                        sm[:, 112 + 8 * t:120 + 8 * t].unsqueeze(2).broadcast_to([P, FOXH, HD]), ALU.mult)\
                    .then_inc(sem("mix_rows"), 1)
            for b in (0, 2):
                dve.wait_ge(sem("cols_ps"), 8 + b + 1)
                nc.vector.tensor_copy(flat(xT[:, 2 * b:2 * b + 2, :]), pb(b)).then_inc(sem("cols"), 1)
            add_plain("w_out", (4, 5, 6, 7))

            def head_norm(x, tmp, c0, c1, nth, gain):
                x4 = x.rearrange("p t (h e) -> p t h e", e=XD)
                t4 = tmp.rearrange("p t (h e) -> p t h e", e=XD)
                link(nc.vector.tensor_tensor(tmp, x, x, ALU.mult))
                link(nc.vector.tensor_reduce(sm[:, c0:c0 + 8].rearrange("p (t h) -> p t h", t=NT), t4, AX.X, ALU.add))
                link(nc.vector.tensor_scalar(sm[:, c0:c0 + 8], sm[:, c0:c0 + 8], 1.0 / XD, EPS, ALU.mult, ALU.add))
                nc.vector.reciprocal(sm[:, c1:c1 + 8], sm[:, c0:c0 + 8]).then_inc(sem("inverses"), 1)
                dve.wait_ge(sem("roots"), nth)
                for t in range(NT):
                    for hd in range(XH):
                        last = nc.vector.scalar_tensor_tensor(x4[:, t, hd, :], x4[:, t, hd, :],
                                                              sm[:, c1 + 4 * t + hd:c1 + 4 * t + hd + 1], gain,
                                                              ALU.mult, ALU.mult)
                return last

            dve.wait_ge(sem("h_ready"), 12)
            normed("xattn", h, rows)
            transposed("xattn", xT)
            link(nc.vector.tensor_scalar(xqg, xqg, float(XD) ** -0.5, None, ALU.mult))
            dve.wait_ge(sem("xq"), 4)
            head_norm(xq, xsq, 16, 48, 6, xqg).then_inc(sem("xq_normed"), 1)
            for b in (0, 2):
                dve.wait_ge(sem("cols_ps"), 12 + b + 1)
                nc.vector.tensor_copy(flat(xqT[:, 2 * b:2 * b + 2, :]), pb(4 + b)).then_inc(sem("cols"), 1)
            for n in range(NT * XH + 1):
                if n < NT * XH:
                    dve.wait_ge(sem("xa_s"), n + 1)
                    nc.vector.tensor_reduce(sm[:, 64 + n:65 + n], ps[:, n % 2, 0:N], AX.X, ALU.max, negate=True)\
                        .then_inc(sem("xa_max"), 1)
                if n >= 1:
                    m = n - 1
                    dve.wait_ge(sem("xa_pT_ps"), m + 1)
                    if m >= 2:
                        dve.wait_ge(sem("xa_pv"), m - 1)
                    nc.vector.tensor_copy(xpT[:, m % 2, :], ps[:, 2 + m % 2, 0:N]).then_inc(sem("xa_pT"), 1)
            dve.wait_ge(sem("xa_pv"), NT * XH)
            link(nc.vector.reciprocal(sm[:, 112:120], sm[:, 96:104]))
            for t in range(NT):
                for b in range(2):
                    nc.vector.tensor_tensor(rows[:, t, 512 * b:512 * b + 512].rearrange("p (h e) -> p h e", e=XD),
                                            pb(4 + 2 * t + b).rearrange("p (h e) -> p h e", e=XD),
                                            sm[:, 112 + 4 * t + 2 * b:114 + 4 * t + 2 * b].unsqueeze(2)
                                            .broadcast_to([P, 2, XD]), ALU.mult).then_inc(sem("xo"), 1)
            for b in (0, 2):
                dve.wait_ge(sem("cols_ps"), 16 + b + 1)
                nc.vector.tensor_copy(flat(xT[:, 2 * b:2 * b + 2, :]), pb(b)).then_inc(sem("cols"), 1)
            def w_low(kind, j):
                for n, i, w, lo, hi in mlp_halves(kind, j):
                    dve.wait_ge(sem("w_high"), n + 1)
                    nc.vector.tensor_tensor(lo, w, hi.bitcast(F32), ALU.subtract).then_inc(sem("w_split"), 1)

            w_low("up", 0)
            add_plain("wo", (4, 5, 6, 7))

            dve.wait_ge(sem("h_ready"), 16)
            normed("mlp", h, rows)
            transposed("mlp", xT)
            dve.wait_ge(sem("mlp_high"), 1)
            nc.vector.tensor_tensor(xT_r, xT, xT_hi.bitcast(F32), ALU.subtract).then_inc(sem("mlp_split"), 1)
            w_low("up", 1)
            for j in range(8):
                u = uT[:, j % 2]
                dve.wait_ge(sem("mlp_relu"), j + 1)
                nc.vector.tensor_tensor(u, u, u, ALU.mult).then_inc(sem("mlp_u"), 1)
                dve.wait_ge(sem("mlp_high"), j + 2)
                nc.vector.tensor_tensor(uT_lo[:, j % 2], u, uT_hi[:, j % 2].bitcast(F32), ALU.subtract)\
                    .then_inc(sem("mlp_split"), 1)
                w_low("down", j)
                if j + 2 < 8:
                    w_low("up", j + 2)
            dve.wait_ge(sem("w_halves_used"), 2 * len(MLP))
            for t in range(NT):
                for j in range(2):
                    s = slice(512 * j, 512 * j + 512)
                    nc.vector.tensor_tensor(h[:, t, s], h[:, t, s], pb(2 * t + j), ALU.add).then_inc(sem("h_ready"), 1)

        @block.tensor
        def _(pe):
            mm = nc.tensor.matmul

            def used(ins):
                ins.then_inc(sem("chunks_used"), 1)

            def ada(g, c, bank):
                i = FIRST[ADA[g]] + c
                arrived(pe, i)
                for k in (0, 1, 2)[:3 if c == 3 else 2]:
                    for j in range(4):
                        r = 4 * g + j
                        lhs, rhs = (sil[:, 2 * c + k, :], slot2(i)[:, k, 512 * j:512 * (j + 1)]) if k < 2 else \
                            (ident[:, r:r + 1].broadcast_to([P, 32]), ada_b)
                        last = mm(ps[32 * j:32 * j + 32, bank, :], lhs, rhs, start=(c == k == 0), stop=(k == 2))
                used(last)

            def ada_columns(g, bank):
                pe.wait_ge(sem("ada_rows"), g + 1)
                for b in range(4):
                    last = nc.tensor.transpose(ps[:, bank, P * b:P * (b + 1)], mrow[:, g % 3, b, :], ident)
                last.then_inc(sem("mod_T"), 1)

            def transposes(name, src):
                u, v, bank = NORMS.index(name), TRANSPOSED.index(name), NORM_BANKS[name]
                pe.wait_ge(sem("norm_rows"), 2 * u + 2)
                for k in range(KD):
                    for t in range(NT):
                        last = nc.tensor.transpose(ps[:, bank[k // 2], 256 * (k % 2) + P * t:256 * (k % 2) + P * (t + 1)],
                                                   src[:, t, P * k:P * (k + 1)], ident)
                    if k % 2:
                        last.then_inc(sem("norm_T"), 1)

            def normed_columns(name):
                pe.wait_ge(sem("xT_ready"), 4 * TRANSPOSED.index(name) + 4)

            def to_rows(i, lhs, banks, width=512, col=0):
                for t in range(NT):
                    for k in range(KD):
                        last = mm(ps[:, banks[t], col:col + width], lhs[:, k, P * t:P * (t + 1)], slot8(i)[:, k, 0:width],
                                  start=(k == 0), stop=(k == KD - 1))
                return last

            def to_columns(i, rhs, banks):
                for c in range(4):
                    for k in range(KD):
                        last = mm(ps[:, banks[c // 2], N * (c % 2):N * (c % 2 + 1)], slot8(i)[:, k, P * c:P * (c + 1)],
                                  rhs[:, k, :], start=(k == 0), stop=(k == KD - 1))
                return last

            def row_transposes(src, banks):
                for k in range(KD):
                    for t in range(NT):
                        last = nc.tensor.transpose(ps[:, banks[k // 2], N * (k % 2) + P * t:N * (k % 2) + P * (t + 1)],
                                                   src[:, t, P * k:P * (k + 1)], ident)
                    if k % 2:
                        last.then_inc(sem("cols_ps"), 1)

            pe.wait_ge(sem("c_in"), 3 * 16)
            nc.tensor.transpose(ps[:, 2, 0:2 * KD], crow[0:2 * KD, :], ident[0:2 * KD, 0:2 * KD]).then_inc(sem("c_ps"), 1)
            pe.wait_ge(sem("gains_in"), 7 * 16)
            nc.tensor.transpose(ps[:, 1, 0:GAINS], grow[0:GAINS, :], ident[0:GAINS, 0:GAINS]).then_inc(sem("gains_ps"), 1)
            pe.wait_ge(sem("sil"), 1)
            pe.wait_ge(sem("ada_b_in"), 16)
            for q in range(4):
                ada(0, q, 0)
            transposes("x", rows)
            ada_columns(0, 0)
            pe.wait_ge(sem("gain_cols"), 1)
            pe.wait_ge(sem("mod_cols"), 1)
            transposes("ctx", ctx_rows)
            normed_columns("x")
            normed_columns("ctx")
            pe.wait_ge(sem("params_in"), PARAMS * 16)
            for c in range(CT):
                last = nc.tensor.transpose(ps[:, 4, 34 * c:34 * c + 34], cwrow[0:34, P * c:P * (c + 1)], ident[0:34, 0:34])
            last.then_inc(sem("cw_ps"), 1)
            i = FIRST["ev_q"]
            arrived(pe, i)
            used(to_rows(i, xT, (0, 1)))
            i = FIRST["ev_kv"]
            arrived(pe, i)
            for bank, lhs in ((2, xT), (3, cT)):
                for t in range(NT):
                    for k in range(KD):
                        last = mm(ps[:, bank, 256 * t:256 * t + 256], lhs[:, k, P * t:P * (t + 1)], slot8(i)[:, k, 0:256],
                                  start=(k == 0), stop=(k == KD - 1))
            used(last)
            pe.wait_ge(sem("cw"), 1)
            for name, banks in (("ev_u", (4, 5)), ("ev_gate", (6, 7))):
                i = FIRST[name]
                arrived(pe, i)
                used(to_columns(i, xT, banks))
            pe.wait_ge(sem("ev_rows"), 10)
            for q in range(4):
                ada(1, q, 3)
            pe.wait_ge(sem("ev_rope"), 4)
            for i in range(4):
                for t in range(NT):
                    last = nc.tensor.transpose(ps[:, i // 2, N * (i % 2) + P * t:N * (i % 2) + P * (t + 1)],
                                               qk[:, t, 2 * i:2 * i + 2, :].rearrange("p h e -> p (h e)"), ident)
            last.then_inc(sem("ev_qkT_ps"), 1)
            for s in range(4):
                last = nc.tensor.transpose(ps[:, 2, P * s:P * (s + 1)],
                                           qk[:, s % 2, 10 - 2 * (s // 2):12 - 2 * (s // 2), :].rearrange("p h e -> p (h e)"),
                                           ident)
            last.then_inc(sem("ev_qkT_ps"), 1)
            ada_columns(1, 3)
            pe.wait_ge(sem("ev_qT"), 2)
            pe.wait_ge(sem("ev_kT"), 1)

            def ev_scores(n):
                t, i, w = n // 8, n % 8 // 2, n % 2
                if n >= 3:
                    pe.wait_ge(sem("ev_p"), n - 2)
                mm(pb(n % 3), qT[64 * w:64 * w + 64, i, P * t:P * (t + 1)], kT[64 * w:64 * w + 64, :],
                   start=True, stop=True).then_inc(sem("ev_s"), 1)

            def ev_transposed(n):
                pe.wait_ge(sem("ev_p"), n + 1)
                if n >= 2:
                    pe.wait_ge(sem(("ev_pT_dve", "ev_pT_act")[n % 2]), n // 2)
                for s in range(4):
                    last = nc.tensor.transpose(ps[:, 4 + n % 2, P * s:P * (s + 1)], pexp[:, n % 2, P * s:P * (s + 1)], ident)
                last.then_inc(sem("ev_pT_ps"), 1)

            def ev_values(n):
                t, i, w = n // 8, n % 8 // 2, n % 2
                pe.wait_ge(sem(("ev_pT_dve", "ev_pT_act")[w]), n // 2 + 1)
                for s in range(4):
                    last = mm(ps[:, 6 + t, 64 * (n % 8):64 * (n % 8) + 64], pT[:, w, s, :], vall[:, s, 64 * w:64 * w + 64],
                              start=(s == 0), stop=(s == 3))
                last.then_inc(sem("ev_pv"), 1)

            pe.wait_ge(sem("gpad"), 2)
            pe.wait_ge(sem("cv_gate"), 2)
            def cv_sums(n):
                if n == 0:
                    pe.wait_ge(sem("conv"), CT * CONVK)
                    pe.wait_ge(sem("cleared"), 3)
                    pe.wait_ge(sem("ev_attn"), 2)
                else:
                    pe.wait_ge(sem("cv_sq"), 1)
                for c in range(CT):
                    last = mm(ps[:, 6, N * n:N * (n + 1)], ones[:, 0:P], (cacc, csq)[n][:, c, :],
                              start=(c == 0), stop=(c == CT - 1))
                last.then_inc(sem("cv_sum"), 1)

            ev_scores(0)
            ev_scores(1)
            for n in range(NT * NQ):
                if n + 2 < NT * NQ:
                    ev_scores(n + 2)
                ev_transposed(n)
                if n:
                    ev_values(n - 1)
                if n % 4 == 0 and n:
                    ada_columns(1 + n // 4, 3)
                if n in (LN_AT, LN_AT + 1):
                    cv_sums(n - LN_AT)
                if n % 4 == 0:
                    pe.wait_ge(sem("mod_cols"), 2 + n // 4)
                ada(2 + n // 4, n % 4, 3)
            ev_values(NT * NQ - 1)
            pe.wait_ge(sem("ev_attn"), 4)
            pe.wait_ge(sem("ev_pT_dve"), 8)
            pe.wait_ge(sem("ev_pT_act"), 8)
            for k in range(4):
                for t in range(NT):
                    last = nc.tensor.transpose(ps[:, 4 + k // 2, N * (k % 2) + P * t:N * (k % 2) + P * (t + 1)],
                                               attn[:, t, P * k:P * (k + 1)], ident)
                if k % 2:
                    last.then_inc(sem("ev_aT_ps"), 1)
            ada_columns(5, 3)
            pe.wait_ge(sem("ev_aT"), 2)
            pe.wait_ge(sem("cv_out"), 4)
            pe.wait_ge(sem("ev_p"), NT * NQ)
            pe.wait_ge(sem("roots"), 2)
            for j in range(2):
                i = FIRST["ev_out"] + j
                arrived(pe, i)
                for t in range(NT):
                    for k in range(KD):
                        src = aT[:, k, P * t:P * (t + 1)] if k < 4 else cacc[:, k - 4, P * t:P * (t + 1)]
                        last = mm(pb(((6, 7), (0, 1))[j][t]), src, slot8(i)[:, k, :], start=(k == 0), stop=(k == KD - 1))
                used(last)

            def route(l):
                name = f"moe{l}"
                pe.wait_ge(sem("h_ready"), 4 * (l + 1))
                transposes(name, rows)
                normed_columns(name)
                pe.wait_ge(sem("params_in"), PARAMS * 16)
                for t in range(NT):
                    for k in range(KD):
                        last = mm(ps[:, 0, E * t:E * (t + 1)], xT[:, k, P * t:P * (t + 1)], wr[:, l, k, :],
                                  start=(k == 0), stop=(k == KD - 1))
                last.then_inc(sem("mo_logits"), 1)
                pe.wait_ge(sem("mo_aff"), l + 1)
                for t in range(NT):
                    last = nc.tensor.transpose(ps[0:E, 1, P * t:P * (t + 1)], aff[:, t, :], ident)
                    if l == t == 0:
                        last.then_inc(sem("mo_comb"), 1)
                last.then_inc(sem("mo_affT_ps"), 1)
                pe.wait_ge(sem("mo_rank"), l + 1)
                for t in range(NT):
                    last = nc.tensor.transpose(ps[:, 2, E * t:E * (t + 1)], rank[0:E, P * t:P * (t + 1)], ident[0:E, 0:E])
                    if l == t == 0:
                        last.then_inc(sem("mo_hT_ps"), 1)
                last.then_inc(sem("mo_rankT_ps"), 1)
                pe.wait_ge(sem("mo_lists"), l + 1)

            def experts(loop):
                l, g0, g1, base = loop
                with pe.Fori(g0, g1) as g:
                    n = g + GROUPS * l

                    def chunk(c):
                        i = base + c
                        pe.wait_ge(sem(f"slot{i % SLOTS}_loaded"), 16 * (PER_GROUP // SLOTS) * g + 16 * (i // SLOTS + 1))
                        return slot4(i)

                    def product(c0, banks, src):
                        for k in range(KD):
                            w = chunk(c0 + k)
                            for half in range(2):
                                for j in range(EG):
                                    last = mm(ps[32 * j:32 * j + 32, banks[half], :], src[:, k, CAP * j:CAP * (j + 1)],
                                              w[:, j, 512 * half:512 * half + 512], start=(k == 0), stop=(k == KD - 1))
                            used(last)

                    pe.wait_ge(sem("mo_h"), 4 * n + 1)
                    for k in range(KD):
                        for t in range(NT):
                            last = mm(ps[:, 6 + k // 4, P * (k % 4):P * (k % 4 + 1)], rows[:, t, P * k:P * (k + 1)],
                                      onehot[:, t, bass.ds(g * P, P)], start=(t == 0), stop=(t == NT - 1))
                        if k % 4 == 3:
                            last.then_inc(sem("mo_gather"), 1)
                    mm(pb(4), cst[0:E, C_E4:C_E4 + P], RA[0:E].rearrange("e g v n -> e (g v n)")[:, bass.ds(g * 2 * N, 2 * N)],
                       start=True, stop=True).then_inc(sem("mo_bc"), 1)
                    pe.wait_ge(sem("mo_xsT_dve"), n + 1)
                    pe.wait_ge(sem("mo_xsT_act"), n + 1)
                    product(0, (0, 1), xsT)
                    product(KD, (2, 3), xsT)
                    pe.wait_ge(sem("mo_hid"), n + 1)
                    for k in range(KD):
                        last = nc.tensor.transpose(ps[:, 6 + k // 4, P * (k % 4):P * (k % 4 + 1)], hid[:, P * k:P * (k + 1)],
                                                   ident)
                        if k % 4 == 3:
                            last.then_inc(sem("mo_hT_ps"), 1)
                    pe.wait_ge(sem("mo_hT_dve"), n + 1)
                    pe.wait_ge(sem("mo_hT_act"), n + 1)
                    pe.wait_ge(sem("mo_sel"), n + 1)
                    product(2 * KD, (4, 5), hT)
                    pe.wait_ge(sem("mo_ym"), 2 * n + 2)
                    for i in range(4):
                        t, half = i // 2, i % 2
                        mm(pb((6, 7, 4, 5)[i]), sel_w[:, P * t:P * (t + 1)], ym[:, 512 * half:512 * half + 512],
                           start=True, stop=True).then_inc(sem("mo_comb"), 1)
                pe.wait_ge(sem("mo_h"), 4 * (GROUPS * l + g1) + 1)

            route(0)
            experts(LOOPS[0])
            transposes("mem", mem_rows)
            normed_columns("mem")
            for j in range(4):
                i = FIRST["wkv"] + j
                arrived(pe, i)
                used(to_rows(i, memT, ((2 * j + 4) % 8, (2 * j + 5) % 8)))
            pe.wait_ge(sem("xk_normed"), 1)
            pe.wait_ge(sem("xkv"), 4)
            row_transposes(xk, (4, 5, 6, 7))
            pe.wait_ge(sem("cols"), 4)
            pe.wait_ge(sem("xkv"), 8)
            experts(LOOPS[1])

            transposes("mix1", rows)
            normed_columns("mix1")
            for j in range(6):
                i = FIRST["sc_in"] + j
                arrived(pe, i)
                if j >= 4:
                    pe.wait_ge(sem("sc_bc"), j - 3)
                used(to_columns(i, xT, (2 * j % 8, 2 * j % 8 + 1)))
            pe.wait_ge(sem("sc_y"), 2)
            pe.wait_ge(sem("sc_bc"), 4)
            for j in range(2):
                i = FIRST["sc_out"] + j
                arrived(pe, i)
                used(to_rows(i, yS, (4 + 2 * j, 5 + 2 * j)))

            route(1)
            experts(LOOPS[2])

            transposes("mix2", rows)
            normed_columns("mix2")
            i = FIRST["w_small"]
            arrived(pe, i)
            pe.wait_ge(sem("forget_cols"), 16)
            for c0, m, col in ((0, FOXH, 0), (32, 16, N)):
                for k in range(KD):
                    last = mm(ps[0:m, 0, col:col + N], slot8(i)[:, k, c0:c0 + m], xT[:, k, :],
                              start=(k == 0), stop=(k == KD - 1))
            used(last)
            i = FIRST["w_gqk"]
            arrived(pe, i)
            used(to_columns(i, xT, (1, 2)))
            pe.wait_ge(sem("glr"), 1)
            pe.wait_ge(sem("gate2_in"), 4 * 16)
            for r in range(2):
                last = mm(ps[:, 3, N * r:N * (r + 1)], gate2[:, P * r:P * (r + 1)], glrT[0:16, :], start=True, stop=True)
            last.then_inc(sem("gl_ps"), 1)
            for name, banks in (("w_fq", (4, 5)), ("w_fk", (6, 7)), ("w_fv", (0, 1)), ("w_gv", (2, 3)), ("w_gr", (6, 7))):
                i = FIRST[name]
                arrived(pe, i)
                if name == "w_fv":
                    pe.wait_ge(sem("gate_abs"), 1)
                    pe.wait_ge(sem("gqk"), 2)
                if name == "w_gv":
                    pe.wait_ge(sem("gate_abs"), 2)
                if name == "w_gr":
                    pe.wait_ge(sem("fqk"), 4)
                used(to_rows(i, xT, banks))
            pe.wait_ge(sem("values"), 4)
            pe.wait_ge(sem("fqk_normed"), 1)
            for w in range(2):
                for r in range(4):
                    for t in range(NT):
                        last = nc.tensor.transpose(ps[:, 2 * w + r // 2, N * (r % 2) + P * t:N * (r % 2) + P * (t + 1)],
                                                   fqk[:, t, 8 * w + 2 * r:8 * w + 2 * r + 2, :].rearrange("p h e -> p (h e)"),
                                                   ident)
                    if r % 2:
                        last.then_inc(sem("cols_ps"), 1)
            pe.wait_ge(sem("gl_klast"), 1)
            for t in range(NT):
                for r in range(2):
                    last = nc.tensor.transpose(ps[:, 4, P * (2 * t + r):P * (2 * t + r + 1)], gkT[:, r, P * t:P * (t + 1)], ident)
            last.then_inc(sem("kl_ps"), 1)
            pe.wait_ge(sem("gr"), 2)
            for w in range(2):
                for t in range(NT):
                    for r in range(2):
                        s = slice(64 * w, 64 * w + 64)
                        last = mm(ps[:, 5 + w, P * (2 * t + r):P * (2 * t + r + 1)], kdec[s, r, P * t:P * (t + 1)],
                                  gqT[s, r, P * t:P * (t + 1)], start=True, stop=True)
                last.then_inc(sem("A_ps"), 1)
            pe.wait_ge(sem("klrow"), 1)
            for chunks, bank in (((0, 2), 7), ((1,), 4)):
                for c in chunks:
                    s, t = slice(GCH * (c % 2), GCH * (c % 2) + GCH), c // 2
                    for hd in range(GLAH):
                        r, w = hd // 2, hd % 2
                        col = GDV * (2 * r + c // 2) if bank == 7 else GDV * r
                        last = mm(ps[64 * w:64 * w + 64, bank, col:col + GDV], klrow[s, t, r, 64 * w:64 * w + 64],
                                  gv[s, t, GDV * hd:GDV * (hd + 1)], start=True, stop=True)
                last.then_inc(sem("dS_ps"), 1)
            pe.wait_ge(sem("cols"), 8)
            pe.wait_ge(sem("lf_cum"), 1)
            for t in range(NT):
                last = nc.tensor.transpose(ps[:, 0, FOXH * t:FOXH * (t + 1)], lf2[0:FOXH, P * t:P * (t + 1)],
                                           ident[0:FOXH, 0:FOXH])
            last.then_inc(sem("ccol_ps"), 1)
            for j, b in enumerate((1, 2, 3, 5)):
                if b == 5:
                    pe.wait_ge(sem("AT"), 2)
                for w in range(2):
                    hd = 2 * j + w
                    last = mm(ps[:, b, N * w:N * (w + 1)], ident[0:FOXH, hd:hd + 1].broadcast_to([FOXH, P]), lf2[0:FOXH, :],
                              start=True, stop=True)
                last.then_inc(sem("nb_ps"), 1)
            pe.wait_ge(sem("states"), 1)
            pe.wait_ge(sem("ccol"), 1)
            pe.wait_ge(sem("AT"), 2)
            for t in range(NT):
                for hd in range(GLAH):
                    r, w = hd // 2, hd % 2
                    for c in (2 * t, 2 * t + 1):
                        o = slice(GCH * (c % 2), GCH * (c % 2) + GCH)
                        out = ps[o, GO[t][w], GDV * r:GDV * (r + 1)]
                        last = mm(out, AT[:, t, hd, o], gv[:, t, GDV * hd:GDV * (hd + 1)], start=True, stop=(c == 0))
                        if c:
                            last = mm(out, gqT[64 * w:64 * w + 64, r, GCH * c:GCH * (c + 1)],
                                      state[64 * w:64 * w + 64, r, c - 1, :], start=False, stop=True)
                last.then_inc(sem("go_ps"), 1)

            def fox_scores(m):
                t, r = m // 4, m % 4
                for w in range(2):
                    n = 2 * m + w
                    if n >= 4:
                        pe.wait_ge(sem("fx_max"), n - 3)
                    s, nk = slice(64 * w, 64 * w + 64), P * (t + 1)
                    mm(ps[:, FS[n % 4], 0:nk], fT[s, 0, r, P * t:P * (t + 1)], fT[s, 1, r, 0:nk],
                       start=True, stop=True).then_inc(sem("fx_s"), 1)

            def fox_transposed(n):
                pe.wait_ge(sem("fx_p"), n + 1)
                if n >= 2:
                    pe.wait_ge(sem(("fx_pT_dve", "fx_pT_act")[n % 2]), n // 2)
                for s in range(n // FOXH + 1):
                    last = nc.tensor.transpose(ps[:, FTB[n % 2], P * s:P * (s + 1)], fp[:, n % 2, P * s:P * (s + 1)], ident)
                last.then_inc(sem("fx_pT_ps"), 1)

            def fox_values(n):
                t, hd = n // FOXH, n % FOXH
                pe.wait_ge(sem(("fx_pT_dve", "fx_pT_act")[n % 2]), n // 2 + 1)
                for s in range(t + 1):
                    last = mm(ps[:, FO[t], HD * hd:HD * (hd + 1)], fpT[:, n % 2, P * s:P * (s + 1)],
                              fv[:, s, HD * hd:HD * (hd + 1)], start=(s == 0), stop=(s == t))
                last.then_inc(sem("fx_pv"), 1)

            pe.wait_ge(sem("nb"), 4)
            pe.wait_ge(sem("AT"), 2)
            pe.wait_ge(sem("go_sb"), 1)
            fox_scores(0)
            for n in range(NT * FOXH):
                if n % 2 == 0 and n // 2 + 1 < NT * FOXH // 2:
                    fox_scores(n // 2 + 1)
                fox_transposed(n)
                if n:
                    fox_values(n - 1)
            fox_values(NT * FOXH - 1)
            pe.wait_ge(sem("mix_rows"), 3)
            row_transposes(rows, (0, 1, 2, 3))
            pe.wait_ge(sem("cols"), 12)
            for j in range(2):
                i = FIRST["w_out"] + j
                arrived(pe, i)
                used(to_rows(i, xT, (4 + 2 * j, 5 + 2 * j)))

            pe.wait_ge(sem("h_ready"), 12)
            transposes("xattn", rows)
            normed_columns("xattn")
            for j in range(2):
                i = FIRST["wq"] + j
                arrived(pe, i)
                used(to_rows(i, xT, (2 * j, 2 * j + 1)))
            pe.wait_ge(sem("xq_normed"), 1)
            row_transposes(xq, (4, 5, 6, 7))
            pe.wait_ge(sem("cols"), 16)

            pe.wait_ge(sem("memkv_in"), 32)

            def x_scores(n):
                t, hd = n // XH, n % XH
                if n >= 2:
                    pe.wait_ge(sem("xa_p"), n - 1)
                for kk in range(2):
                    last = mm(ps[:, n % 2, 0:N], xqT[:, 2 * hd + kk, P * t:P * (t + 1)], xkT[:, 2 * hd + kk, :],
                              start=(kk == 0), stop=(kk == 1))
                last.then_inc(sem("xa_s"), 1)

            def x_transposed(n):
                pe.wait_ge(sem("xa_p"), n + 1)
                if n >= 2:
                    pe.wait_ge(sem("xa_pT"), n - 1)
                for s in range(2):
                    last = nc.tensor.transpose(ps[:, 2 + n % 2, P * s:P * (s + 1)], xp[:, n % 2, P * s:P * (s + 1)], ident)
                last.then_inc(sem("xa_pT_ps"), 1)

            def x_values(n):
                t, hd = n // XH, n % XH
                pe.wait_ge(sem("xa_pT"), n + 1)
                for s in range(2):
                    last = mm(ps[:, 4 + 2 * t + hd // 2, XD * (hd % 2):XD * (hd % 2) + XD], xpT[:, n % 2, P * s:P * (s + 1)],
                              xv[:, s, XD * hd:XD * (hd + 1)], start=(s == 0), stop=(s == 1))
                last.then_inc(sem("xa_pv"), 1)

            x_scores(0)
            for n in range(NT * XH):
                if n + 1 < NT * XH:
                    x_scores(n + 1)
                x_transposed(n)
                if n:
                    x_values(n - 1)
            x_values(NT * XH - 1)
            pe.wait_ge(sem("xo"), 4)
            row_transposes(rows, (0, 1, 2, 3))
            pe.wait_ge(sem("cols"), 20)
            for j in range(2):
                i = FIRST["wo"] + j
                arrived(pe, i)
                used(to_rows(i, xT, (4 + 2 * j, 5 + 2 * j)))

            pe.wait_ge(sem("h_ready"), 16)
            transposes("mlp", rows)
            normed_columns("mlp")

            pe.wait_ge(sem("mlp_split"), 1)

            def split_product(out, lhs, rhs, start, stop):
                for n, (x, y) in enumerate(((0, 1), (1, 0), (0, 0))):
                    last = mm(out, lhs[x], rhs[y], start=start and n == 0, stop=stop and n == 2)
                return last

            def up(j):
                if j >= 2:
                    pe.wait_ge(sem("mlp_relu"), j - 1)
                for half, (n, i, w, lo, hi) in enumerate(mlp_halves("up", j)):
                    pe.wait_ge(sem("w_split"), n + 1)
                    for c in range(2):
                        s = slice(P * c, P * (c + 1))
                        for k in range(KD):
                            last = split_product(ps[:, 4 + 2 * (j % 2) + half, N * c:N * (c + 1)], (hi[:, k, s], lo[:, k, s]),
                                                 (xT_hi[:, k, :], xT_r[:, k, :]), k == 0, k == KD - 1)
                    last.then_inc(sem("w_halves_used"), 1)

            def down(j):
                pe.wait_ge(sem("mlp_split"), j + 2)
                for half, (n, i, w, lo, hi) in enumerate(mlp_halves("down", j)):
                    pe.wait_ge(sem("w_split"), n + 1)
                    for kk in range(2):
                        k = 2 * half + kk
                        for t in range(NT):
                            s = slice(P * t, P * (t + 1))
                            for col in range(2):
                                c = slice(512 * col, 512 * col + 512)
                                last = split_product(pb(2 * t + col),
                                                     (uT_hi[:, j % 2, k, s], uT_lo[:, j % 2, k, s]),
                                                     (hi[:, kk, c], lo[:, kk, c]), j == k == 0, j == 7 and k == 3)
                    last.then_inc(sem("w_halves_used"), 1)

            for kind, j in MLP:
                (up if kind == "up" else down)(j)


_WEIGHTS = ['x', 'c', 'ctx', 'c_ctx', 'ada_w', 'ada_b', 'norm1_g', 'norm2_g', 'ev_w_in', 'ev_q_g', 'ev_k_g', 'ev_conv_w',
            'ev_conv_b', 'ev_ln_g', 'ev_ln_b', 'ev_w_out', 'sc_w_in', 'sc_conv_w', 'sc_w_out', 'moe_w_r', 'moe_w_gate',
            'moe_w_up', 'moe_w_down', 'final_g', 'mem_2', 'norm_mix_g_2', 'w_in_2', 'fox_b_f_2', 'fox_q_norm_g_2',
            'fox_k_norm_g_2', 'gla_w_gate2_2', 'gla_b_gate_2', 'gla_out_norm_g_2', 'w_out_2', 'norm_xattn_g_2',
            'norm_mem_g_2', 'xattn_wq_2', 'xattn_wkv_2', 'xattn_q_norm_g_2', 'xattn_k_norm_g_2', 'xattn_wo_2',
            'norm_mlp_g_2', 'mlp_w1_2', 'mlp_w2_2']


def kernel(**inputs):
    import concourse.bacc as bacc
    from concourse.bass_utils import run_bass_kernel_spmd

    nc = bacc.Bacc("TRN2", target_bir_lowering=False, num_devices=1)
    arrays = {n: np.ascontiguousarray(inputs[n]) for n in _WEIGHTS}
    arrays["cst"], arrays["cst_i"] = constants()
    a = {n: nc.dram_tensor(f"in_{n}", v.shape, mybir.dt.from_np(v.dtype), kind="ExternalInput").ap()
         for n, v in arrays.items()}
    a["out"] = nc.dram_tensor("out", (1, N, D), F32, kind="ExternalOutput").ap()
    build(nc, a)
    r = run_bass_kernel_spmd(nc, [{f"in_{n}": v for n, v in arrays.items()}], core_ids=[0])
    return r.results[0]["out"]
```

```python
import numpy as np
import concourse.bass as bass
from concourse import mybir
from contextlib import ExitStack

F32 = mybir.dt.float32
I32 = mybir.dt.int32
F32R = mybir.dt.float32r
ACT = mybir.ActivationFunctionType
ALU = mybir.AluOpType
AX = mybir.AxisListType

P = 128
D = 1024
N = 256
NT = N // P
KD = D // P
EPS = 1e-6
HD = 64
NQ, NKV = 8, 2
AW = NQ * HD
CONVK = 31
CT = 4
PADW = N + CONVK - 1
SCK = 3
E, CAP, F = 16, 32, 1024
EG = 4
GROUPS = E // EG
FOXH, GLAH, GDK, GDV, GCH = 8, 4, 64, 128, 64
GLA_TAU = 16.0
XH, XD = 4, 256
SLOTS = 8
SLOT = 4096
MASKED = -1e30

C_ID, C_FOX, C_COS, C_SIN, C_T, C_IOTA, C_SCAN, C_E4, C_GRP = 0, 128, 256, 320, 384, 385, 417, 673, 801
C_W = 805

ADA = ["ada0a", "ada0b", "ada0c", "ada1a", "ada1b", "ada1c"]
NORMS = ["x", "ctx", "moe0", "mem", "mix1", "moe1", "final", "mix2", "xattn", "mlp"]
TRANSPOSED = [n for n in NORMS if n != "final"]
NORMED = [n for n in NORMS if n not in ("mem", "mix2", "xattn", "mlp")]


def constants():
    c = np.zeros((P, C_W), np.float32)
    p = np.arange(P)
    c[:, C_ID:C_ID + P] = np.eye(P, dtype=np.float32)
    c[:, C_FOX:C_FOX + P] = np.where(p[None, :] <= p[:, None], 0.0, MASKED)
    half = np.float32(32)
    inv = np.float32(10000.0) ** (-np.arange(0, 32, 2, dtype=np.float32) / half)
    n = np.arange(N)
    ang = np.concatenate([(n // 64).astype(np.float32)[:, None] * inv,
                          (n % 64).astype(np.float32)[:, None] * inv], axis=1).astype(np.float32)
    for t in range(NT):
        c[:, C_COS + 32 * t:C_COS + 32 * t + 32] = np.cos(ang[t * P:(t + 1) * P])
        c[:, C_SIN + 32 * t:C_SIN + 32 * t + 32] = np.sin(ang[t * P:(t + 1) * P])
    c[:, C_T] = p % CAP + 1
    c[:, C_IOTA:C_IOTA + CAP] = np.arange(CAP) + 1
    c[:, C_SCAN:C_SCAN + N] = (n % GCH != 0)
    e = np.arange(E)
    c[0:E, C_E4:C_E4 + P] = (p[None, :] // CAP == e[:, None] % EG)
    c[0:E, C_GRP:C_GRP + GROUPS] = (np.arange(GROUPS)[None, :] == e[:, None] // EG)
    m = ((p[:, None] // GCH == p[None, :] // GCH) & (p[:, None] <= p[None, :])).astype(np.int32)
    return c, m


STREAM = [("ada0a", 4), ("ev_q", 1), ("ev_kv", 1), ("ev_u", 1), ("ada0b", 2), ("ev_gate", 1),
          ("ada0b_rest", 2), ("ada0c", 4), ("ada1a", 4), ("ada1b", 4), ("ada1c", 4), ("ev_out", 2), ("moe0", 48), ("wk", 2),
          ("moe0b", 24), ("wv", 2), ("moe0c", 24),
          ("sc_in", 6), ("sc_out", 2), ("moe1", 96),
          ("w_small", 1), ("w_gqk", 1), ("w_fq", 1), ("w_fk", 1), ("w_fv", 1), ("w_gv", 1), ("w_gr", 1),
          ("w_out", 2), ("wq", 2), ("wo", 2), ("mlp", 16)]
FIRST = {}
_n = 0
for _name, _k in STREAM:
    FIRST[_name] = _n
    _n += _k
PER_GROUP = 3 * KD
assert PER_GROUP % SLOTS == 0
N0, RAW = FIRST["w_small"], SLOTS - 2


def slot_of(i):
    return i % SLOTS if i < N0 else (N0 + (i - N0) % RAW) % SLOTS


def loads_until(i):
    return i // SLOTS + 1 if i < N0 else (N0 - 1 - slot_of(i)) // SLOTS + 1 + (i - N0) // RAW + 1


def chunk_before(i):
    return i - SLOTS if i < N0 + RAW else i - RAW


LOOPS = [(0, 0, 2, FIRST["moe0"]), (0, 2, 3, FIRST["moe0b"] - 2 * PER_GROUP), (0, 3, GROUPS, FIRST["moe0c"] - 3 * PER_GROUP),
         (1, 0, GROUPS, FIRST["moe1"])]


def build(nc, a):
    ctx = ExitStack()
    with ctx:
        place = {}

        def sb(name, shape, dt=F32):
            place[name] = -(-nc.sbuf_base // 32) * 32
            return ctx.enter_context(nc.sbuf_tensor(name, shape, dt))

        def parts_of(name, floats, first=0):
            return nc.alloc_sbuf_tensor_at(f"{name}_parts_{first}", [P, floats], F32R, offset=place[name] + 4 * first)[:, :]

        sems = {}

        def sem(name):
            if name not in sems:
                sems[name] = ctx.enter_context(nc.semaphore(name))
            return sems[name]

        ring = sb("ring", [P, SLOTS, SLOT])
        h_t = sb("h", [P, NT * D])
        rows_t = sb("rows", [P, NT * D])
        xT_t = sb("xT", [P, KD * N])
        cst = sb("cst", [P, C_W])
        glam = sb("gla_mask", [P, P], I32)
        gcol = sb("gain_cols", [P, 8 + SCK, KD])
        mcol = sb("mod_cols", [P, 10, KD])
        acol = sb("scale_cols", [P, 5, KD])
        wr = sb("router_w", [P, 2, KD, E])
        gate_bc = sb("gate_bc", [P, 1280])
        ss = sb("ss", [P, len(NORMS), NT])
        ms = sb("ms", [P, len(NORMS), NT])
        rstd = sb("rstd", [P, len(NORMS), NT])
        mhalf = sb("mhalf", [P, NT])
        sil = sb("silu_c", [P, KD, 32])
        ones = sb("ones", [P, N])
        lnrow = sb("ln_row", [P, N])
        sm = sb("small", [P, 256])
        scr = sb("scratch", [P, 10496])
        ps = ctx.enter_context(nc.psum_tensor("ps", [P, 8, 512], F32))
        memk_dram = nc.dram_tensor("memory_keys", (P, KD * N), F32).ap()
        memv_dram = nc.dram_tensor("memory_values", (P, NT * D), F32).ap()
        gate_dram = nc.dram_tensor("gate_scratch", (2, 2, D), F32).ap()

        h = h_t[:, :].rearrange("p (t d) -> p t d", t=NT)
        rows = rows_t[:, :].rearrange("p (t d) -> p t d", t=NT)
        xT = xT_t[:, :].rearrange("p (k n) -> p k n", k=KD)
        ident = cst[:, C_ID:C_ID + P]
        scan_mask = cst[:, C_SCAN:C_SCAN + N]

        def at(off, **dims):
            n = 1
            for v in dims.values():
                n *= v
            v = scr[:, off:off + n]
            if len(dims) == 1:
                return v
            names = " ".join(dims)
            return v.rearrange(f"p ({names}) -> p {names}", **dims)

        mrow = at(0, b=3, q=4, i=P)
        ctx_rows = at(1536, t=NT, d=D)
        cT = at(3584, k=KD, n=N)
        qk = at(5632, t=NT, h=12, e=HD)
        vall = at(7168, t=4, e=128)
        gpad = at(7680, c=CT, n=PADW)
        sg = cacc = at(8824, c=CT, n=N)
        csq = at(5632, c=CT, n=N)
        cw = at(9848, c=CT, j=34)
        cwrow = at(8824, d=512)
        grow = at(9336, i=P)
        crow = at(9464, i=P)
        ada_b = at(9984, i=512)
        sq = rows_t[:, 0:1536].rearrange("p (t h e) -> p t h e", t=NT, h=12)
        ra = rows_t[:, 0:640].rearrange("p (t h e) -> p t h e", t=NT, h=10)
        rb = rows_t[:, 640:1280].rearrange("p (t h e) -> p t h e", t=NT, h=10)
        rc = at(3584, t=NT, h=10, e=32)
        rd = at(4224, t=NT, h=10, e=32)
        kT = at(1536, s=512)
        qT = at(2048, i=4, n=N)
        pexp = at(3584, b=2, s=512)
        pT = at(4608, b=2, s=4, q=P)
        attn = xT_t[:, 0:1024].rearrange("p (t e) -> p t e", t=NT)
        xsT = at(0, k=KD, c=P)
        hid = at(1024, f=F)
        hT = at(2048, k=KD, c=P)
        ym = at(3072, d=D)
        sel_w = at(4096, n=N)
        aff_bc = at(4352, n=N)
        RA = at(4608, g=GROUPS, v=2, n=N)
        onehot = at(6656, t=NT, s=E * CAP)
        affT = at(7680, n=N)
        work = at(7936, n=N)
        rank = at(8192, n=N)
        final_bc = at(8448, d=D)
        aff = at(9472, t=NT, e=E)
        rankT = at(9504, t=NT, e=E)
        smaskE = at(9600, n=N)
        yS = at(0, c=KD, n=N)
        cS = at(2048, c=KD, n=N)
        cx = at(4096, c=KD, n=N + 2)
        gqT = at(0, r=2, n=N)
        gkT = at(512, r=2, n=N)
        kdec = at(1024, r=2, n=N)
        glog = at(1536, r=2, n=N)
        bcum = at(2048, r=2, n=N)
        ex = at(2560, x=2, r=2, n=N)
        AT = at(2560, t=NT, h=GLAH, c=P)
        gv = at(3584, t=NT, e=512)
        gr = at(4608, t=NT, e=512)
        klrow = at(5632, t=NT, r=2, e=P)
        state = at(6144, r=2, n=3, v=GDV)
        fqk = at(6912, t=NT, h=16, e=HD)
        NB = at(6912, h=FOXH, n=N)
        NB0 = rows[:, :, 0:512].rearrange("p t (h n) -> p t h n", n=P)
        fv = at(8960, t=NT, e=512)
        fp = at(5632, b=2, s=N)
        fpT = at(9984, b=2, s=N)
        lf = wr[:, :, :, :].rearrange("p l k e -> p (l k e)")
        lf2 = lnrow[:, :]
        glrT = sil[:, :, :].rearrange("p k v -> p (k v)")
        fsq = at(5632, t=NT, h=8, e=HD)
        fT = xT_t[:, :].rearrange("p (w r n) -> p w r n", w=2, r=4)
        gsq = at(0, t=NT, e=512)
        go = at(1024, t=NT, e=512)
        mem_rows = by_rows = xT_t[:, :].rearrange("p (t d) -> p t d", t=NT)
        xk = at(0, t=NT, d=D)
        memT = xT
        memkT = at(2048, k=KD, n=N)
        memv = by_rows
        xv = at(6144, t=NT, d=D)
        xkT = at(8192, k=KD, n=N)
        xq = at(0, t=NT, d=D)
        xqT = at(2048, k=KD, n=N)
        xp = gate_bc[:, 0:512].rearrange("p (b s) -> p b s", b=2)
        xpT = gate_bc[:, 512:1024].rearrange("p (b s) -> p b s", b=2)
        ring_r = [parts_of("ring", SLOT, SLOT * i) for i in range(SLOTS)]
        xT_r = parts_of("xT", KD * N).rearrange("p (k n) -> p k n", k=KD)

        rows_hi = parts_of("rows", KD * N).rearrange("p (k n) -> p k n", k=KD)
        x_hi = parts_of("scratch", KD * N, 4096).rearrange("p (k n) -> p k n", k=KD)
        gla_x = [parts_of("scratch", 4 * N, 2048 + 4 * N * v).rearrange("p (k n) -> p k n", k=4) for v in range(2)]
        small_hi = parts_of("ln_row", KD * 24).rearrange("p (k n) -> p k n", k=KD)
        w_hi = [ring_r[(N0 + RAW + b // 2) % SLOTS][:, SLOT // 2 * (b % 2):SLOT // 2 * (b % 2 + 1)] for b in range(4)]
        cpool = xT_t[:, 1024:1280]
        evw_hi = [rows_hi.rearrange("p k n -> p (k n)"), parts_of("scratch", SLOT // 2, 5632)]
        ev_x = [[parts_of("scratch", 4 * N, first).rearrange("p (k n) -> p k n", k=4) for first in pair]
                for pair in ((1536, 7680), (2560, 3584))]
        sc_hi = parts_of("scratch", KD * N, 6160).rearrange("p (k n) -> p k n", k=KD)
        scw_hi = [parts_of("scratch", SLOT // 2, 8208), rows_hi.rearrange("p k n -> p (k n)")]
        y_lo = parts_of("scratch", KD * N, 0).rearrange("p (k n) -> p k n", k=KD)
        y_hi = parts_of("scratch", KD * N, 2048).rearrange("p (k n) -> p k n", k=KD)
        uT = at(0, b=2, k=4, n=N)
        uT_lo = parts_of("scratch", 2048, 0).rearrange("p (b k n) -> p b k n", b=2, k=4)
        uT_hi = parts_of("scratch", 2048, 2048).rearrange("p (b k n) -> p b k n", b=2, k=4)

        class Steps:

            def __init__(self, eng, name):
                self.eng, self.sem, self.n = eng, sem(name), 0

            def mark(self, ins):
                ins.then_inc(self.sem, 1)
                self.n += 1

            def wait(self):
                self.eng.wait_ge(self.sem, self.n)

            def __call__(self, ins):
                self.mark(ins)
                self.wait()

        def arrived(eng, i):
            eng.wait_ge(sem(f"slot{slot_of(i)}_loaded"), 16 * loads_until(i))

        def used_up(eng, i):
            if i <= N0:
                eng.wait_ge(sem("chunks_used"), i + 1)
            else:
                eng.wait_ge(sem("w_halves_used"), 2 * (i - N0))

        def ada_chunk(g, c):
            return FIRST["ada0b_rest"] + c - 2 if g == 1 and c >= 2 else FIRST[ADA[g]] + c

        def whole(eng, name, j=0):
            used_up(eng, FIRST[name] + j)

        def slot8(i):
            return ring[:, slot_of(i), :].rearrange("p (k n) -> p k n", k=KD)

        def slot2(i):
            return ring[:, slot_of(i), :].rearrange("p (k n) -> p k n", k=2)

        def slot4(i):
            return ring[:, slot_of(i), :].rearrange("p (e f) -> p e f", e=EG)

        def pb(b):
            return ps[:, b, :]

        def flat(v):
            return v.rearrange("p a b -> p (a b)")

        def by_token(v):
            return v.rearrange("p (t d) -> p t d", t=NT)

        MODS = {"x": 1, "ctx": 1, "moe0": 3, "mix1": 4, "moe1": 6}
        SHIFT = {"x": 0, "ctx": 4, "moe0": 2, "mix1": 6, "moe1": 8}
        SCALE = {"x": 0, "ctx": 1, "moe0": 2, "mix1": 3, "moe1": 4}
        GAIN = {"mix2": 4, "mem": 5, "xattn": 6, "mlp": 7}

        def affine(name):
            if name in SHIFT:
                return acol[:, SCALE[name], :], mcol[:, SHIFT[name], :]
            return gcol[:, GAIN[name], :], None

        SPLIT_INPUTS = ["ev_out", "mix1", "y", "mix2", "w_out", "xattn", "wo", "mlp"]
        NORM_BANKS = {n: (4, 5, 6, 7) for n in TRANSPOSED}
        NORM_BANKS["ctx"] = (0, 1, 2, 3)
        NORM_BANKS["xattn"] = (0, 4, 6, 7)
        NORM_BANKS["mlp"] = (2, 3, 6, 7)
        qkg = gate_bc[:, 1024:1152].rearrange("p (w e) -> p w e", w=2)
        foxg = gate_bc[:, 0:128].rearrange("p (w e) -> p w e", w=2)
        glag = gate_bc[:, 128:640]
        xqg, xkg = sm[:, 216:218], gate_bc[:, 1024:1280]
        row_scale = ms[:, NORMS.index("final"), :]
        scale_bc = gate_bc[:, 1024:1280]
        gate2 = at(6912, n=N)[0:16, :]
        FS, FTB, FO = (1, 2), (6, 7), (0, 4)
        WO = ((3, 5), (1, 2))
        GLA_AT = 5
        XQT = (4, 5, 6, 7)
        XPT, XO = (6, 2), (4, 6)
        EV_SPLITS = 4
        SC_SPLITS = EV_SPLITS + 16
        GAINS = (8 + SCK) * KD
        cw1 = gcol[:, 8:8 + SCK, :].rearrange("p j c -> p c j")
        PARAMS = 10
        SMALL2 = 9
        POOL_TAPS = 19
        LN_AT = 12
        GO = ((0, 6), (4, 7))

        MLP = [("up", 0)]
        for j in range(8):
            MLP += [("up", j + 1)] * (j < 7) + [("down", j)]

        def mlp(kind, j):
            return FIRST["mlp"] + MLP.index((kind, j))

        def by_columns(i):
            return i == FIRST["w_gqk"] or i >= FIRST["mlp"] and MLP[i - FIRST["mlp"]][0] == "up"

        def halves(i):
            for half in range(2):
                n = 2 * (i - N0 - 1) + half
                hi = w_hi[n % 4]
                if by_columns(i):
                    w, lo = (v.rearrange("p (k n) -> p k n", k=KD)[:, :, 256 * half:256 * half + 256]
                             for v in (ring[:, slot_of(i), :], ring_r[slot_of(i)]))
                    hi = hi.rearrange("p (k n) -> p k n", k=KD)
                else:
                    s = slice(SLOT // 2 * half, SLOT // 2 * (half + 1))
                    w, lo = ring[:, slot_of(i), s], ring_r[slot_of(i)][:, s]
                yield n, w, lo, hi

        def ev_half(j, p):
            i, s = FIRST["ev_out"] + j, slice(SLOT // 2 * (1 - p), SLOT // 2 * (2 - p))
            return 2 * j + p, ring[:, slot_of(i), s], ring_r[slot_of(i)][:, s], evw_hi[p]

        def sc_halves(m):
            i = FIRST["sc_in"] + m
            for half in range(2):
                w, lo, hi = ring[:, slot_of(i), :], ring_r[slot_of(i)], scw_hi[half]
                if m < 6:
                    w, lo = (v.rearrange("p (k n) -> p k n", k=KD)[:, :, 256 * half:256 * half + 256] for v in (w, lo))
                    hi = hi.rearrange("p (k n) -> p k n", k=KD)
                else:
                    s = slice(SLOT // 2 * half, SLOT // 2 * (half + 1))
                    w, lo = w[:, s], lo[:, s]
                yield EV_SPLITS + 2 * m + half, w, lo, hi

        def low(eng, ops, i):
            for n, w, lo, hi in halves(i):
                eng.wait_ge(sem("w_high"), SC_SPLITS + n + 2)
                eng.wait_ge(sem("w_split"), SC_SPLITS + n + 1)
                ops.tensor_tensor(lo, w, hi.bitcast(F32), ALU.subtract).then_inc(sem("w_split"), 1)

        block = ctx.enter_context(nc.Block())

        @block.sync
        def _(sp):
            def load(i, dst, src):
                if i >= SLOTS:
                    used_up(sp, chunk_before(i))
                sp.dma_start(dst, src).then_inc(sem(f"slot{slot_of(i)}_loaded"), 16)

            def columns(name, w, count, width=512, col0=0):
                v = w.rearrange("(k p) n -> p k n", k=KD)
                for j in range(count):
                    i, c = FIRST[name] + j, col0 + width * j
                    load(i, slot8(i)[:, :, 0:width], v[:, :, c:c + width])

            def modulations(g, chunks=(0, 1, 2, 3)):
                v = a["ada_w"][g // 3].rearrange("(c k p) n -> c p k n", c=4, p=P)
                for c in chunks:
                    i = ada_chunk(g, c)
                    load(i, slot2(i), v[c, :, :, 2 * D * (g % 3):2 * D * (g % 3 + 1)])

            def experts(loop):
                l, g0, g1, base = loop
                gate = a["moe_w_gate"][l].rearrange("(g e) (k p) f -> g k p e f", e=EG, k=KD)
                up = a["moe_w_up"][l].rearrange("(g e) (k p) f -> g k p e f", e=EG, k=KD)
                down = a["moe_w_down"][l].rearrange("(g e) (k p) d -> g k p e d", e=EG, p=P)
                with sp.Fori(g0, g1) as g:
                    for c in range(PER_GROUP):
                        w, k = (gate, up, down)[c // KD], c % KD
                        sp.wait_ge(sem("chunks_used"), PER_GROUP * g + (base + c - SLOTS + 1))
                        sp.dma_start(slot4(base + c), w[g, k])\
                            .then_inc(sem(f"slot{(base + c) % SLOTS}_loaded"), 16)

            for v, c in enumerate((a["c"][0], a["c_ctx"])):
                sp.dma_start(crow[KD * v:KD * (v + 1), :], c.rearrange("(k p) -> k p", k=KD)).then_inc(sem("c_in"), 16)
            sp.dma_start(ident, a["cst"][:, C_ID:C_ID + P]).then_inc(sem("c_in"), 16)
            first = 0
            for g in (a["norm1_g"], a["norm2_g"], a["norm_mix_g_2"].unsqueeze(0), a["norm_mem_g_2"].unsqueeze(0),
                      a["norm_xattn_g_2"].unsqueeze(0), a["norm_mlp_g_2"].unsqueeze(0), a["sc_conv_w"][0]):
                n = KD * g.shape[0]
                sp.dma_start(grow[first:first + n, :], g.rearrange("l (k p) -> (l k) p", k=KD)).then_inc(sem("gains_in"), 16)
                first += n
            sp.wait_ge(sem("cleared"), 2)
            sp.dma_start(ada_b[0:24, :], a["ada_b"].rearrange("l (q n) -> (l q) n", n=512)).then_inc(sem("ada_b_in"), 16)
            modulations(0, (0, 1))
            sp.dma_start(h, a["x"][0].rearrange("(t p) d -> p t d", p=P)).then_inc(sem("x_in"), 16)
            modulations(0, (2, 3))
            sp.dma_start(ctx_rows, a["ctx"][0].rearrange("(t p) d -> p t d", p=P)).then_inc(sem("ctx_in"), 16)
            evw = a["ev_w_in"][0]
            columns("ev_q", evw, 1)
            columns("ev_kv", evw, 1, width=256, col0=512)
            columns("ev_u", evw, 1, col0=768)
            modulations(1, (0, 1))
            columns("ev_gate", evw, 1, col0=1280)
            modulations(1, (2, 3))
            for g in range(2, len(ADA)):
                modulations(g)
            columns("ev_out", a["ev_w_out"][0], 2)
            experts(LOOPS[0])
            columns("wk", a["xattn_wkv_2"], 2)
            experts(LOOPS[1])
            columns("wv", a["xattn_wkv_2"], 2, col0=D)
            experts(LOOPS[2])
            sc_in = a["sc_w_in"][0].rearrange("(k p) n -> p k n", k=KD)
            for j in range(6):
                c = D * (1, 2, 0)[j % 3] + 512 * (j // 3)
                load(FIRST["sc_in"] + j, slot8(FIRST["sc_in"] + j), sc_in[:, :, c:c + 512])
            columns("sc_out", a["sc_w_out"][0], 2)
            experts(LOOPS[3])
            w2 = a["w_in_2"]
            i = FIRST["w_small"]
            v = w2.rearrange("(k p) n -> p k n", k=KD)
            used_up(sp, chunk_before(i))
            sp.dma_start(slot8(i)[:, :, 0:8], v[:, :, 1536:1544]).then_inc(sem("forget_cols"), 16)
            sp.dma_start(slot8(i)[:, :, 32:48], v[:, :, 2568:2584]).then_inc(sem(f"slot{slot_of(i)}_loaded"), 16)
            for name, col in (("w_gqk", 1544), ("w_fq", 0), ("w_fk", 512), ("w_fv", 1024), ("w_gv", 2056), ("w_gr", 2584)):
                columns(name, w2, 1, col0=col)
            columns("w_out", a["w_out_2"], 2)
            columns("wq", a["xattn_wq_2"], 2)
            columns("wo", a["xattn_wo_2"], 2)
            w1 = a["mlp_w1_2"].rearrange("(k p) f -> p k f", k=KD)
            wd = a["mlp_w2_2"].rearrange("(c k p) d -> c p k d", k=4, p=P)
            for m, (kind, j) in enumerate(MLP):
                i = FIRST["mlp"] + m
                load(i, *((slot8(i), w1[:, :, 512 * j:512 * (j + 1)]) if kind == "up" else (slot4(i), wd[j])))
            for t in range(NT):
                for j in range(2):
                    s = slice(512 * j, 512 * j + 512)
                    sp.wait_ge(sem("h_ready"), 16 + 2 * t + j + 1)
                    sp.dma_start(a["out"][0, t * P:(t + 1) * P, s], h[:, t, s]).then_inc(sem("stored"), 16)
            sp.wait_ge(sem("stored"), 2 * 16 * NT)

        @block.scalar
        def _(act):
            link = Steps(act, "act_steps")

            act.dma_start(cwrow[0:CONVK, :], a["ev_conv_w"][0]).then_inc(sem("params_in"), 16)
            for j, n in enumerate(("ev_conv_b", "ev_ln_g", "ev_ln_b")):
                act.dma_start(cwrow[CONVK + j:CONVK + j + 1, :], a[n]).then_inc(sem("params_in"), 16)
            for j, n in enumerate(("ev_q_g", "ev_k_g")):
                act.dma_start(qkg[:, j, :], a[n][0].partition_broadcast(P)).then_inc(sem("params_in"), 16)
            act.dma_start(cst[:, C_FOX:], a["cst"][:, C_FOX:]).then_inc(sem("params_in"), 16)
            for l in range(2):
                act.dma_start(wr[:, l], a["moe_w_r"][l].rearrange("(k p) e -> p k e", k=KD)).then_inc(sem("params_in"), 16)
            act.dma_start(glam[:, :], a["cst_i"]).then_inc(sem("params_in"), 16)

            act.wait_ge(sem("c_ps"), 1)
            act.wait_ge(sem("cleared"), 1)
            nc.scalar.activation(sil[:, :, 0:2], ps[:, 2, 0:2 * KD].rearrange("p (v k) -> p k v", v=2), ACT.Silu)\
                .then_inc(sem("sil"), 1)

            def squares(name, src, junk, ready=None, first=0, step=1):
                u = NORMS.index(name)
                for t in range(NT):
                    if ready:
                        act.wait_ge(sem(ready), first + step * t)
                    nc.scalar.activation(junk[:, t, :], src[:, t, :], ACT.Square,
                                         accum_out=ss[:, u, t:t + 1]).then_inc(sem("norm_ss"), 1)

            def transposed(name, dst):
                v, bank, (scale, shift) = TRANSPOSED.index(name), NORM_BANKS[name], affine(name)
                if name in MODS:
                    act.wait_ge(sem("mod_cols"), MODS[name])
                for b in (1, 3):
                    act.wait_ge(sem("norm_T"), 4 * v + b + 1)
                    for k in (2 * b, 2 * b + 1):
                        src = ps[:, bank[b], 256 * (k % 2):256 * (k % 2) + 256]
                        if shift is None:
                            last = nc.scalar.activation(dst[:, k, :], src, ACT.Copy, scale=scale[:, k:k + 1])
                        else:
                            last = nc.scalar.activation(dst[:, k, :], src, ACT.Identity, scale=scale[:, k:k + 1],
                                                        bias=shift[:, k:k + 1])
                    last.then_inc(sem("xT_ready"), 1)

            xT_rows = by_token(xT_t[:, :])

            def high(i, only=(0, 1)):
                arrived(act, i)
                for half, (n, w, lo, hi) in enumerate(halves(i)):
                    if half in only:
                        if n < 4:
                            used_up(act, N0 - 1)
                        else:
                            act.wait_ge(sem("w_halves_used"), n - 3)
                        nc.scalar.activation(hi, w, ACT.Copy).then_inc(sem("w_high"), 1)

            def norm_high(name, dst):
                v, bank, scale = TRANSPOSED.index(name), NORM_BANKS[name], affine(name)[0]
                for b in range(4):
                    act.wait_ge(sem("norm_T"), 4 * v + (4 if dst is rows_hi else b + 1))
                    for k in (2 * b, 2 * b + 1):
                        last = nc.scalar.activation(dst[:, k, :], ps[:, bank[b], 256 * (k % 2):256 * (k % 2) + 256], ACT.Copy,
                                                    scale=scale[:, k:k + 1])
                    last.then_inc(sem("x_high"), 1)

            def columns_high(first, banks, dst):
                for b, bank in enumerate(banks):
                    act.wait_ge(sem("cols_ps"), first + b + 1)
                    nc.scalar.activation(flat(dst[:, 2 * b:2 * b + 2, :]), pb(bank), ACT.Copy).then_inc(sem("x_high"), 1)

            act.wait_ge(sem("x_in"), 16)
            squares("x", h, xT_rows)
            act.wait_ge(sem("ctx_in"), 16)
            squares("ctx", ctx_rows, by_token(flat(cT)))
            transposed("x", xT)
            transposed("ctx", cT)
            whole(act, "ev_q")
            for t in range(NT):
                nc.scalar.activation(qk[:, t, 0:NQ, :].rearrange("p (i w) e -> p w i e", w=2),
                                     pb(t).rearrange("p (w i e) -> p w i e", w=2, e=HD), ACT.Copy)\
                    .then_inc(sem("ev_rows"), 1)
            whole(act, "ev_kv")
            for w, bank in ((0, 2), (1, 3)):
                for t in range(NT):
                    src = ps[:, bank, 256 * t:256 * t + 256]
                    nc.scalar.activation(qk[:, t, 8 + 2 * w:10 + 2 * w, :],
                                         src[:, 0:128].rearrange("p (h e) -> p h e", e=HD), ACT.Copy)\
                        .then_inc(sem("ev_rows"), 1)
                    nc.scalar.activation(vall[:, 2 - 2 * w + t, :], src[:, 128:256], ACT.Copy).then_inc(sem("ev_rows"), 1)
            act.wait_ge(sem("inverses"), 1)
            nc.scalar.activation(sm[:, 24:48], sm[:, 24:48], ACT.Sqrt).then_inc(sem("roots"), 1)
            whole(act, "ev_gate")
            for j in range(2):
                nc.scalar.activation(flat(sg[:, 2 * j:2 * j + 2, :]), pb(6 + j), ACT.Sigmoid).then_inc(sem("cv_gate"), 1)
            act.wait_ge(sem("ev_qkT_ps"), 1)
            for b in range(2):
                nc.scalar.activation(flat(qT[:, 2 * b:2 * b + 2, :]), pb(b), ACT.Copy).then_inc(sem("ev_qT"), 1)

            def ev_probs_T(m):
                act.wait_ge(sem("ev_pT_ps"), m + 1)
                if m >= 2:
                    act.wait_ge(sem("ev_pv"), m - 1)
                nc.scalar.activation(flat(pT[:, 1]), pb(5), ACT.Copy).then_inc(sem("ev_pT_act"), 1)

            for n in range(NT * NQ):
                act.wait_ge(sem("ev_max"), n + 1)
                if n >= 2:
                    act.wait_ge(sem("ev_pT_ps"), n - 1)
                nc.scalar.activation(pexp[:, n % 2, :], pb(n % 3), ACT.Exp, bias=sm[:, 64 + n:65 + n],
                                     accum_out=sm[:, 96 + n:97 + n]).then_inc(sem("ev_p"), 1)
                if n % 2 == 0 and n >= 2:
                    ev_probs_T(n - 1)
                if n == LN_AT:
                    act.wait_ge(sem("cv_centered"), 1)
                    nc.scalar.activation(flat(csq), flat(cacc), ACT.Square).then_inc(sem("cv_sq"), 1)
                if n == LN_AT + 1:
                    act.wait_ge(sem("inverses"), 2)
                    nc.scalar.activation(lnrow[:, :], lnrow[:, :], ACT.Sqrt).then_inc(sem("roots"), 1)
            ev_probs_T(NT * NQ - 1)
            def ev_high(j, p):
                n, w, lo, hi = ev_half(j, p)
                arrived(act, FIRST["ev_out"] + j)
                if j and p == 0:
                    act.wait_ge(sem("half_used"), 1)
                elif j:
                    whole(act, "ev_out", 0)
                nc.scalar.activation(hi, w, ACT.Copy).then_inc(sem("w_high"), 1)

            ev_high(0, 0)
            act.wait_ge(sem("cv_norm"), 1)
            for c in range(CT):
                nc.scalar.activation(cacc[:, c, :], cacc[:, c, :], ACT.Silu, scale=cw[:, c, 32:33],
                                     bias=cw[:, c, 33:34]).then_inc(sem("cv_out"), 1)
            for b in range(2):
                c = slice(2 * b, 2 * b + 2)
                act.wait_ge(sem("cv_out"), 2 * b + 2)
                nc.scalar.activation(ev_x[0][0][:, c, :], cacc[:, c, :], ACT.Copy).then_inc(sem("x_high"), 1)
            for b in range(2):
                act.wait_ge(sem("ev_aT_ps"), b + 1)
                nc.scalar.activation(flat(ev_x[1][0][:, 2 * b:2 * b + 2, :]), pb(4 + b), ACT.Copy).then_inc(sem("x_high"), 1)
            act.wait_ge(sem("ev_pv"), NT * NQ)
            ev_high(0, 1)
            ev_high(1, 0)
            ev_high(1, 1)

            def route(l):
                name = f"moe{l}"
                squares(name, h, xT_rows, "h_ready", 4 * l + 3)
                transposed(name, xT)
                act.wait_ge(sem("mo_max"), l + 1)
                for t in range(NT):
                    nc.scalar.activation(aff[:, t, :], ps[:, 0, E * t:E * t + E], ACT.Exp, bias=sm[:, 130 + t:131 + t],
                                         accum_out=sm[:, 132 + t:133 + t]).then_inc(sem("mo_exp"), 1)

            def experts(loop):
                l, g0, g1, base = loop
                scale, shift = affine(f"moe{l}")
                with act.Fori(g0, g1) as g:
                    n = g + GROUPS * l
                    act.wait_ge(sem("mo_gather"), 2 * n + 2)
                    for k in range(4, KD):
                        last = nc.scalar.activation(xsT[:, k, :], ps[:, 7, P * (k - 4):P * (k - 3)], ACT.Identity,
                                                    scale=scale[:, k:k + 1], bias=shift[:, k:k + 1])
                    last.then_inc(sem("mo_xsT_act"), 1)
                    act.wait_ge(sem("mo_bc"), n + 1)
                    nc.scalar.activation(aff_bc, ps[:, 4, N:2 * N], ACT.Copy).then_inc(sem("mo_affbc"), 1)
                    act.wait_ge(sem("chunks_used"), PER_GROUP * g + (base + KD))
                    act.wait_ge(sem("mo_hT_ps"), 2 * n + 1)
                    nc.scalar.activation(hid, ps[:, 0:2, :].rearrange("p b f -> p (b f)"), ACT.Silu)\
                        .then_inc(sem("mo_silu"), 1)
                    act.wait_ge(sem("mo_hT_ps"), 2 * n + 3)
                    if g0:
                        act.wait_ge(sem("mem_out"), 16)
                    nc.scalar.activation(flat(hT[:, 4:8, :]), pb(7), ACT.Copy).then_inc(sem("mo_hT_act"), 1)

            route(0)
            experts(LOOPS[0])
            act.wait_ge(sem("mem_in"), 32)
            act.wait_ge(sem("mo_h"), 4 * 2 + 1)
            squares("mem", mem_rows, xk)
            act.wait_ge(sem("norm_T"), 4 * TRANSPOSED.index("mem") + 4)
            act.wait_ge(sem("norm_ss"), 2 * NORMS.index("mem") + 2)
            transposed("mem", memT)
            for j in range(2):
                whole(act, "wk", j)
                for t in range(NT):
                    for w in range(2):
                        u, done = 4 * j + 2 * t + w, 4 * j + 2 * t + w
                        if done:
                            act.wait_ge(sem("xk_ss"), done)
                        nc.scalar.activation(lnrow[:, :], pb(4 + 2 * j + t)[:, XD * w:XD * (w + 1)], ACT.Square,
                                             accum_out=sm[:, u:u + 1]).then_inc(sem("xk_ss"), 1)
            for b in (1, 3):
                act.wait_ge(sem("cols_ps"), b + 1)
                nc.scalar.activation(flat(memkT[:, 2 * b:2 * b + 2, :]), pb(4 + b), ACT.Copy).then_inc(sem("cols"), 1)
            experts(LOOPS[1])
            u = NORMS.index("mem")
            act.wait_ge(sem("norm_rstd"), 2 * u + 2)
            whole(act, "wv", 1)
            for j in range(2):
                for t in range(NT):
                    nc.scalar.activation(memv[:, t, 512 * j:512 * j + 512], pb(2 * j + t), ACT.Copy, scale=rstd[:, u, t:t + 1]).then_inc(sem("xkv"), 1)
            experts(LOOPS[2])

            def sc_high(m, half):
                n, w, lo, hi = list(sc_halves(m))[half]
                arrived(act, FIRST["sc_in"] + m)
                if m and half == 0:
                    act.wait_ge(sem("half_used"), m + 2)
                elif m:
                    whole(act, "sc_in", m - 1)
                nc.scalar.activation(hi, w, ACT.Copy).then_inc(sem("w_high"), 1)

            def sc_gate(j):
                whole(act, "sc_in", 3 * j)
                for b in range(2):
                    c = 4 * j + 2 * b
                    last = nc.scalar.activation(flat(cS[:, c:c + 2, :]), pb(6 * j + b), ACT.Copy)
                last.then_inc(sem("sc_c"), 1)

            def y_high(j):
                act.wait_ge(sem("sc_y"), j + 1)
                for c in (4 * j, 4 * j + 2):
                    nc.scalar.activation(y_hi[:, c:c + 2, :], yS[:, c:c + 2, :], ACT.Copy).then_inc(sem("x_high"), 1)

            sc_high(0, 0)
            act.wait_ge(sem("mem_out"), 32)
            squares("mix1", h, xT_rows, "mo_h", 4 * GROUPS - 1, 2)
            transposed("mix1", xT)
            act.wait_ge(sem("xT_ready"), 4 * TRANSPOSED.index("mix1") + 4)
            for c in range(0, KD, 2):
                nc.scalar.activation(sc_hi[:, c:c + 2, :], xT[:, c:c + 2, :], ACT.Copy).then_inc(sem("x_high"), 1)
            sc_high(0, 1)
            sc_high(1, 0)
            sc_gate(0)
            sc_high(1, 1)
            for m in (2, 3):
                sc_high(m, 0)
                sc_high(m, 1)
            y_high(0)
            sc_high(4, 0)
            sc_gate(1)
            sc_high(4, 1)
            for m in (5, 6):
                sc_high(m, 0)
                sc_high(m, 1)
            y_high(1)
            sc_high(7, 0)
            sc_high(7, 1)

            route(1)
            experts(LOOPS[3])

            arrived(act, N0)
            act.wait_ge(sem("forget_cols"), 16)
            nc.scalar.activation(small_hi[:, :, 0:8], slot8(N0)[:, :, 0:8], ACT.Copy)
            nc.scalar.activation(small_hi[:, :, 8:24], slot8(N0)[:, :, 32:48], ACT.Copy).then_inc(sem("w_high"), 1)
            high(FIRST["w_gqk"])
            squares("final", h, xT_rows, "mo_h", 8 * GROUPS - 1, 2)
            act.wait_ge(sem("h_final"), 2)
            norm_high("mix2", rows_hi)
            squares("mix2", h, xk, "h_final", 1)
            high(FIRST["w_fq"])
            act.wait_ge(sem("gate_abs"), 1)
            link(nc.scalar.activation(lf2[0:FOXH, :], lf2[0:FOXH, :], ACT.Exp, scale=-1.0))
            nc.scalar.activation(lf2[0:FOXH, :], lf2[0:FOXH, :], ACT.Ln, bias=1.0).then_inc(sem("gate_ln"), 1)
            high(FIRST["w_fk"])
            act.wait_ge(sem("gate_abs"), 2)
            link(nc.scalar.activation(ex[:, 0], ex[:, 0], ACT.Exp, scale=-1.0))
            nc.scalar.activation(ex[:, 0], ex[:, 0], ACT.Ln, bias=1.0).then_inc(sem("gate_ln"), 1)
            act.wait_ge(sem("gl_cum"), 1)
            nc.scalar.activation(ex[:, 0], bcum, ACT.Exp)
            nc.scalar.activation(ex[:, 1], bcum, ACT.Exp, scale=-1.0)
            nc.scalar.activation(sm[:, 200:208].rearrange("p (r c) -> p r c", r=2),
                                 bcum.rearrange("p r (c j) -> p r c j", j=GCH)[:, :, :, GCH - 1], ACT.Exp)\
                .then_inc(sem("gl_exp"), 1)
            act.wait_ge(sem("gl_dec"), 1)
            for r in range(2):
                for c in range(4):
                    s = slice(GCH * c, GCH * (c + 1))
                    last = nc.scalar.activation(ex[:, 0, r, s], bcum[:, r, s], ACT.Exp, scale=-1.0,
                                                bias=bcum[:, r, GCH * (c + 1) - 1:GCH * (c + 1)])
            last.then_inc(sem("gl_exp"), 1)
            act.wait_ge(sem("h_final"), 3)
            for w, name in enumerate(("w_fq", "w_fk")):
                whole(act, name)
                for t in range(NT):
                    nc.scalar.activation(fqk[:, t, 8 * w:8 * w + 8, :], pb(4 + 2 * w + t).rearrange("p (h e) -> p h e", e=HD),
                                         ACT.Copy, scale=row_scale[:, t:t + 1]).then_inc(sem("fqk"), 1)
                high(FIRST[("w_fv", "w_gv")[w]])
            act.wait_ge(sem("inverses"), 3)
            nc.scalar.activation(sm[:, 32:64], sm[:, 32:64], ACT.Sqrt).then_inc(sem("roots"), 1)
            for name, dst, bank, ahead in (("w_fv", fv, 0, FIRST["w_gr"]), ("w_gv", gv, 2, FIRST["w_out"])):
                whole(act, name)
                for t in range(NT):
                    nc.scalar.activation(dst[:, t, :], pb(bank + t), ACT.Copy, scale=row_scale[:, t:t + 1]).then_inc(sem("values"), 1)
                high(ahead)
            whole(act, "w_gr")
            for t in range(NT):
                nc.scalar.activation(gr[:, t, :], pb(6 + t), ACT.Silu, scale=row_scale[:, t:t + 1]).then_inc(sem("values"), 1)
            for w in range(2):
                act.wait_ge(sem("cols_ps"), 4 + 2 * w + 2)
                nc.scalar.activation(flat(fT[:, w, 2:4, :]), pb(1 + 2 * w), ACT.Copy).then_inc(sem("cols"), 1)
            high(FIRST["w_out"] + 1)
            act.wait_ge(sem("go_sb"), 1)
            for t in range(NT):
                for hd in range(GLAH):
                    s = slice(GDV * hd, GDV * (hd + 1))
                    last = nc.scalar.activation(gsq[:, t, s], go[:, t, s], ACT.Square,
                                                accum_out=sm[:, 152 + 4 * t + hd:153 + 4 * t + hd])
            last.then_inc(sem("head_ss"), 1)

            def fox_probs_T(m):
                mk = P * (m // FOXH + 1)
                act.wait_ge(sem("fx_pT_ps"), m + 1)
                if m >= 2:
                    act.wait_ge(sem("fx_pv"), m - 1)
                nc.scalar.activation(fpT[:, 1, 0:mk], ps[:, FTB[1], 0:mk], ACT.Copy).then_inc(sem("fx_pT_act"), 1)

            for n in range(NT * FOXH):
                nk = P * (n // FOXH + 1)
                act.wait_ge(sem("fx_max"), n + 1)
                nc.scalar.activation(fp[:, n % 2, 0:nk], fp[:, n % 2, 0:nk], ACT.Exp, bias=sm[:, 64 + n:65 + n],
                                     accum_out=sm[:, 96 + n:97 + n]).then_inc(sem("fx_p"), 1)
                if n % 2 == 0 and n >= 2:
                    fox_probs_T(n - 1)
                if n == GLA_AT:
                    columns_high(8, WO[0], gla_x[0])
            fox_probs_T(NT * FOXH - 1)
            columns_high(10, FTB, x_hi)

            high(FIRST["wq"])
            norm_high("xattn", x_hi)
            squares("xattn", h, rows, "h_ready", 11)
            high(FIRST["wq"] + 1)
            def xq_rows(j):
                whole(act, "wq", j)
                for t in range(NT):
                    nc.scalar.activation(xq[:, t, 512 * j:512 * j + 512], pb(2 * j + t), ACT.Copy).then_inc(sem("xq"), 1)
                act.wait_ge(sem("norm_ss"), 2 * NORMS.index("xattn") + 2)
                for t in range(NT):
                    for hd in range(2 * j, 2 * j + 2):
                        e, u = slice(XD * hd, XD * (hd + 1)), 16 + NT * hd + t
                        last = nc.scalar.activation(rows[:, t, e], pb(2 * j + t)[:, XD * (hd % 2):XD * (hd % 2 + 1)], ACT.Square,
                                                    accum_out=sm[:, u:u + 1])
                last.then_inc(sem("head_ss"), 1)

            def xq_columns(b):
                act.wait_ge(sem("cols_ps"), 12 + b + 1)
                for k in range(2):
                    last = nc.scalar.activation(xqT[:, 2 * b + k, :], pb(XQT[b])[:, N * k:N * (k + 1)], ACT.Identity,
                                                scale=xqg[:, k:k + 1])
                last.then_inc(sem("cols"), 1)

            def x_probs(n):
                act.wait_ge(sem("xa_max"), n + 1)
                if n >= 2:
                    act.wait_ge(sem("xa_pT_ps"), n - 1)
                nc.scalar.activation(xp[:, n % 2, :], ps[:, n % 2, 0:N], ACT.Exp, bias=sm[:, 64 + n:65 + n],
                                     scale=sm[:, 48 + n:49 + n], accum_out=sm[:, 96 + n:97 + n]).then_inc(sem("xa_p"), 1)

            xq_rows(0)
            high(FIRST["wo"])
            xq_columns(1)
            for n in range(4):
                x_probs(n)
            xq_rows(1)
            xq_columns(3)
            x_probs(4)
            columns_high(16, (4, 5), x_hi)
            x_probs(5)
            high(FIRST["wo"] + 1, (0,))
            x_probs(6)
            x_probs(7)
            high(FIRST["wo"] + 1, (1,))
            columns_high(18, (2, 3), x_hi[:, 4:8])

            high(mlp("up", 0))
            norm_high("mlp", x_hi)
            squares("mlp", h, rows, "h_ready", 15)
            high(mlp("up", 1))
            for j in range(8):
                used_up(act, mlp("up", j))
                if j >= 2:
                    used_up(act, mlp("down", j - 2))
                for b in range(2):
                    last = nc.scalar.activation(flat(uT[:, j % 2, 2 * b:2 * b + 2, :]), pb(4 + 2 * (j % 2) + b), ACT.Relu)
                last.then_inc(sem("mlp_relu"), 1)
                high(mlp("down", j), (0,))
                act.wait_ge(sem("mlp_u"), j + 1)
                nc.scalar.activation(uT_hi[:, j % 2], uT[:, j % 2], ACT.Copy).then_inc(sem("mlp_u_high"), 1)
                high(mlp("down", j), (1,))
                if j + 2 < 8:
                    high(mlp("up", j + 2))

        @block.gpsimd
        def _(pool):
            link = Steps(pool, "pool_steps")
            nc.gpsimd.memset(sil[:, :, :], 0.0).then_inc(sem("cleared"), 1)
            nc.gpsimd.memset(ada_b, 0.0).then_inc(sem("cleared"), 1)
            link(nc.gpsimd.memset(mhalf[:, :], -0.5))
            nc.gpsimd.memset(ones[:, :], 1.0).then_inc(sem("cleared"), 1)
            def store_gate(g):
                pool.wait_ge(sem("ada_rows"), g + 1)
                l, s = g // 3, g % 3 - 1
                for j in range(2):
                    r = 32 * (2 * s + j)
                    pool.dma_start(gate_dram[l, s:s + 1, 512 * j:512 * (j + 1)], flat(mrow[r:r + 1, g % 3]))\
                        .then_inc(sem(f"gate{g}_out"), 16)

            def load_gate(l, s):
                pool.wait_ge(sem(f"gate{3 * l + s + 1}_out"), 2 * 16)
                pool.dma_start(gate_bc[:, 0:D], gate_dram[l, s].partition_broadcast(P)).then_inc(sem("gate_in"), 16)

            def rms(name):
                u = NORMS.index(name)
                for t in range(NT):
                    c = slice(t, t + 1)
                    pool.wait_ge(sem("norm_ss"), 2 * u + t + 1)
                    link(nc.gpsimd.tensor_scalar(ms[:, u, c], ss[:, u, c], 1.0 / D, EPS, ALU.mult, ALU.add))
                    nc.gpsimd.tensor_tensor(rstd[:, u, c], ms[:, u, c], mhalf[:, c], ALU.pow).then_inc(sem("norm_rstd"), 1)

            rms("x")
            rms("ctx")
            store_gate(1)
            load_gate(0, 0)
            pool.wait_ge(sem("cw"), 1)
            pool.wait_ge(sem("gpad"), 2)
            c = CT - 1
            for k in range(CONVK - POOL_TAPS, CONVK):
                dst = cpool if k == CONVK - POOL_TAPS else lnrow[:, :]
                link(nc.gpsimd.tensor_scalar(dst, gpad[:, c, k:k + N], cw[:, c, k:k + 1], None, ALU.mult))
                if k > CONVK - POOL_TAPS:
                    last = nc.gpsimd.tensor_tensor(cpool, cpool, lnrow[:, :], ALU.add)
                    if k < CONVK - 1:
                        link(last)
            last.then_inc(sem("conv_last"), 1)
            for g in (2, 4, 5):
                store_gate(g)
            rms("moe0")
            pool.wait_ge(sem("gate_used"), 4)
            for g in (4, 5):
                pool.wait_ge(sem(f"gate{g}_out"), 2 * 16)
            load_gate(0, 1)
            pool.dma_start(xkg, a["xattn_k_norm_g_2"].partition_broadcast(P)).then_inc(sem("mem_in"), 16)
            pool.wait_ge(sem("mo_logits"), 1)
            pool.dma_start(mem_rows, a["mem_2"][0].rearrange("(t p) d -> p t d", p=P)).then_inc(sem("mem_in"), 16)
            rms("mem")
            u = NORMS.index("mem")
            pool.wait_ge(sem("norm_rstd"), 2 * u + 2)
            link(nc.gpsimd.tensor_scalar(ms[:, u, :], ms[:, u, :], XD * EPS, None, ALU.mult))
            for j in range(2):
                v = sm[:, 4 * j:4 * j + 4].rearrange("p (t w) -> p t w", t=NT)
                pool.wait_ge(sem("xk_ss"), 4 * j + 4)
                link(nc.gpsimd.tensor_tensor(v, v, ms[:, u, :].unsqueeze(2).broadcast_to([P, NT, 2]), ALU.add))
                link(nc.gpsimd.tensor_scalar(sm[:, 4 * j:4 * j + 4], sm[:, 4 * j:4 * j + 4], 1.0 / XD, None, ALU.mult))
                nc.gpsimd.tensor_tensor(sm[:, 32 + 4 * j:36 + 4 * j], sm[:, 4 * j:4 * j + 4], mhalf[:, 0:1].broadcast_to([P, 4]),
                                        ALU.pow).then_inc(sem("head_rstd"), 1)
            pool.wait_ge(sem("cols"), 4)
            pool.dma_start(memk_dram.rearrange("p (k n) -> p k n", k=KD), memkT).then_inc(sem("mem_out"), 16)
            pool.wait_ge(sem("xkv"), 4)
            pool.wait_ge(sem("mem_out"), 16)
            pool.dma_start(memv_dram.rearrange("p (t d) -> p t d", t=NT), memv).then_inc(sem("mem_out"), 16)
            rms("mix1")
            n, w, lo, hi = list(sc_halves(0))[0]
            pool.wait_ge(sem("w_high"), n + 1)
            nc.gpsimd.tensor_tensor(lo, w, hi.bitcast(F32), ALU.subtract).then_inc(sem("w_split"), 1)
            load_gate(1, 0)
            rms("moe1")
            pool.wait_ge(sem("gate_used"), 8)
            load_gate(1, 1)
            pool.wait_ge(sem("mo_lists"), 3)
            pool.dma_start(final_bc, a["final_g"].partition_broadcast(P)).then_inc(sem("final_in"), 16)
            pool.wait_ge(sem("mo_ym"), 4 * GROUPS)
            for n, o, w in (("fox_q_norm_g_2", 0, 64), ("fox_k_norm_g_2", 64, 64), ("gla_out_norm_g_2", 128, 512)):
                pool.dma_start(gate_bc[:, o:o + w], a[n].partition_broadcast(P)).then_inc(sem("small2_in"), 16)
            pool.dma_start(sm[0:FOXH, 140:141], a["fox_b_f_2"].unsqueeze(1)).then_inc(sem("small2_in"), 16)
            for r in range(2):
                pool.dma_start(sm[:, 141 + r:142 + r], a["gla_b_gate_2"][P * r:P * (r + 1)].unsqueeze(1))\
                    .then_inc(sem("small2_in"), 16)
                pool.dma_start(xqg[:, r:r + 1], a["xattn_q_norm_g_2"][P * r:P * (r + 1)].unsqueeze(1))\
                    .then_inc(sem("small2_in"), 16)
            rms("final")
            pool.dma_start(gate2, a["gla_w_gate2_2"]).then_inc(sem("small2_in"), 16)
            rms("mix2")
            pool.wait_ge(sem("norm_rstd"), 2 * NORMS.index("mix2") + 2)
            nc.gpsimd.tensor_tensor(row_scale, rstd[:, NORMS.index("final"), :], rstd[:, NORMS.index("mix2"), :], ALU.mult)\
                .then_inc(sem("h_final"), 1)
            pool.wait_ge(sem("mem_out"), 32)
            low(pool, nc.gpsimd, FIRST["w_out"])
            pool.wait_ge(sem("small2_in"), SMALL2 * 16)
            pool.wait_ge(sem("values"), 6)
            link(nc.gpsimd.tensor_tensor(gr, gr, glag.unsqueeze(1).broadcast_to([P, NT, 512]), ALU.mult))
            mask = cst[:, C_FOX:C_FOX + P].unsqueeze(1).broadcast_to([P, FOXH, P])
            pool.wait_ge(sem("params_in"), PARAMS * 16)
            pool.wait_ge(sem("nb"), 4)
            nc.gpsimd.tensor_tensor(NB0, NB[:, :, 0:P].rearrange("p (t h) n -> p t h n", t=NT), mask.rearrange("p (t h) n -> p t h n", t=NT), ALU.add).then_inc(sem("nb"), 1)
            nc.gpsimd.tensor_tensor(NB[:, :, P:N], NB[:, :, P:N], mask, ALU.add).then_inc(sem("nb"), 1)
            pool.wait_ge(sem("go_sb"), 1)
            pool.wait_ge(sem("head_ss"), 1)
            link(nc.gpsimd.tensor_scalar(sm[:, 152:160], sm[:, 152:160], 1.0 / GDV, EPS, ALU.mult, ALU.add))
            link.mark(nc.gpsimd.tensor_tensor(go, go, gr, ALU.mult))
            link(nc.gpsimd.tensor_tensor(sm[:, 160:168], sm[:, 152:160], mhalf[:, 0:1].broadcast_to([P, 8]), ALU.pow))
            nc.gpsimd.tensor_tensor(rows[:, :, 512:1024].rearrange("p t (h v) -> p t h v", v=GDV),
                                    go.rearrange("p t (h v) -> p t h v", v=GDV),
                                    sm[:, 160:168].rearrange("p (t h) -> p t h", t=NT).unsqueeze(3)
                                    .broadcast_to([P, NT, GLAH, GDV]), ALU.mult).then_inc(sem("mix_rows"), 1)
            low(pool, nc.gpsimd, FIRST["w_out"] + 1)
            pool.wait_ge(sem("x_split"), 4 * SPLIT_INPUTS.index("w_out") + 4)
            pool.dma_start(xkT, memk_dram.rearrange("p (k n) -> p k n", k=KD)).then_inc(sem("memkv_in"), 16)
            pool.dma_start(xv, memv_dram.rearrange("p (t d) -> p t d", t=NT)).then_inc(sem("memkv_in"), 16)
            low(pool, nc.gpsimd, FIRST["wq"])
            u = NORMS.index("xattn")
            pool.wait_ge(sem("norm_ss"), 2 * u + 2)
            nc.gpsimd.tensor_scalar(ms[:, u, :], ss[:, u, :], XD * EPS / D, XD * EPS * EPS, ALU.mult, ALU.add)\
                .then_inc(sem("norm_rstd"), 2)
            pool.wait_ge(sem("norm_rstd"), 2 * u + 2)
            for j in range(2):
                c0, c1 = slice(16 + 4 * j, 20 + 4 * j), slice(48 + 4 * j, 52 + 4 * j)
                pool.wait_ge(sem("head_ss"), 2 + j)
                v = sm[:, c0].rearrange("p (h t) -> p h t", t=NT)
                link(nc.gpsimd.tensor_tensor(v, v, ms[:, u, :].unsqueeze(1).broadcast_to([P, 2, NT]), ALU.add))
                nc.gpsimd.tensor_tensor(sm[:, c1], sm[:, c0], mhalf[:, 0:1].broadcast_to([P, 4]), ALU.pow)\
                    .then_inc(sem("head_rstd"), 1)
                low(pool, nc.gpsimd, FIRST["wo"] + j)
            low(pool, nc.gpsimd, mlp("up", 0))
            rms("mlp")

        @block.vector
        def _(dve):
            link = Steps(dve, "dve_steps")

            def normed(name, src, dst):
                u = NORMS.index(name)
                for t in range(NT):
                    dve.wait_ge(sem("norm_rstd"), 2 * u + t + 1)
                    nc.vector.tensor_scalar(dst[:, t, :], src[:, t, :], rstd[:, u, t:t + 1], None, ALU.mult)\
                        .then_inc(sem("norm_rows"), 1)

            def transposed(name, dst):
                v, bank, (scale, shift) = TRANSPOSED.index(name), NORM_BANKS[name], affine(name)
                if name in MODS:
                    dve.wait_ge(sem("mod_cols"), MODS[name])
                for b in (0, 2):
                    dve.wait_ge(sem("norm_T"), 4 * v + b + 1)
                    for k in (2 * b, 2 * b + 1):
                        src = ps[:, bank[b], 256 * (k % 2):256 * (k % 2) + 256]
                        if shift is None:
                            last = nc.vector.tensor_scalar(dst[:, k, :], src, scale[:, k:k + 1], None, ALU.mult)
                        else:
                            last = nc.vector.tensor_scalar(dst[:, k, :], src, scale[:, k:k + 1], shift[:, k:k + 1],
                                                           ALU.mult, ALU.add)
                    last.then_inc(sem("xT_ready"), 1)

            def norm_low(name, hi):
                v, bank, scale = TRANSPOSED.index(name), NORM_BANKS[name], affine(name)[0]
                for b in range(4):
                    dve.wait_ge(sem("x_high"), 4 * SPLIT_INPUTS.index(name) + b + 1)
                    for k in (2 * b, 2 * b + 1):
                        last = nc.vector.scalar_tensor_tensor(xT_r[:, k, :], ps[:, bank[b], 256 * (k % 2):256 * (k % 2) + 256],
                                                              scale[:, k:k + 1], hi[:, k, :].bitcast(F32),
                                                              ALU.mult, ALU.subtract)
                    last.then_inc(sem("x_split"), 1)

            def columns_low(name, first, banks, lo, hi):
                for b, bank in enumerate(banks):
                    dve.wait_ge(sem("x_high"), 4 * SPLIT_INPUTS.index(name) + first + b + 1)
                    nc.vector.tensor_tensor(flat(lo[:, 2 * b:2 * b + 2, :]), pb(bank), flat(hi[:, 2 * b:2 * b + 2, :]).bitcast(F32),
                                            ALU.subtract).then_inc(sem("x_split"), 1)

            def ada_rows(g, bank):
                used_up(dve, ada_chunk(g, 3))
                if g == 3:
                    dve.wait_ge(sem("mod_T"), 1)
                if g > 3:
                    dve.wait_ge(sem(f"gate{g - 3}_out"), 2 * 16)
                nc.vector.tensor_copy(flat(mrow[:, g % 3]), pb(bank)).then_inc(sem("ada_rows"), 1)

            def mod_cols(g, bank):
                dve.wait_ge(sem("mod_T"), g + 1)
                v = pb(bank).rearrange("p (b s j c) -> p s j b c", b=4, s=2, c=32)

                def k_order(x):
                    return x.rearrange("p (j b) -> p j b", b=4)

                def shift(name, s, cond=0):
                    return nc.vector.tensor_copy(k_order(mcol[:, SHIFT[name], :]), v[:, s, :, :, cond])

                def scale(name, s, gain, cond=0):
                    return nc.vector.scalar_tensor_tensor(k_order(acol[:, SCALE[name], :]), v[:, s, :, :, cond], 1.0,
                                                          k_order(gcol[:, gain, :]), ALU.add, ALU.mult)
                if g == 0:
                    shift("ctx", 0, 1)
                    scale("ctx", 1, 0, 1)
                if g % 3 == 0:
                    shift(("x", "mix1")[g // 3], 0)
                    last = scale(("x", "mix1")[g // 3], 1, g // 3)
                elif g % 3 == 1:
                    last = shift(("moe0", "moe1")[g // 3], 1)
                else:
                    last = scale(("moe0", "moe1")[g // 3], 0, 2 + g // 3)
                last.then_inc(sem("mod_cols"), 1)

            def tile_whole(n, name, j, t):
                if j == 1 and t == 0:
                    dve.wait_ge(sem("tile_0_whole"), n + 1)
                else:
                    whole(dve, name, j)

            def add_gated(n, name, banks, rows=rows):
                for j in range(2):
                    s = slice(512 * j, 512 * j + 512)
                    for t in range(NT):
                        tile_whole(n, name, j, t)
                        nc.vector.tensor_tensor(rows[:, t, s], pb(banks[2 * j + t]), gate_bc[:, s], ALU.mult)\
                            .then_inc(sem("gate_used"), 1)
                        dve.wait_ge(sem("gate_used"), 4 * n + 2 * j + t + 1)
                        nc.vector.tensor_tensor(h[:, t, s], h[:, t, s], rows[:, t, s], ALU.add).then_inc(sem("h_ready"), 1)

            def add_plain(n, name, banks):
                for j in range(2):
                    for t in range(NT):
                        s = slice(512 * j, 512 * j + 512)
                        tile_whole(n, name, j, t)
                        nc.vector.tensor_tensor(h[:, t, s], h[:, t, s], pb(banks[2 * j + t]), ALU.add)\
                            .then_inc(sem("h_ready"), 1)

            dve.wait_ge(sem("gains_ps"), 1)
            nc.vector.tensor_copy(flat(gcol[:, :, :]), ps[:, 1, 0:GAINS]).then_inc(sem("gain_cols"), 1)
            normed("x", h, rows)
            normed("ctx", ctx_rows, ctx_rows)
            ada_rows(0, 0)
            dve.wait_ge(sem("gain_cols"), 1)
            mod_cols(0, 0)
            transposed("x", xT)
            transposed("ctx", cT)
            dve.wait_ge(sem("cw_ps"), 1)
            nc.vector.tensor_copy(flat(cw), ps[:, 4, 0:CT * 34]).then_inc(sem("cw"), 1)
            dve.wait_ge(sem("params_in"), PARAMS * 16)
            link.mark(nc.vector.tensor_scalar(qkg[:, 0, :], qkg[:, 0, :], float(HD) ** -0.5, None, ALU.mult))
            edge = CONVK // 2
            link.mark(nc.vector.memset(gpad[:, :, 0:edge], 0.0))
            link(nc.vector.memset(gpad[:, :, edge + N:PADW], 0.0))
            dve.wait_ge(sem("ev_rows"), 10)
            link(nc.vector.tensor_tensor(sq, qk, qk, ALU.mult))
            link(nc.vector.tensor_reduce(sm[:, 0:24].rearrange("p (t h) -> p t h", t=NT), sq, AX.X, ALU.add))
            link(nc.vector.tensor_scalar(sm[:, 0:24], sm[:, 0:24], 1.0 / HD, EPS, ALU.mult, ALU.add))
            nc.vector.reciprocal(sm[:, 24:48], sm[:, 0:24]).then_inc(sem("inverses"), 1)
            dve.wait_ge(sem("roots"), 1)
            hr = sm[:, 24:48].rearrange("p (t h) -> p t h", t=NT).unsqueeze(3).broadcast_to([P, NT, 12, HD])
            link(nc.vector.tensor_tensor(qk, qk, hr, ALU.mult))
            for t in range(NT):
                link.mark(nc.vector.tensor_tensor(qk[:, t, 0:8, :], qk[:, t, 0:8, :],
                                                  qkg[:, 0:1, :].broadcast_to([P, 8, HD]), ALU.mult))
                link.mark(nc.vector.tensor_tensor(qk[:, t, 8:12, :], qk[:, t, 8:12, :],
                                                  qkg[:, 1:2, :].broadcast_to([P, 4, HD]), ALU.mult))
            link.wait()
            for t in range(NT):
                cos = cst[:, C_COS + 32 * t:C_COS + 32 * t + 32].unsqueeze(1).broadcast_to([P, 10, 32])
                sin = cst[:, C_SIN + 32 * t:C_SIN + 32 * t + 32].unsqueeze(1).broadcast_to([P, 10, 32])
                x1, x2 = qk[:, t, 0:10, 0:32], qk[:, t, 0:10, 32:64]
                link.mark(nc.vector.tensor_tensor(ra[:, t], x1, cos, ALU.mult))
                link.mark(nc.vector.tensor_tensor(rb[:, t], x2, sin, ALU.mult))
                link.mark(nc.vector.tensor_tensor(rc[:, t], x2, cos, ALU.mult))
                link(nc.vector.tensor_tensor(rd[:, t], x1, sin, ALU.mult))
                nc.vector.tensor_tensor(x1, ra[:, t], rb[:, t], ALU.subtract).then_inc(sem("ev_rope"), 1)
                nc.vector.tensor_tensor(x2, rc[:, t], rd[:, t], ALU.add).then_inc(sem("ev_rope"), 1)
            whole(dve, "ev_u")
            for j in range(2):
                dve.wait_ge(sem("cv_gate"), j + 1)
                nc.vector.tensor_tensor(gpad[:, 2 * j:2 * j + 2, edge:edge + N],
                                        pb(4 + j).rearrange("p (c n) -> p c n", c=2), sg[:, 2 * j:2 * j + 2, :], ALU.mult)\
                    .then_inc(sem("gpad"), 1)
            ada_rows(1, 3)
            dve.wait_ge(sem("ev_qkT_ps"), 2)
            nc.vector.tensor_copy(kT, pb(2)).then_inc(sem("ev_kT"), 1)
            mod_cols(1, 3)

            taps_left = [(k, c) for k in range(CONVK) for c in range(CT) if c < CT - 1 or k < CONVK - POOL_TAPS]
            TAPS, tap_of = len(taps_left), {}

            def taps(n):
                for _ in range(min(n, len(taps_left))):
                    k, c = taps_left.pop(0)
                    if k:
                        dve.wait_ge(sem("conv"), tap_of[c])
                        ins = nc.vector.scalar_tensor_tensor(cacc[:, c, :], gpad[:, c, k:k + N], cw[:, c, k:k + 1],
                                                             cacc[:, c, :], ALU.mult, ALU.add)
                    else:
                        ins = nc.vector.tensor_scalar(cacc[:, c, :], gpad[:, c, 0:N], cw[:, c, 0:1], cw[:, c, 31:32],
                                                      ALU.mult, ALU.add)
                    ins.then_inc(sem("conv"), 1)
                    tap_of[c] = TAPS - len(taps_left)

            def pool_taps():
                dve.wait_ge(sem("conv_last"), 1)
                dve.wait_ge(sem("conv"), TAPS)
                nc.vector.tensor_tensor(cacc[:, CT - 1, :], cacc[:, CT - 1, :], cpool, ALU.add).then_inc(sem("conv"), 1)

            def attn_rows(t):
                dve.wait_ge(sem("ev_pv"), NQ * (t + 1))
                link(nc.vector.reciprocal(sm[:, 112 + 8 * t:120 + 8 * t], sm[:, 96 + 8 * t:104 + 8 * t]))
                for w in range(2):
                    nc.vector.tensor_tensor(attn[:, t, 256 * w:256 * w + 256].rearrange("p (i e) -> p i e", e=HD),
                                            pb(6 + t).rearrange("p (i w e) -> p w i e", w=2, e=HD)[:, w],
                                            sm[:, 112 + 8 * t:120 + 8 * t].rearrange("p (i w) -> p w i", w=2)[:, w]
                                            .unsqueeze(2).broadcast_to([P, 4, HD]), ALU.mult)\
                        .then_inc(sem("ev_attn"), 1)

            mu = lnrow[:, :].unsqueeze(1).broadcast_to([P, CT, N])

            def ln_center():
                dve.wait_ge(sem("cv_sum"), 1)
                link(nc.vector.tensor_scalar(lnrow[:, :], ps[:, 6, 0:N], 1.0 / 512, None, ALU.mult))
                nc.vector.tensor_tensor(cacc, cacc, mu, ALU.subtract).then_inc(sem("cv_centered"), 1)

            def ln_inverse():
                dve.wait_ge(sem("cv_sum"), 2)
                link(nc.vector.tensor_scalar(lnrow[:, :], ps[:, 6, N:2 * N], 1.0 / 512, EPS, ALU.mult, ALU.add))
                nc.vector.reciprocal(lnrow[:, :], lnrow[:, :]).then_inc(sem("inverses"), 1)

            def ln_scale():
                dve.wait_ge(sem("roots"), 2)
                nc.vector.tensor_tensor(cacc, cacc, mu, ALU.mult).then_inc(sem("cv_norm"), 1)

            dve.wait_ge(sem("cw"), 1)
            dve.wait_ge(sem("gpad"), 2)
            for n in range(NT * NQ):
                dve.wait_ge(sem("ev_s"), n + 1)
                nc.vector.tensor_reduce(sm[:, 64 + n:65 + n], pb(n % 3), AX.X, ALU.max, negate=True)\
                    .then_inc(sem("ev_max"), 1)
                if n % 2 == 1:
                    dve.wait_ge(sem("ev_pT_ps"), n)
                    if n >= 3:
                        dve.wait_ge(sem("ev_pv"), n - 2)
                    nc.vector.tensor_copy(flat(pT[:, 0]), pb(4)).then_inc(sem("ev_pT_dve"), 1)
                if n % 4 == 0 and n:
                    ada_rows(1 + n // 4, 3)
                taps(9)
                if n == LN_AT - 1:
                    pool_taps()
                if n % 4 == 0 and n:
                    mod_cols(1 + n // 4, 3)
                if n == NQ + 1:
                    attn_rows(0)
                if n == LN_AT:
                    ln_center()
                if n == LN_AT + 1:
                    ln_inverse()
                if n == LN_AT + 2:
                    ln_scale()
            ada_rows(5, 3)
            attn_rows(1)

            def ev_low(j, p):
                n, w, lo, hi = ev_half(j, p)
                dve.wait_ge(sem("w_high"), n + 1)
                nc.vector.tensor_tensor(lo, w, hi.bitcast(F32), ALU.subtract).then_inc(sem("w_split"), 1)

            ev_low(0, 0)
            for p in range(2):
                for b in range(2):
                    hi, lo = (flat(v[:, 2 * b:2 * b + 2, :]) for v in ev_x[p])
                    dve.wait_ge(sem("x_high"), 2 * p + b + 1)
                    nc.vector.tensor_tensor(lo, pb(4 + b) if p else flat(cacc[:, 2 * b:2 * b + 2, :]), hi.bitcast(F32),
                                            ALU.subtract).then_inc(sem("x_split"), 1)
            ev_low(0, 1)
            mod_cols(5, 3)
            ev_low(1, 0)
            ev_low(1, 1)
            dve.wait_ge(sem("gate_in"), 16)
            add_gated(0, "ev_out", (0, 1, 6, 7), by_token(xT_t[:, :]))

            def route(l):
                name = f"moe{l}"
                dve.wait_ge(sem("h_ready"), 4 * (l + 1))
                normed(name, h, rows)
                transposed(name, xT)
                dve.wait_ge(sem("mo_logits"), l + 1)
                nc.vector.tensor_reduce(sm[:, 130:132], ps[:, 0, 0:NT * E].rearrange("p (t e) -> p t e", t=NT), AX.X,
                                        ALU.max, negate=True).then_inc(sem("mo_max"), 1)
                dve.wait_ge(sem("mo_exp"), 2 * l + 2)
                link(nc.vector.reciprocal(sm[:, 134:136], sm[:, 132:134]))
                nc.vector.tensor_tensor(aff, aff, sm[:, 134:136].unsqueeze(2).broadcast_to([P, NT, E]), ALU.mult)\
                    .then_inc(sem("mo_aff"), 1)
                dve.wait_ge(sem("mo_affT_ps"), l + 1)
                link.mark(nc.vector.tensor_copy(affT[0:E, :], ps[0:E, 1, 0:N]))
                link(nc.vector.tensor_copy(work[0:E, :], ps[0:E, 1, 0:N]))
                for _ in range(CAP // 8):
                    link(nc.vector.max(sm[0:E, 144:152], work[0:E, :]))
                    link(nc.vector.match_replace(work[0:E, :], sm[0:E, 144:152], work[0:E, :], -1.0))
                link(nc.vector.tensor_scalar(smaskE[0:E, :], work[0:E, :], 0.0, None, ALU.is_lt))
                link(nc.vector.tensor_tensor_scan(rank[0:E, :], ones[0:E, :], smaskE[0:E, :], 0.0, ALU.mult, ALU.add))
                nc.vector.tensor_tensor(rank[0:E, :], rank[0:E, :], smaskE[0:E, :], ALU.mult).then_inc(sem("mo_rank"), 1)
                dve.wait_ge(sem("mo_rank"), l + 1)
                dve.wait_ge(sem("mo_rankT_ps"), l + 1)
                dve.wait_ge(sem("gate_in"), 32 * (l + 1))
                link(nc.vector.tensor_copy(flat(rankT), ps[:, 2, 0:NT * E]))
                iota = cst[:, C_IOTA:C_IOTA + CAP].unsqueeze(1).broadcast_to([P, E, CAP])
                for t in range(NT):
                    last = nc.vector.tensor_tensor(onehot[:, t, :].rearrange("p (e c) -> p e c", c=CAP), iota,
                                                   rankT[:, t, :].unsqueeze(2).broadcast_to([P, E, CAP]), ALU.is_equal)
                    if l == t == 0:
                        last.then_inc(sem("mo_h"), 1)
                last.then_inc(sem("mo_lists"), 1)
                grp = cst[0:E, C_GRP:C_GRP + GROUPS].unsqueeze(2).broadcast_to([E, GROUPS, N])
                for v, src in ((0, rank), (1, affT)):
                    ins = nc.vector.tensor_tensor(RA[0:E, :, v, :], src[0:E, :].unsqueeze(1).broadcast_to([E, GROUPS, N]),
                                                  grp, ALU.mult)
                ins.then_inc(sem("mo_lists"), 1)

            def experts(loop):
                l, g0, g1, base = loop
                scale, shift = affine(f"moe{l}")
                with dve.Fori(g0, g1) as g:
                    n = g + GROUPS * l
                    dve.wait_ge(sem("mo_gather"), 2 * n + 1)
                    for k in range(4):
                        last = nc.vector.tensor_scalar(xsT[:, k, :], ps[:, 6, P * k:P * (k + 1)], scale[:, k:k + 1],
                                                       shift[:, k:k + 1], ALU.mult, ALU.add)
                    last.then_inc(sem("mo_xsT_dve"), 1)
                    dve.wait_ge(sem("mo_affbc"), n + 1)
                    dve.wait_ge(sem("mo_comb"), 4 * n + 1)
                    nc.vector.scalar_tensor_tensor(sel_w, ps[:, 4, 0:N], cst[:, C_T:C_T + 1], aff_bc, ALU.is_equal, ALU.mult)\
                        .then_inc(sem("mo_sel"), 1)
                    dve.wait_ge(sem("mo_silu"), n + 1)
                    dve.wait_ge(sem("chunks_used"), PER_GROUP * g + (base + 2 * KD))
                    nc.vector.tensor_tensor(hid, hid, ps[:, 2:4, :].rearrange("p b f -> p (b f)"), ALU.mult)\
                        .then_inc(sem("mo_hid"), 1)
                    dve.wait_ge(sem("mo_hT_ps"), 2 * n + 2)
                    if g0:
                        dve.wait_ge(sem("mem_out"), 16)
                    nc.vector.tensor_copy(flat(hT[:, 0:4, :]), pb(6)).then_inc(sem("mo_hT_dve"), 1)
                    dve.wait_ge(sem("chunks_used"), PER_GROUP * g + (base + 3 * KD))
                    for j in range(2):
                        nc.vector.tensor_tensor(ym[:, 512 * j:512 * j + 512], pb(4 + j), gate_bc[:, 512 * j:512 * j + 512],
                                                ALU.mult).then_inc(sem("mo_ym"), 1)
                    dve.wait_ge(sem("mo_h"), 4 * n + 1)
                    for i in range(4):
                        dve.wait_ge(sem("mo_comb"), 4 * n + i + 2)
                        t, s = i // 2, slice(512 * (i % 2), 512 * (i % 2) + 512)
                        nc.vector.tensor_tensor(h[:, t, s], h[:, t, s], pb((6, 7, 4, 5)[i]), ALU.add).then_inc(sem("mo_h"), 1)
                dve.wait_ge(sem("mo_h"), 4 * (GROUPS * l + g1) + 1)

            route(0)
            experts(LOOPS[0])
            dve.wait_ge(sem("norm_T"), 4 * TRANSPOSED.index("mem") + 4)
            dve.wait_ge(sem("norm_ss"), 2 * NORMS.index("mem") + 2)
            transposed("mem", memT)
            dve.wait_ge(sem("mem_in"), 32)
            for j in range(2):
                dve.wait_ge(sem("head_rstd"), j + 1)
                for t in range(NT):
                    for w in range(2):
                        e, u = slice(XD * (2 * j + w), XD * (2 * j + w + 1)), 32 + 4 * j + 2 * t + w
                        last = nc.vector.scalar_tensor_tensor(xk[:, t, e], pb(4 + 2 * j + t)[:, XD * w:XD * (w + 1)], sm[:, u:u + 1],
                                                              xkg, ALU.mult, ALU.mult)
                last.then_inc(sem("xk_normed"), 1)
            for b in (0, 2):
                dve.wait_ge(sem("cols_ps"), b + 1)
                nc.vector.tensor_copy(flat(memkT[:, 2 * b:2 * b + 2, :]), pb(4 + b)).then_inc(sem("cols"), 1)
            experts(LOOPS[1])
            experts(LOOPS[2])

            def sc_low(m, half):
                n, w, lo, hi = list(sc_halves(m))[half]
                dve.wait_ge(sem("w_high"), n + 1)
                if m == 0:
                    dve.wait_ge(sem("w_split"), n)
                nc.vector.tensor_tensor(lo, w, hi.bitcast(F32), ALU.subtract).then_inc(sem("w_split"), 1)

            def sc_taps(j):
                dve.wait_ge(sem("sc_c"), j + 1)
                whole(dve, "sc_in", 3 * j + 1)
                for b in range(2):
                    c = 4 * j + 2 * b
                    link.mark(nc.vector.tensor_tensor(cx[:, c:c + 2, 1:N + 1],
                                                      pb((2, 0)[j] + b).rearrange("p (c n) -> p c n", c=2),
                                                      cS[:, c:c + 2, :], ALU.mult))
                link.wait()
                for c in range(4 * j, 4 * j + 4):
                    link.mark(nc.vector.tensor_scalar(yS[:, c, :], cx[:, c, 0:N], cw1[:, c, 0:1], None, ALU.mult))
                for k in range(1, SCK):
                    link.wait()
                    for c in range(4 * j, 4 * j + 4):
                        link.mark(nc.vector.scalar_tensor_tensor(yS[:, c, :], cx[:, c, k:k + N], cw1[:, c, k:k + 1],
                                                                 yS[:, c, :], ALU.mult, ALU.add))
                link.wait()

            def y_whole(j):
                whole(dve, "sc_in", 3 * j + 2)
                for b in range(2):
                    c = 4 * j + 2 * b
                    last = nc.vector.tensor_tensor(yS[:, c:c + 2, :], yS[:, c:c + 2, :],
                                                   pb((4, 2)[j] + b).rearrange("p (c n) -> p c n", c=2), ALU.mult)
                last.then_inc(sem("sc_y"), 1)

            def y_low(j):
                for b in range(2):
                    c = 4 * j + 2 * b
                    dve.wait_ge(sem("x_high"), 4 * SPLIT_INPUTS.index("y") + 2 * j + b + 1)
                    nc.vector.tensor_tensor(y_lo[:, c:c + 2, :], yS[:, c:c + 2, :], y_hi[:, c:c + 2, :].bitcast(F32),
                                            ALU.subtract).then_inc(sem("x_split"), 1)

            normed("mix1", h, rows)
            transposed("mix1", xT)
            for b in range(4):
                dve.wait_ge(sem("x_high"), 4 * SPLIT_INPUTS.index("mix1") + b + 1)
                c = slice(2 * b, 2 * b + 2)
                nc.vector.tensor_tensor(xT_r[:, c, :], xT[:, c, :], sc_hi[:, c, :].bitcast(F32), ALU.subtract)\
                    .then_inc(sem("x_split"), 1)
            sc_low(0, 1)
            link.mark(nc.vector.memset(cx[:, :, 0:1], 0.0))
            link(nc.vector.memset(cx[:, :, N + 1:N + 2], 0.0))
            for m in (1, 2):
                sc_low(m, 0)
                sc_low(m, 1)
            sc_taps(0)
            sc_low(3, 0)
            sc_low(3, 1)
            y_whole(0)
            y_low(0)
            for m in (4, 5):
                sc_low(m, 0)
                sc_low(m, 1)
            sc_taps(1)
            sc_low(6, 0)
            y_whole(1)
            sc_low(6, 1)
            y_low(1)
            sc_low(7, 0)
            sc_low(7, 1)
            dve.wait_ge(sem("gate_in"), 48)
            add_gated(1, "sc_out", (4, 5, 6, 7), by_token(xT_t[:, :]))

            route(1)
            experts(LOOPS[3])

            dve.wait_ge(sem("final_in"), 16)
            u = NORMS.index("final")
            for t in range(NT):
                nc.vector.tensor_tensor(rows[:, t, :], h[:, t, :], final_bc, ALU.mult).then_inc(sem("norm_rows"), 1)
            for t in range(NT):
                dve.wait_ge(sem("norm_rstd"), 2 * u + t + 1)
                dve.wait_ge(sem("norm_rows"), 2 * NORMED.index("final") + t + 1)
                nc.vector.tensor_scalar(h[:, t, :], rows[:, t, :], rstd[:, u, t:t + 1], None, ALU.mult).then_inc(sem("h_final"), 1)
            dve.wait_ge(sem("w_high"), SC_SPLITS + 1)
            for c, m, c0 in ((0, 8, 0), (8, 16, 32)):
                last = nc.vector.tensor_tensor(ring_r[slot_of(N0)].rearrange("p (k n) -> p k n", k=KD)[:, :, c0:c0 + m],
                                               slot8(N0)[:, :, c0:c0 + m], small_hi[:, :, c:c + m].bitcast(F32), ALU.subtract)
            last.then_inc(sem("w_split"), 1)
            norm_low("mix2", rows_hi)
            low(dve, nc.vector, FIRST["w_gqk"])
            low(dve, nc.vector, FIRST["w_fq"])
            dve.wait_ge(sem("small2_in"), SMALL2 * 16)
            whole(dve, "w_small")
            dve.wait_ge(sem("scale_ps"), 1)
            link(nc.vector.tensor_copy(scale_bc, ps[:, 3, 0:N]))
            nc.vector.tensor_tensor(glrT[0:16, :], ps[0:16, 0, N:2 * N], scale_bc[0:16, :], ALU.mult).then_inc(sem("glr"), 1)
            lfr, lf2r = lf[0:FOXH, :], lf2[0:FOXH, :]
            link(nc.vector.tensor_tensor(lfr, ps[0:FOXH, 0, 0:N], scale_bc[0:FOXH, :], ALU.mult))
            link(nc.vector.tensor_scalar(lfr, lfr, sm[0:FOXH, 140:141], None, ALU.add))
            nc.vector.scalar_tensor_tensor(lf2r, lfr, -1.0, lfr, ALU.mult, ALU.max).then_inc(sem("gate_abs"), 1)
            dve.wait_ge(sem("gl_ps"), 1)
            for r in range(2):
                link.mark(nc.vector.tensor_scalar(glog[:, r, :], ps[:, 3, N * r:N * (r + 1)], sm[:, 141 + r:142 + r], None,
                                                  ALU.add))
            link.wait()
            nc.vector.scalar_tensor_tensor(flat(ex[:, 0]), flat(glog), -1.0, flat(glog), ALU.mult, ALU.max).then_inc(sem("gate_abs"), 1)
            low(dve, nc.vector, FIRST["w_fk"])
            dve.wait_ge(sem("gate_ln"), 1)
            link(nc.vector.scalar_tensor_tensor(lfr, lfr, 0.0, lf2r, ALU.min, ALU.subtract))
            nc.vector.tensor_tensor_scan(lf2r, ones[0:FOXH, :], lfr, 0.0, ALU.mult, ALU.add).then_inc(sem("lf_cum"), 1)
            dve.wait_ge(sem("gate_ln"), 2)
            link(nc.vector.scalar_tensor_tensor(flat(glog), flat(glog), 0.0, flat(ex[:, 0]), ALU.min, ALU.subtract))
            link(nc.vector.tensor_scalar(glog, glog, 1.0 / GLA_TAU, None, ALU.mult))
            for r in range(2):
                last = nc.vector.tensor_tensor_scan(bcum[:, r, :], scan_mask, glog[:, r, :], 0.0, ALU.mult, ALU.add)
            last.then_inc(sem("gl_cum"), 1)
            whole(dve, "w_gqk")
            for j, dst in enumerate((gqT, gkT)):
                nc.vector.tensor_tensor(dst, pb(1 + j).rearrange("p (r n) -> p r n", r=2),
                                        scale_bc.unsqueeze(1).broadcast_to([P, 2, N]), ALU.mult).then_inc(sem("gqk"), 1)
            dve.wait_ge(sem("gqk"), 2)
            dve.wait_ge(sem("gl_exp"), 1)
            nc.vector.scalar_tensor_tensor(flat(gqT), flat(gqT), float(GDK) ** -0.5, flat(ex[:, 0]), ALU.mult, ALU.mult)
            nc.vector.tensor_tensor(kdec, gkT, ex[:, 1], ALU.mult).then_inc(sem("gl_dec"), 1)
            dve.wait_ge(sem("gl_exp"), 2)
            dve.wait_ge(sem("gl_dec"), 1)
            nc.vector.tensor_tensor(gkT, gkT, ex[:, 0], ALU.mult).then_inc(sem("gl_klast"), 1)
            low(dve, nc.vector, FIRST["w_fv"])
            sums = sm[:, 0:32].rearrange("p (t w h) -> p w t h", t=NT, w=2)
            for w in range(2):
                dve.wait_ge(sem("fqk"), 2 * w + 2)
                x = fqk[:, :, 8 * w:8 * w + 8, :]
                link(nc.vector.tensor_tensor(fsq, x, x, ALU.mult))
                link(nc.vector.tensor_reduce(sums[:, w], fsq, AX.X, ALU.add))
            link(nc.vector.tensor_scalar(sm[:, 0:32], sm[:, 0:32], 1.0 / HD, EPS, ALU.mult, ALU.add))
            nc.vector.reciprocal(sm[:, 32:64], sm[:, 0:32]).then_inc(sem("inverses"), 1)
            low(dve, nc.vector, FIRST["w_gv"])
            dve.wait_ge(sem("small2_in"), SMALL2 * 16)
            link(nc.vector.tensor_scalar(foxg[:, 0, :], foxg[:, 0, :], float(HD) ** -0.5, None, ALU.mult))
            dve.wait_ge(sem("roots"), 3)
            fr = sm[:, 32:64].rearrange("p (t h) -> p t h", t=NT).unsqueeze(3).broadcast_to([P, NT, 16, HD])
            link(nc.vector.tensor_tensor(fqk, fqk, fr, ALU.mult))
            for t in range(NT):
                for w in range(2):
                    last = nc.vector.tensor_tensor(fqk[:, t, 8 * w:8 * w + 8, :], fqk[:, t, 8 * w:8 * w + 8, :],
                                                   foxg[:, w:w + 1, :].broadcast_to([P, 8, HD]), ALU.mult)
            last.then_inc(sem("fqk_normed"), 1)
            low(dve, nc.vector, FIRST["w_gr"])
            dve.wait_ge(sem("gl_klast"), 1)
            link(nc.vector.memset(AT, 0.0))
            for w in range(2):
                dve.wait_ge(sem("cols_ps"), 4 + 2 * w + 1)
                nc.vector.tensor_copy(flat(fT[:, w, 0:2, :]), pb(2 * w)).then_inc(sem("cols"), 1)
            dve.wait_ge(sem("kl_ps"), 1)
            nc.vector.tensor_copy(klrow.rearrange("p t r e -> p (t r e)"), pb(4)).then_inc(sem("klrow"), 1)
            dve.wait_ge(sem("params_in"), PARAMS * 16)
            for w in range(2):
                dve.wait_ge(sem("A_ps"), w + 1)
                for t in range(NT):
                    last = nc.vector.copy_predicated(AT[:, t].rearrange("p (r w) c -> p w r c", w=2)[:, w],
                                                     glam[:, :].unsqueeze(1).broadcast_to([P, 2, P]),
                                                     pb(5 + w)[:, 256 * t:256 * t + 256].rearrange("p (r c) -> p r c", r=2))
                last.then_inc(sem("AT"), 1)
            dve.wait_ge(sem("dS_ps"), 2)
            decay = sm[:, 200:208].rearrange("p (r c) -> p r c", r=2)
            dS02 = pb(7).rearrange("p (r c v) -> p r c v", r=2, c=2)
            dS1 = pb(4)[:, 0:N].rearrange("p (r v) -> p r v", r=2)
            link(nc.vector.tensor_copy(state[:, :, 0, :], dS02[:, :, 0, :]))
            for r in range(2):
                link(nc.vector.scalar_tensor_tensor(state[:, r, 1, :], state[:, r, 0, :], decay[:, r, 1:2], dS1[:, r, :],
                                                    ALU.mult, ALU.add))
            for r in range(2):
                last = nc.vector.scalar_tensor_tensor(state[:, r, 2, :], state[:, r, 1, :], decay[:, r, 2:3],
                                                      dS02[:, r, 1, :], ALU.mult, ALU.add)
            last.then_inc(sem("states"), 1)
            dve.wait_ge(sem("ccol_ps"), 1)
            ccol = sm[:, 184:200]
            nc.vector.tensor_copy(ccol, ps[:, 0, 0:16]).then_inc(sem("ccol"), 1)
            for j, b in enumerate((1, 2, 3, 5)):
                dve.wait_ge(sem("nb_ps"), j + 1)
                nc.vector.tensor_scalar(flat(NB[:, 2 * j:2 * j + 2, :]), pb(b), -1.0, None, ALU.mult).then_inc(sem("nb"), 1)
            for t in range(NT):
                dve.wait_ge(sem("go_ps"), t + 1)
                for w in range(2):
                    link.mark(nc.vector.tensor_copy(go[:, t, :].rearrange("p (r w v) -> p w r v", w=2, v=GDV)[:, w],
                                                    pb(GO[t][w])[:, 0:N].rearrange("p (r v) -> p r v", v=GDV)))
            link.wait()
            nc.vector.tensor_copy(sm[:, 208:209], go[:, 1, 0:1]).then_inc(sem("go_sb"), 1)
            dve.wait_ge(sem("nb"), 4)
            dve.wait_ge(sem("ccol"), 1)
            for n in range(NT * FOXH):
                t, hd, nk = n // FOXH, n % FOXH, P * (n // FOXH + 1)
                x = fp[:, n % 2, 0:nk]
                if n == FOXH:
                    columns_low("w_out", 0, WO[0], gla_x[1], gla_x[0])
                dve.wait_ge(sem("fx_s"), n + 1)
                if n >= 2:
                    dve.wait_ge(sem("fx_pT_ps"), n - 1)
                if n % FOXH == 0:
                    dve.wait_ge(sem("nb"), 5 + t)
                link(nc.vector.scalar_tensor_tensor(x, ps[:, FS[n % 2], 0:nk], ccol[:, 8 * t + hd:8 * t + hd + 1],
                                                    NB[:, hd, :] if t else NB0[:, hd // 4, hd % 4, :], ALU.add, ALU.add))
                nc.vector.tensor_reduce(sm[:, 64 + n:65 + n], x, AX.X, ALU.max, negate=True).then_inc(sem("fx_max"), 1)
                if n % 2 == 1:
                    dve.wait_ge(sem("fx_pT_ps"), n)
                    mk = P * ((n - 1) // FOXH + 1)
                    if n >= 3:
                        dve.wait_ge(sem("fx_pv"), n - 2)
                    nc.vector.tensor_copy(fpT[:, 0, 0:mk], ps[:, FTB[0], 0:mk]).then_inc(sem("fx_pT_dve"), 1)
            for t in range(NT):
                dve.wait_ge(sem("fx_pv"), FOXH * (t + 1))
                link(nc.vector.reciprocal(sm[:, 112 + 8 * t:120 + 8 * t], sm[:, 96 + 8 * t:104 + 8 * t]))
                nc.vector.tensor_tensor(rows[:, t, 0:512].rearrange("p (h e) -> p h e", e=HD),
                                        pb(FO[t]).rearrange("p (h e) -> p h e", e=HD),
                                        sm[:, 112 + 8 * t:120 + 8 * t].unsqueeze(2).broadcast_to([P, FOXH, HD]), ALU.mult)\
                    .then_inc(sem("mix_rows"), 1)
            columns_low("w_out", 2, FTB, xT_r, x_hi)
            add_plain(2, "w_out", WO[0] + WO[1])

            norm_low("xattn", x_hi)
            low(dve, nc.vector, FIRST["wq"] + 1)
            for g in range(2):
                b = 2 * g
                dve.wait_ge(sem("cols_ps"), 12 + b + 1)
                nc.vector.tensor_tensor(xqT[:, 2 * b:2 * b + 2, :], pb(XQT[b]).rearrange("p (k n) -> p k n", k=2),
                                        xqg.unsqueeze(2).broadcast_to([P, 2, N]), ALU.mult).then_inc(sem("cols"), 1)
                dve.wait_ge(sem("head_rstd"), g + 3)
                for n in range(4 * g, 4 * g + 5):
                    if n < 4 * g + 4:
                        dve.wait_ge(sem("xa_s"), n + 1)
                        link(nc.vector.tensor_reduce(sm[:, 64 + n:65 + n], ps[:, n % 2, 0:N], AX.X, ALU.max, negate=True))
                        nc.vector.tensor_tensor(sm[:, 64 + n:65 + n], sm[:, 64 + n:65 + n], sm[:, 48 + n:49 + n], ALU.mult)\
                            .then_inc(sem("xa_max"), 1)
                    if g == 1 and n == 5:
                        columns_low("wo", 0, (4, 5), xT_r, x_hi)
                    m = n - 1
                    if m >= 4 * g:
                        dve.wait_ge(sem("xa_pT_ps"), m + 1)
                        if m >= 2:
                            dve.wait_ge(sem("xa_pv"), m - 1)
                        nc.vector.tensor_copy(xpT[:, m % 2, :], pb(XPT[g] + m % 2)[:, 0:N]).then_inc(sem("xa_pT"), 1)
                dve.wait_ge(sem("xa_pv"), 4 * g + 4)
                link(nc.vector.reciprocal(sm[:, 112 + 4 * g:116 + 4 * g], sm[:, 96 + 4 * g:100 + 4 * g]))
                for t in range(NT):
                    r = sm[:, 112 + 4 * g:116 + 4 * g].rearrange("p (h t) -> p t h", t=NT)[:, t]
                    nc.vector.tensor_tensor(rows[:, t, 512 * g:512 * g + 512].rearrange("p (h e) -> p h e", e=XD),
                                            pb(XO[g] + t).rearrange("p (h e) -> p h e", e=XD),
                                            r.unsqueeze(2).broadcast_to([P, 2, XD]), ALU.mult).then_inc(sem("xo"), 1)
            columns_low("wo", 2, (2, 3), xT_r[:, 4:8], x_hi[:, 4:8])
            add_plain(3, "wo", (4, 5, 0, 1))

            norm_low("mlp", x_hi)
            low(dve, nc.vector, mlp("up", 1))
            for j in range(8):
                u = uT[:, j % 2]
                dve.wait_ge(sem("mlp_relu"), j + 1)
                nc.vector.tensor_tensor(u, u, u, ALU.mult).then_inc(sem("mlp_u"), 1)
                dve.wait_ge(sem("mlp_u_high"), j + 1)
                nc.vector.tensor_tensor(uT_lo[:, j % 2], u, uT_hi[:, j % 2].bitcast(F32), ALU.subtract)\
                    .then_inc(sem("mlp_u_split"), 1)
                low(dve, nc.vector, mlp("down", j))
                if j + 2 < 8:
                    low(dve, nc.vector, mlp("up", j + 2))
            u = NORMS.index("mlp")
            dve.wait_ge(sem("norm_rstd"), 2 * u + 2)
            link(nc.vector.tensor_tensor(ms[:, u, :], rstd[:, u, :], rstd[:, u, :], ALU.mult))
            dve.wait_ge(sem("h_ready"), 16)
            for t in range(NT):
                if t == 0:
                    dve.wait_ge(sem("tile_0_whole"), 5)
                else:
                    whole(dve, "mlp", len(MLP) - 1)
                for j in range(2):
                    s = slice(512 * j, 512 * j + 512)
                    nc.vector.scalar_tensor_tensor(h[:, t, s], pb(2 * t + j), ms[:, u, t:t + 1], h[:, t, s], ALU.mult, ALU.add)\
                        .then_inc(sem("h_ready"), 1)

        @block.tensor
        def _(pe):
            mm = nc.tensor.matmul

            def used(ins):
                ins.then_inc(sem("chunks_used"), 1)

            def ada(g, c, bank):
                i = ada_chunk(g, c)
                arrived(pe, i)
                for k in (0, 1, 2)[:3 if c == 3 else 2]:
                    for j in range(4):
                        r = 4 * g + j
                        lhs, rhs = (sil[:, 2 * c + k, :], slot2(i)[:, k, 512 * j:512 * (j + 1)]) if k < 2 else \
                            (ident[:, r:r + 1].broadcast_to([P, 32]), ada_b)
                        last = mm(ps[32 * j:32 * j + 32, bank, :], lhs, rhs, start=(c == k == 0), stop=(k == 2))
                used(last)

            def ada_columns(g, bank):
                pe.wait_ge(sem("ada_rows"), g + 1)
                for b in range(4):
                    last = nc.tensor.transpose(ps[:, bank, P * b:P * (b + 1)], mrow[:, g % 3, b, :], ident)
                last.then_inc(sem("mod_T"), 1)

            def transposes(name, src, ready="norm_rows", first=None):
                v, bank = TRANSPOSED.index(name), NORM_BANKS[name]
                first = 2 * NORMED.index(name) + 1 if first is None else first
                for t in range(NT):
                    if ready:
                        pe.wait_ge(sem(ready), first + t)
                    for k in range(KD):
                        last = nc.tensor.transpose(ps[:, bank[k // 2], 256 * (k % 2) + P * t:256 * (k % 2) + P * (t + 1)],
                                                   src[:, t, P * k:P * (k + 1)], ident)
                        if t == NT - 1 and k % 2:
                            last.then_inc(sem("norm_T"), 1)

            def normed_columns(name):
                pe.wait_ge(sem("xT_ready"), 4 * TRANSPOSED.index(name) + 4)

            def to_rows(i, lhs, banks, width=512, col=0):
                for t in range(NT):
                    for k in range(KD):
                        last = mm(ps[:, banks[t], col:col + width], lhs[:, k, P * t:P * (t + 1)], slot8(i)[:, k, 0:width],
                                  start=(k == 0), stop=(k == KD - 1))
                return last

            def to_columns(i, rhs, banks):
                for c in range(4):
                    for k in range(KD):
                        last = mm(ps[:, banks[c // 2], N * (c % 2):N * (c % 2 + 1)], slot8(i)[:, k, P * c:P * (c + 1)],
                                  rhs[:, k, :], start=(k == 0), stop=(k == KD - 1))
                return last

            def split_product(out, lhs, rhs, start, stop):
                for n, (x, y) in enumerate(((0, 1), (1, 0), (0, 0))):
                    last = mm(out, lhs[x], rhs[y], start=start and n == 0, stop=stop and n == 2)
                return last

            def split_block(i, half, t, kk, x, bank, order=(0, 1)):
                n, w, lo, hi = list(halves(i))[half]
                pe.wait_ge(sem("w_split"), SC_SPLITS + n + 2)
                k, s, c = (4 * half + kk) % x[0].shape[1], slice(P * t, P * (t + 1)), slice(512 * kk, 512 * kk + 512)
                return split_product(pb(bank), (x[0][:, k, s], x[1][:, k, s]), (hi[:, c], lo[:, c]),
                                     half == order[0] and kk == 0, half == order[1] and kk == 3)

            def split_half(i, half, x, banks, last_half=False, order=(0, 1), waits=None):
                for t in range(NT):
                    for kk in range(4):
                        if waits and t == 0 and kk % 2 == 0:
                            input_split(waits[0], waits[1] + kk // 2)
                        last = split_block(i, half, t, kk, x, banks[t], order)
                    if last_half and t == 0:
                        last.then_inc(sem("tile_0_whole"), 1)
                return last

            def split_rows(i, x, banks, last_chunk=False, waits=None):
                for half in range(2):
                    split_half(i, half, x, banks, last_chunk and half == 1, waits=waits and (waits, 2 * half)).then_inc(sem("w_halves_used"), 1)

            def split_columns(i, x, banks, waits=None):
                for half, (n, w, lo, hi) in enumerate(halves(i)):
                    pe.wait_ge(sem("w_split"), SC_SPLITS + n + 2)
                    for c in range(2):
                        s = slice(P * c, P * (c + 1))
                        for k in range(KD):
                            if waits and half == c == k % 2 == 0:
                                input_split(waits, k // 2)
                            last = split_product(ps[:, banks[half], N * c:N * (c + 1)], (hi[:, k, s], lo[:, k, s]),
                                                 (x[0][:, k, :], x[1][:, k, :]), k == 0, k == KD - 1)
                    last.then_inc(sem("w_halves_used"), 1)

            def input_split(name, b=3):
                pe.wait_ge(sem("x_split"), 4 * SPLIT_INPUTS.index(name) + b + 1)

            def row_transposes(src, banks, ks=range(KD)):
                for k in ks:
                    for t in range(NT):
                        last = nc.tensor.transpose(ps[:, banks[k // 2], N * (k % 2) + P * t:N * (k % 2) + P * (t + 1)],
                                                   src[:, t, P * k:P * (k + 1)], ident)
                    if k % 2:
                        last.then_inc(sem("cols_ps"), 1)

            pe.wait_ge(sem("c_in"), 3 * 16)
            nc.tensor.transpose(ps[:, 2, 0:2 * KD], crow[0:2 * KD, :], ident[0:2 * KD, 0:2 * KD]).then_inc(sem("c_ps"), 1)
            pe.wait_ge(sem("gains_in"), 7 * 16)
            nc.tensor.transpose(ps[:, 1, 0:GAINS], grow[0:GAINS, :], ident[0:GAINS, 0:GAINS]).then_inc(sem("gains_ps"), 1)
            pe.wait_ge(sem("sil"), 1)
            pe.wait_ge(sem("ada_b_in"), 16)
            for q in range(4):
                ada(0, q, 0)
            transposes("x", rows)
            ada_columns(0, 0)
            pe.wait_ge(sem("gain_cols"), 1)
            pe.wait_ge(sem("mod_cols"), 1)
            transposes("ctx", ctx_rows)
            normed_columns("x")
            normed_columns("ctx")
            pe.wait_ge(sem("params_in"), PARAMS * 16)
            for c in range(CT):
                last = nc.tensor.transpose(ps[:, 4, 34 * c:34 * c + 34], cwrow[0:34, P * c:P * (c + 1)], ident[0:34, 0:34])
            last.then_inc(sem("cw_ps"), 1)
            i = FIRST["ev_q"]
            arrived(pe, i)
            used(to_rows(i, xT, (0, 1)))
            i = FIRST["ev_kv"]
            arrived(pe, i)
            for bank, lhs in ((2, xT), (3, cT)):
                for t in range(NT):
                    for k in range(KD):
                        last = mm(ps[:, bank, 256 * t:256 * t + 256], lhs[:, k, P * t:P * (t + 1)], slot8(i)[:, k, 0:256],
                                  start=(k == 0), stop=(k == KD - 1))
            used(last)
            pe.wait_ge(sem("cw"), 1)
            for name, banks in (("ev_u", (4, 5)), ("ev_gate", (6, 7))):
                i = FIRST[name]
                arrived(pe, i)
                used(to_columns(i, xT, banks))
                pe.wait_ge(sem("ev_rows"), 10)
                for c in range(2):
                    ada(1, (2 if name == "ev_gate" else 0) + c, 3)
            pe.wait_ge(sem("ev_rope"), 4)
            for i in range(4):
                for t in range(NT):
                    last = nc.tensor.transpose(ps[:, i // 2, N * (i % 2) + P * t:N * (i % 2) + P * (t + 1)],
                                               qk[:, t, 2 * i:2 * i + 2, :].rearrange("p h e -> p (h e)"), ident)
            last.then_inc(sem("ev_qkT_ps"), 1)
            for s in range(4):
                last = nc.tensor.transpose(ps[:, 2, P * s:P * (s + 1)],
                                           qk[:, s % 2, 10 - 2 * (s // 2):12 - 2 * (s // 2), :].rearrange("p h e -> p (h e)"),
                                           ident)
            last.then_inc(sem("ev_qkT_ps"), 1)
            ada_columns(1, 3)
            pe.wait_ge(sem("ev_qT"), 2)
            pe.wait_ge(sem("ev_kT"), 1)

            def ev_scores(n):
                t, i, w = n // 8, n % 8 // 2, n % 2
                if n >= 3:
                    pe.wait_ge(sem("ev_p"), n - 2)
                mm(pb(n % 3), qT[64 * w:64 * w + 64, i, P * t:P * (t + 1)], kT[64 * w:64 * w + 64, :],
                   start=True, stop=True).then_inc(sem("ev_s"), 1)

            def ev_transposed(n):
                pe.wait_ge(sem("ev_p"), n + 1)
                if n >= 2:
                    pe.wait_ge(sem(("ev_pT_dve", "ev_pT_act")[n % 2]), n // 2)
                for s in range(4):
                    last = nc.tensor.transpose(ps[:, 4 + n % 2, P * s:P * (s + 1)], pexp[:, n % 2, P * s:P * (s + 1)], ident)
                last.then_inc(sem("ev_pT_ps"), 1)

            def ev_values(n):
                t, i, w = n // 8, n % 8 // 2, n % 2
                pe.wait_ge(sem(("ev_pT_dve", "ev_pT_act")[w]), n // 2 + 1)
                for s in range(4):
                    last = mm(ps[:, 6 + t, 64 * (n % 8):64 * (n % 8) + 64], pT[:, w, s, :], vall[:, s, 64 * w:64 * w + 64],
                              start=(s == 0), stop=(s == 3))
                last.then_inc(sem("ev_pv"), 1)

            pe.wait_ge(sem("gpad"), 2)
            pe.wait_ge(sem("cv_gate"), 2)
            def cv_sums(n):
                if n == 0:
                    pe.wait_ge(sem("conv"), CT * CONVK - POOL_TAPS + 1)
                    pe.wait_ge(sem("cleared"), 3)
                    pe.wait_ge(sem("ev_attn"), 2)
                else:
                    pe.wait_ge(sem("cv_sq"), 1)
                for c in range(CT):
                    last = mm(ps[:, 6, N * n:N * (n + 1)], ones[:, 0:P], (cacc, csq)[n][:, c, :],
                              start=(c == 0), stop=(c == CT - 1))
                last.then_inc(sem("cv_sum"), 1)

            ev_scores(0)
            ev_scores(1)
            for n in range(NT * NQ):
                if n + 2 < NT * NQ:
                    ev_scores(n + 2)
                ev_transposed(n)
                if n:
                    ev_values(n - 1)
                if n % 4 == 0 and n:
                    ada_columns(1 + n // 4, 3)
                if n in (LN_AT, LN_AT + 1):
                    cv_sums(n - LN_AT)
                if n % 4 == 0:
                    pe.wait_ge(sem("mod_cols"), 2 + n // 4)
                ada(2 + n // 4, n % 4, 3)
            ev_values(NT * NQ - 1)
            pe.wait_ge(sem("ev_attn"), 4)
            pe.wait_ge(sem("ev_pT_dve"), 8)
            pe.wait_ge(sem("ev_pT_act"), 8)
            for k in range(4):
                for t in range(NT):
                    last = nc.tensor.transpose(ps[:, 4 + k // 2, N * (k % 2) + P * t:N * (k % 2) + P * (t + 1)],
                                               attn[:, t, P * k:P * (k + 1)], ident)
                if k % 2:
                    last.then_inc(sem("ev_aT_ps"), 1)
            ada_columns(5, 3)
            pe.wait_ge(sem("ev_p"), NT * NQ)
            pe.wait_ge(sem("roots"), 2)
            for j in range(2):
                for p in range(2):
                    n, w, lo, hi = ev_half(j, p)
                    pe.wait_ge(sem("w_split"), n + 1)
                    for t in range(NT):
                        s = slice(P * t, P * (t + 1))
                        for k in range(4):
                            c = slice(512 * k, 512 * k + 512)
                            if j == t == k % 2 == 0:
                                input_split("ev_out", 2 * p + k // 2)
                            last = split_product(pb(((0, 1), (6, 7))[j][t]), (ev_x[p][0][:, k, s], ev_x[p][1][:, k, s]),
                                                 (hi[:, c], lo[:, c]), p == k == 0, p == 1 and k == 3)
                        if j == p == 1 and t == 0:
                            last.then_inc(sem("tile_0_whole"), 1)
                    if p:
                        used(last)
                    else:
                        last.then_inc(sem("half_used"), 1)

            def route(l):
                name = f"moe{l}"
                pe.wait_ge(sem("h_ready"), 4 * (l + 1))
                transposes(name, rows)
                normed_columns(name)
                pe.wait_ge(sem("params_in"), PARAMS * 16)
                for t in range(NT):
                    for k in range(KD):
                        last = mm(ps[:, 0, E * t:E * (t + 1)], xT[:, k, P * t:P * (t + 1)], wr[:, l, k, :],
                                  start=(k == 0), stop=(k == KD - 1))
                last.then_inc(sem("mo_logits"), 1)
                pe.wait_ge(sem("mo_aff"), l + 1)
                for t in range(NT):
                    last = nc.tensor.transpose(ps[0:E, 1, P * t:P * (t + 1)], aff[:, t, :], ident)
                    if l == t == 0:
                        last.then_inc(sem("mo_comb"), 1)
                last.then_inc(sem("mo_affT_ps"), 1)
                pe.wait_ge(sem("mo_rank"), l + 1)
                for t in range(NT):
                    last = nc.tensor.transpose(ps[:, 2, E * t:E * (t + 1)], rank[0:E, P * t:P * (t + 1)], ident[0:E, 0:E])
                    if l == t == 0:
                        last.then_inc(sem("mo_hT_ps"), 1)
                last.then_inc(sem("mo_rankT_ps"), 1)
                pe.wait_ge(sem("mo_lists"), 2 * l + 1)

            def experts(loop):
                l, g0, g1, base = loop
                with pe.Fori(g0, g1) as g:
                    n = g + GROUPS * l

                    def chunk(c):
                        i = base + c
                        pe.wait_ge(sem(f"slot{i % SLOTS}_loaded"), 16 * (PER_GROUP // SLOTS) * g + 16 * (i // SLOTS + 1))
                        return slot4(i)

                    def product(c0, banks, src, second=None):
                        for k in range(KD):
                            w = chunk(c0 + k)
                            if second and k == KD // 2:
                                pe.wait_ge(sem(second), n + 1)
                            for half in range(2):
                                for j in range(EG):
                                    last = mm(ps[32 * j:32 * j + 32, banks[half], :], src[:, k, CAP * j:CAP * (j + 1)],
                                              w[:, j, 512 * half:512 * half + 512], start=(k == 0), stop=(k == KD - 1))
                            used(last)

                    pe.wait_ge(sem("mo_h"), 4 * n + 1)
                    for k in range(KD):
                        for t in range(NT):
                            last = mm(ps[:, 6 + k // 4, P * (k % 4):P * (k % 4 + 1)], rows[:, t, P * k:P * (k + 1)],
                                      onehot[:, t, bass.ds(g * P, P)], start=(t == 0), stop=(t == NT - 1))
                        if k % 4 == 3:
                            last.then_inc(sem("mo_gather"), 1)
                    pe.wait_ge(sem("mo_xsT_dve"), n + 1)
                    product(0, (0, 1), xsT, "mo_xsT_act")
                    pe.wait_ge(sem("mo_lists"), 2 * l + 2)
                    mm(pb(4), cst[0:E, C_E4:C_E4 + P], RA[0:E].rearrange("e g v n -> e (g v n)")[:, bass.ds(g * 2 * N, 2 * N)],
                       start=True, stop=True).then_inc(sem("mo_bc"), 1)
                    product(KD, (2, 3), xsT)
                    pe.wait_ge(sem("mo_hid"), n + 1)
                    for k in range(KD):
                        last = nc.tensor.transpose(ps[:, 6 + k // 4, P * (k % 4):P * (k % 4 + 1)], hid[:, P * k:P * (k + 1)],
                                                   ident)
                        if k % 4 == 3:
                            last.then_inc(sem("mo_hT_ps"), 1)
                    pe.wait_ge(sem("mo_hT_dve"), n + 1)
                    pe.wait_ge(sem("mo_hT_act"), n + 1)
                    pe.wait_ge(sem("mo_sel"), n + 1)
                    product(2 * KD, (4, 5), hT)
                    pe.wait_ge(sem("mo_ym"), 2 * n + 2)
                    for i in range(4):
                        t, half = i // 2, i % 2
                        mm(pb((6, 7, 4, 5)[i]), sel_w[:, P * t:P * (t + 1)], ym[:, 512 * half:512 * half + 512],
                           start=True, stop=True).then_inc(sem("mo_comb"), 1)
                pe.wait_ge(sem("mo_h"), 4 * (GROUPS * l + g1) + 1)

            route(0)
            experts(LOOPS[0])
            pe.wait_ge(sem("mem_in"), 32)
            transposes("mem", mem_rows, None, 0)
            normed_columns("mem")
            for j in range(2):
                arrived(pe, FIRST["wk"] + j)
                used(to_rows(FIRST["wk"] + j, memT, (4 + 2 * j, 5 + 2 * j)))
            for j in range(2):
                pe.wait_ge(sem("xk_normed"), j + 1)
                row_transposes(xk, (4, 5, 6, 7), range(4 * j, 4 * j + 4))
            pe.wait_ge(sem("cols"), 4)
            experts(LOOPS[1])
            for j in range(2):
                arrived(pe, FIRST["wv"] + j)
                used(to_rows(FIRST["wv"] + j, memT, (2 * j, 2 * j + 1)))
            pe.wait_ge(sem("xkv"), 4)
            experts(LOOPS[2])

            transposes("mix1", rows)

            def sc_used(half, last):
                if half:
                    used(last)
                else:
                    last.then_inc(sem("half_used"), 1)

            for m in range(6):
                if m == 4:
                    pe.wait_ge(sem("sc_c"), 1)
                if m == 5:
                    pe.wait_ge(sem("sc_y"), 1)
                for half, (n, w, lo, hi) in enumerate(sc_halves(m)):
                    pe.wait_ge(sem("w_split"), n + 1)
                    for c in range(2):
                        s = slice(P * c, P * (c + 1))
                        for k in range(KD):
                            if m == half == c == k % 2 == 0:
                                input_split("mix1", k // 2)
                            last = split_product(ps[:, 2 * m % 8 + half, N * c:N * (c + 1)], (hi[:, k, s], lo[:, k, s]),
                                                 (sc_hi[:, k, :], xT_r[:, k, :]), k == 0, k == KD - 1)
                    sc_used(half, last)
            pe.wait_ge(sem("sc_c"), 2)
            for j in range(2):
                for half, (n, w, lo, hi) in enumerate(sc_halves(6 + j)):
                    pe.wait_ge(sem("w_split"), n + 1)
                    pe.wait_ge(sem("x_split"), 4 * SPLIT_INPUTS.index("y") + 2 * half + 2)
                    for t in range(NT):
                        s = slice(P * t, P * (t + 1))
                        for kk in range(4):
                            k, c = 4 * half + kk, slice(512 * kk, 512 * kk + 512)
                            last = split_product(pb(4 + 2 * j + t), (y_hi[:, k, s], y_lo[:, k, s]), (hi[:, c], lo[:, c]),
                                                 k == 0, k == KD - 1)
                        if j == half == 1 and t == 0:
                            last.then_inc(sem("tile_0_whole"), 1)
                    sc_used(half, last)

            route(1)
            experts(LOOPS[3])

            transposes("mix2", rows, first=2 * NORMED.index("final") + 1)
            x = (rows_hi, xT_r)
            pe.wait_ge(sem("w_split"), SC_SPLITS + 1)
            small_lo = ring_r[slot_of(N0)].rearrange("p (k n) -> p k n", k=KD)
            for c, m, c0, col in ((0, FOXH, 0, 0), (8, 16, 32, N)):
                for k in range(KD):
                    if c == k % 2 == 0:
                        input_split("mix2", k // 2)
                    last = split_product(ps[0:m, 0, col:col + N], (small_hi[:, k, c:c + m], small_lo[:, k, c0:c0 + m]),
                                         (x[0][:, k, :], x[1][:, k, :]), k == 0, k == KD - 1)
            used(last)
            split_columns(FIRST["w_gqk"], x, (1, 2))
            pe.wait_ge(sem("h_final"), 3)
            for t in range(NT):
                last = mm(ps[:, 3, P * t:P * (t + 1)], row_scale[:, t:t + 1].broadcast_to([P, P]), ident, start=True, stop=True)
            last.then_inc(sem("scale_ps"), 1)
            pe.wait_ge(sem("glr"), 1)
            pe.wait_ge(sem("small2_in"), SMALL2 * 16)
            for r in range(2):
                last = mm(ps[:, 3, N * r:N * (r + 1)], gate2[:, P * r:P * (r + 1)], glrT[0:16, :], start=True, stop=True)
            last.then_inc(sem("gl_ps"), 1)
            for name, banks in (("w_fq", (4, 5)), ("w_fk", (6, 7)), ("w_fv", (0, 1)), ("w_gv", (2, 3)), ("w_gr", (6, 7))):
                if name == "w_fv":
                    pe.wait_ge(sem("gate_abs"), 1)
                    pe.wait_ge(sem("gqk"), 2)
                if name == "w_gv":
                    pe.wait_ge(sem("gate_abs"), 2)
                if name == "w_gr":
                    pe.wait_ge(sem("fqk"), 4)
                split_rows(FIRST[name], x, banks)
            pe.wait_ge(sem("values"), 4)
            pe.wait_ge(sem("fqk_normed"), 1)
            for w in range(2):
                for r in range(4):
                    for t in range(NT):
                        last = nc.tensor.transpose(ps[:, 2 * w + r // 2, N * (r % 2) + P * t:N * (r % 2) + P * (t + 1)],
                                                   fqk[:, t, 8 * w + 2 * r:8 * w + 2 * r + 2, :].rearrange("p h e -> p (h e)"),
                                                   ident)
                    if r % 2:
                        last.then_inc(sem("cols_ps"), 1)
            pe.wait_ge(sem("gl_klast"), 1)
            for t in range(NT):
                for r in range(2):
                    last = nc.tensor.transpose(ps[:, 4, P * (2 * t + r):P * (2 * t + r + 1)], gkT[:, r, P * t:P * (t + 1)], ident)
            last.then_inc(sem("kl_ps"), 1)
            pe.wait_ge(sem("values"), 6)
            for w in range(2):
                for t in range(NT):
                    for r in range(2):
                        s = slice(64 * w, 64 * w + 64)
                        last = mm(ps[:, 5 + w, P * (2 * t + r):P * (2 * t + r + 1)], kdec[s, r, P * t:P * (t + 1)],
                                  gqT[s, r, P * t:P * (t + 1)], start=True, stop=True)
                last.then_inc(sem("A_ps"), 1)
            pe.wait_ge(sem("klrow"), 1)
            for chunks, bank in (((0, 2), 7), ((1,), 4)):
                for c in chunks:
                    s, t = slice(GCH * (c % 2), GCH * (c % 2) + GCH), c // 2
                    for hd in range(GLAH):
                        r, w = hd // 2, hd % 2
                        col = GDV * (2 * r + c // 2) if bank == 7 else GDV * r
                        last = mm(ps[64 * w:64 * w + 64, bank, col:col + GDV], klrow[s, t, r, 64 * w:64 * w + 64],
                                  gv[s, t, GDV * hd:GDV * (hd + 1)], start=True, stop=True)
                last.then_inc(sem("dS_ps"), 1)
            pe.wait_ge(sem("cols"), 8)
            pe.wait_ge(sem("lf_cum"), 1)
            for t in range(NT):
                last = nc.tensor.transpose(ps[:, 0, FOXH * t:FOXH * (t + 1)], lf2[0:FOXH, P * t:P * (t + 1)],
                                           ident[0:FOXH, 0:FOXH])
            last.then_inc(sem("ccol_ps"), 1)
            for j, b in enumerate((1, 2, 3, 5)):
                if b == 5:
                    pe.wait_ge(sem("AT"), 2)
                for w in range(2):
                    hd = 2 * j + w
                    last = mm(ps[:, b, N * w:N * (w + 1)], ident[0:FOXH, hd:hd + 1].broadcast_to([FOXH, P]), lf2[0:FOXH, :],
                              start=True, stop=True)
                last.then_inc(sem("nb_ps"), 1)
            pe.wait_ge(sem("states"), 1)
            pe.wait_ge(sem("ccol"), 1)
            pe.wait_ge(sem("AT"), 2)
            for t in range(NT):
                for hd in range(GLAH):
                    r, w = hd // 2, hd % 2
                    for c in (2 * t, 2 * t + 1):
                        o = slice(GCH * (c % 2), GCH * (c % 2) + GCH)
                        out = ps[o, GO[t][w], GDV * r:GDV * (r + 1)]
                        last = mm(out, AT[:, t, hd, o], gv[:, t, GDV * hd:GDV * (hd + 1)], start=True, stop=(c == 0))
                        if c:
                            last = mm(out, gqT[64 * w:64 * w + 64, r, GCH * c:GCH * (c + 1)],
                                      state[64 * w:64 * w + 64, r, c - 1, :], start=False, stop=True)
                last.then_inc(sem("go_ps"), 1)

            def fox_scores(n):
                t, hd = n // FOXH, n % FOXH
                if n >= 2:
                    pe.wait_ge(sem("fx_max"), n - 1)
                s, nk = slice(64 * (hd % 2), 64 * (hd % 2) + 64), P * (t + 1)
                mm(ps[:, FS[n % 2], 0:nk], fT[s, 0, hd // 2, P * t:P * (t + 1)], fT[s, 1, hd // 2, 0:nk],
                   start=True, stop=True).then_inc(sem("fx_s"), 1)

            def fox_transposed(n):
                pe.wait_ge(sem("fx_p"), n + 1)
                if n >= 2:
                    pe.wait_ge(sem(("fx_pT_dve", "fx_pT_act")[n % 2]), n // 2)
                for s in range(n // FOXH + 1):
                    last = nc.tensor.transpose(ps[:, FTB[n % 2], P * s:P * (s + 1)], fp[:, n % 2, P * s:P * (s + 1)], ident)
                last.then_inc(sem("fx_pT_ps"), 1)

            def fox_values(n):
                t, hd = n // FOXH, n % FOXH
                pe.wait_ge(sem(("fx_pT_dve", "fx_pT_act")[n % 2]), n // 2 + 1)
                for s in range(t + 1):
                    last = mm(ps[:, FO[t], HD * hd:HD * (hd + 1)], fpT[:, n % 2, P * s:P * (s + 1)],
                              fv[:, s, HD * hd:HD * (hd + 1)], start=(s == 0), stop=(s == t))
                last.then_inc(sem("fx_pv"), 1)

            pe.wait_ge(sem("nb"), 4)
            pe.wait_ge(sem("AT"), 2)
            pe.wait_ge(sem("go_sb"), 1)
            def w_out_block(j, b):
                split_block(FIRST["w_out"] + j, 1, b // 4, b % 4, gla_x, WO[j][b // 4], (1, 0))

            fox_scores(0)
            for n in range(NT * FOXH):
                if n + 1 < NT * FOXH:
                    fox_scores(n + 1)
                if n == GLA_AT:
                    pe.wait_ge(sem("mix_rows"), 1)
                    row_transposes(rows, (None, None) + WO[0], range(4, 8))
                if n == FOXH:
                    pe.wait_ge(sem("x_split"), 4 * SPLIT_INPUTS.index("w_out") + 2)
                if n >= FOXH:
                    w_out_block(0, n - FOXH)
                fox_transposed(n)
                if n:
                    fox_values(n - 1)
            fox_values(NT * FOXH - 1)
            pe.wait_ge(sem("fx_max"), NT * FOXH)
            for b in range(8):
                if b == 4:
                    pe.wait_ge(sem("mix_rows"), 3)
                    row_transposes(rows, FTB, range(0, 4))
                w_out_block(1, b)
            for j in range(2):
                split_half(FIRST["w_out"] + j, 0, (x_hi, xT_r), WO[j], j == 1, (1, 0), ("w_out", 2) if j == 0 else None).then_inc(sem("w_halves_used"), 2)

            transposes("xattn", h, "h_ready", 11)
            split_rows(FIRST["wq"], (x_hi, xT_r), (0, 1), waits="xattn")

            def x_scores(n):
                hd, t = n // NT, n % NT
                if n >= 2:
                    pe.wait_ge(sem("xa_p"), n - 1)
                for kk in range(2):
                    last = mm(ps[:, n % 2, 0:N], xqT[:, 2 * hd + kk, P * t:P * (t + 1)], xkT[:, 2 * hd + kk, :],
                              start=(kk == 0), stop=(kk == 1))
                last.then_inc(sem("xa_s"), 1)

            def x_transposed(n):
                pe.wait_ge(sem("xa_p"), n + 1)
                if n >= 2:
                    pe.wait_ge(sem("xa_pT"), n - 1)
                for s in range(2):
                    last = nc.tensor.transpose(pb(XPT[n // 4] + n % 2)[:, P * s:P * (s + 1)], xp[:, n % 2, P * s:P * (s + 1)], ident)
                last.then_inc(sem("xa_pT_ps"), 1)

            def x_values(n):
                hd, t = n // NT, n % NT
                pe.wait_ge(sem("xa_pT"), n + 1)
                for s in range(2):
                    last = mm(pb(XO[n // 4] + t)[:, XD * (hd % 2):XD * (hd % 2) + XD], xpT[:, n % 2, P * s:P * (s + 1)],
                              xv[:, s, XD * hd:XD * (hd + 1)], start=(s == 0), stop=(s == 1))
                last.then_inc(sem("xa_pv"), 1)

            def wq_block(b):
                last = split_block(FIRST["wq"] + 1, 1, b // 4, b % 4, (x_hi, xT_r), 2 + b // 4)
                if b == 7:
                    last.then_inc(sem("w_halves_used"), 1)

            def wo_block(b):
                last = split_block(FIRST["wo"], 0, b // 4, b % 4, (x_hi, xT_r), 4 + b // 4)
                if b == 7:
                    last.then_inc(sem("w_halves_used"), 1)

            split_half(FIRST["wq"] + 1, 0, (x_hi, xT_r), (2, 3)).then_inc(sem("w_halves_used"), 1)
            pe.wait_ge(sem("xq"), 2)
            row_transposes(xq, (4, 5), range(0, 4))
            wq_block(0)
            wq_block(1)
            pe.wait_ge(sem("head_ss"), 2)
            pe.wait_ge(sem("memkv_in"), 32)
            pe.wait_ge(sem("cols"), 10)
            x_scores(0)
            for n in range(4):
                if n < 3:
                    wq_block(2 + 2 * n)
                    x_scores(n + 1)
                    wq_block(3 + 2 * n)
                x_transposed(n)
                if n:
                    x_values(n - 1)
            x_values(3)
            pe.wait_ge(sem("xq"), 4)
            row_transposes(xq, XQT, range(4, 8))
            pe.wait_ge(sem("head_ss"), 3)
            pe.wait_ge(sem("cols"), 12)
            x_scores(4)
            for n in range(4, 8):
                if n == 4:
                    x_scores(5)
                    pe.wait_ge(sem("xo"), 2)
                    row_transposes(rows, (4, 5), range(0, 4))
                elif n == 5:
                    pe.wait_ge(sem("x_split"), 4 * SPLIT_INPUTS.index("wo") + 2)
                    wo_block(0)
                    wo_block(1)
                    x_scores(6)
                    wo_block(2)
                elif n == 6:
                    wo_block(3)
                    x_scores(7)
                    wo_block(4)
                    wo_block(5)
                else:
                    wo_block(6)
                    wo_block(7)
                x_transposed(n)
                if n > 4:
                    x_values(n - 1)
            x_values(7)
            for b in range(8):
                if b == 4:
                    pe.wait_ge(sem("xo"), 4)
                    row_transposes(rows, (None, None, 2, 3), range(4, 8))
                split_block(FIRST["wo"] + 1, 0, b // 4, b % 4, (x_hi, xT_r), b // 4)
            split_half(FIRST["wo"], 1, (x_hi, xT_r), (4, 5), waits=("wo", 2)).then_inc(sem("w_halves_used"), 2)
            split_half(FIRST["wo"] + 1, 1, (x_hi, xT_r), (0, 1), True).then_inc(sem("w_halves_used"), 1)

            transposes("mlp", h, "h_ready", 15)
            for kind, j in MLP:
                if kind == "up":
                    if j >= 2:
                        pe.wait_ge(sem("mlp_relu"), j - 1)
                    split_columns(mlp("up", j), (x_hi, xT_r), (4 + 2 * (j % 2), 5 + 2 * (j % 2)), "mlp" if j == 0 else None)
                    continue
                pe.wait_ge(sem("mlp_u_split"), j + 1)
                for half, (n, w, lo, hi) in enumerate(halves(mlp("down", j))):
                    pe.wait_ge(sem("w_split"), SC_SPLITS + n + 2)
                    for t in range(NT):
                        for kk in range(2):
                            k, s = 2 * half + kk, slice(P * t, P * (t + 1))
                            for col in range(2):
                                c = slice(D * kk + 512 * col, D * kk + 512 * col + 512)
                                last = split_product(pb(2 * t + col), (uT_hi[:, j % 2, k, s], uT_lo[:, j % 2, k, s]),
                                                     (hi[:, c], lo[:, c]), j == k == 0, j == 7 and k == 3)
                        if j == 7 and half == 1 and t == 0:
                            last.then_inc(sem("tile_0_whole"), 1)
                    last.then_inc(sem("w_halves_used"), 1)


_WEIGHTS = ['x', 'c', 'ctx', 'c_ctx', 'ada_w', 'ada_b', 'norm1_g', 'norm2_g', 'ev_w_in', 'ev_q_g', 'ev_k_g', 'ev_conv_w',
            'ev_conv_b', 'ev_ln_g', 'ev_ln_b', 'ev_w_out', 'sc_w_in', 'sc_conv_w', 'sc_w_out', 'moe_w_r', 'moe_w_gate',
            'moe_w_up', 'moe_w_down', 'final_g', 'mem_2', 'norm_mix_g_2', 'w_in_2', 'fox_b_f_2', 'fox_q_norm_g_2',
            'fox_k_norm_g_2', 'gla_w_gate2_2', 'gla_b_gate_2', 'gla_out_norm_g_2', 'w_out_2', 'norm_xattn_g_2',
            'norm_mem_g_2', 'xattn_wq_2', 'xattn_wkv_2', 'xattn_q_norm_g_2', 'xattn_k_norm_g_2', 'xattn_wo_2',
            'norm_mlp_g_2', 'mlp_w1_2', 'mlp_w2_2']


def kernel(**inputs):
    import concourse.bacc as bacc
    from concourse.bass_utils import run_bass_kernel_spmd

    nc = bacc.Bacc("TRN2", target_bir_lowering=False, num_devices=1)
    arrays = {n: np.ascontiguousarray(inputs[n]) for n in _WEIGHTS}
    arrays["cst"], arrays["cst_i"] = constants()
    a = {n: nc.dram_tensor(f"in_{n}", v.shape, mybir.dt.from_np(v.dtype), kind="ExternalInput").ap()
         for n, v in arrays.items()}
    a["out"] = nc.dram_tensor("out", (1, N, D), F32, kind="ExternalOutput").ap()
    build(nc, a)
    r = run_bass_kernel_spmd(nc, [{f"in_{n}": v for n, v in arrays.items()}], core_ids=[0])
    return r.results[0]["out"]
```
